# Optimizing a Trainium2 kernel written in Bass

```python
import jax
import jax.numpy as jnp
from jax import lax
import numpy as np

D_MODEL = 1024
BATCH = 1
SEQ = 512
DEPTH = 2

GRID_W = 64
CTX_LEN = 256
N_MIXERS = 4
MIX_CONV = 0
MIX_POOL = 1
MIX_MLA = 2
MIX_CHUNK = 3
BRANCH = D_MODEL
EPS = 1e-6
CONV_WIDTH = 31
POOL_WINDOWS = (2, 4, 8, 16)
POOL_GROUP = BRANCH // len(POOL_WINDOWS)
MLA_HEADS = D_MODEL // 128
MLA_NOPE = 128
MLA_ROPE = 64
MLA_V = 128
MLA_Q_RANK = 3 * D_MODEL // 8
MLA_KV_RANK = D_MODEL // 4
MLA_KVC = MLA_KV_RANK + MLA_ROPE
MLA_SCALE = (MLA_NOPE + MLA_ROPE) ** -0.5
ROPE_THETA = 10000.0
Q_BLOCK = 128
CHUNK = 128
CHUNK_GROUPS = 8
CHUNK_GC = BRANCH // CHUNK_GROUPS


def _n_layers_of(kind):
    return len(range(kind, DEPTH, N_MIXERS))

def _rms(x, g):
    xf = x.astype(jnp.float32)
    y = xf * lax.rsqrt(jnp.mean(xf * xf, axis=-1, keepdims=True) + EPS)
    return (y * g.astype(jnp.float32)).astype(x.dtype)

def _layernorm(x, g, b):
    xf = x.astype(jnp.float32)
    mu = jnp.mean(xf, axis=-1, keepdims=True)
    var = jnp.mean(jnp.square(xf - mu), axis=-1, keepdims=True)
    y = (xf - mu) * lax.rsqrt(var + EPS)
    return (y * g.astype(jnp.float32) + b.astype(jnp.float32)).astype(x.dtype)

def _rope_tables(rows):
    row_id = jnp.repeat(jnp.arange(rows), GRID_W).astype(jnp.float32)
    col_id = jnp.tile(jnp.arange(GRID_W), rows).astype(jnp.float32)
    axis_dim = MLA_ROPE // 2
    freqs = ROPE_THETA ** (-jnp.arange(0, axis_dim, 2, dtype=jnp.float32) / axis_dim)
    ar = row_id[:, None] * freqs
    ac = col_id[:, None] * freqs
    return (jnp.cos(ar), jnp.sin(ar), jnp.cos(ac), jnp.sin(ac))

def _rope1d(x, cos, sin):
    x1, x2 = jnp.split(x, 2, axis=-1)
    return jnp.concatenate([x1 * cos - x2 * sin, x1 * sin + x2 * cos], axis=-1)

def _rope2d(x, tabs):
    cr, sr, cc, sc = [t.astype(x.dtype) for t in tabs]
    if x.ndim == 4:
        cr, sr, cc, sc = cr[:, None], sr[:, None], cc[:, None], sc[:, None]
    xr, xc = jnp.split(x, 2, axis=-1)
    return jnp.concatenate([_rope1d(xr, cr, sr), _rope1d(xc, cc, sc)], axis=-1)

def _conv_mixer(h, w_in, dw, db, ln_g, ln_b, w_out):
    a, b, g = jnp.split(h @ w_in, 3, axis=-1)
    y = a * jax.nn.sigmoid(b)
    y = lax.conv_general_dilated(
        y, dw[:, None, :].astype(y.dtype), window_strides=(1,),
        padding=[(CONV_WIDTH // 2, CONV_WIDTH // 2)],
        dimension_numbers=('NWC', 'WIO', 'NWC'),
        feature_group_count=BRANCH) + db
    y = jax.nn.silu(_layernorm(y, ln_g, ln_b)) * jax.nn.silu(g)
    return y @ w_out

def _window_mean(v, w):
    L = v.shape[1]
    cs = jnp.pad(jnp.cumsum(v.astype(jnp.float32), axis=1), ((0, 0), (1, 0), (0, 0)))
    t = jnp.arange(L)
    start = jnp.clip(t - w // 2, 0, L)
    end = jnp.clip(t + (w - w // 2), 0, L)
    total = jnp.take(cs, end, axis=1) - jnp.take(cs, start, axis=1)
    cnt = (end - start).astype(jnp.float32)
    return (total / cnt[None, :, None]).astype(v.dtype)

def _pool_mixer(h, w_in, w_grp, scale, w_out):
    v, g = jnp.split(h @ w_in, 2, axis=-1)
    B, L, _ = v.shape
    vg = v.reshape(B, L, len(POOL_WINDOWS), POOL_GROUP)
    pooled = jnp.stack([_window_mean(vg[:, :, k], w) for k, w in enumerate(POOL_WINDOWS)], axis=2) - vg
    y = jnp.einsum('blgc,gcd->blgd', pooled, w_grp).reshape(B, L, BRANCH) * scale
    return (y * jax.nn.silu(g)) @ w_out

def _mla_keys(pkv, kv_norm, w_ukv, k_nope_g, k_rope_g, tabs):
    ckv, kr = jnp.split(pkv, [MLA_KV_RANK], axis=-1)
    B, L, _ = ckv.shape
    kv = (_rms(ckv, kv_norm) @ w_ukv).reshape(B, L, MLA_HEADS, MLA_NOPE + MLA_V)
    kn, v = jnp.split(kv, [MLA_NOPE], axis=-1)
    kn = _rms(kn, k_nope_g)
    kr = _rms(kr, k_rope_g)
    if tabs is not None:
        kr = _rope2d(kr, tabs)
    return kn, kr, v

def _mla_queries(cq, q_norm, w_uq, q_nope_g, q_rope_g, tabs):
    B, L, _ = cq.shape
    q = (_rms(cq, q_norm) @ w_uq).reshape(B, L, MLA_HEADS, MLA_NOPE + MLA_ROPE)
    qn, qr = jnp.split(q, [MLA_NOPE], axis=-1)
    qn = _rms(qn, q_nope_g)
    qr = _rms(qr, q_rope_g)
    if tabs is not None:
        qr = _rope2d(qr, tabs)
    return qn, qr

def _attend(qn, qr, kn, kr, v):
    s = (jnp.einsum('bqhd,bkhd->bhqk', qn, kn)
         + jnp.einsum('bqhr,bkr->bhqk', qr, kr)).astype(jnp.float32) * MLA_SCALE
    p = jax.nn.softmax(s, axis=-1).astype(v.dtype)
    return jnp.einsum('bhqk,bkhd->bqhd', p, v)

def _attend_blocks(qn, qr, kn, kr, v):
    B, L, H, _ = qn.shape
    nb = L // Q_BLOCK

    def blk(t):
        return jnp.moveaxis(t.reshape((B, nb, Q_BLOCK) + t.shape[2:]), 1, 0)

    out = lax.map(lambda q: _attend(q[0], q[1], kn, kr, v), (blk(qn), blk(qr)))
    return jnp.moveaxis(out, 0, 1).reshape(B, L, H * MLA_V)

def _mla_mixer(h, hc, with_ctx_out, tabs, w_in, q_norm, kv_norm, w_uq, w_ukv, nope_g, rope_g, w_out):
    pkv, cq, g = jnp.split(h @ w_in, [MLA_KVC, MLA_KVC + MLA_Q_RANK], axis=-1)
    kn, kr, v = _mla_keys(pkv, kv_norm, w_ukv, nope_g[1], rope_g[1], tabs)
    qn, qr = _mla_queries(cq, q_norm, w_uq, nope_g[0], rope_g[0], tabs)
    pc = hc @ (w_in if with_ctx_out else w_in[:, :MLA_KVC])
    knc, krc, vc = _mla_keys(pc[..., :MLA_KVC], kv_norm, w_ukv, nope_g[1], rope_g[1], None)
    o = _attend_blocks(qn, qr,
                       jnp.concatenate([kn, knc], axis=1),
                       jnp.concatenate([kr, krc], axis=1),
                       jnp.concatenate([v, vc], axis=1))
    out = (o * jax.nn.silu(g)) @ w_out
    out_c = None
    if with_ctx_out:
        cqc, gc = jnp.split(pc[..., MLA_KVC:], [MLA_Q_RANK], axis=-1)
        qnc, qrc = _mla_queries(cqc, q_norm, w_uq, nope_g[0], rope_g[0], None)
        Bc, Lc = hc.shape[0], hc.shape[1]
        oc = _attend(qnc, qrc, knc, krc, vc).reshape(Bc, Lc, MLA_HEADS * MLA_V)
        out_c = (oc * jax.nn.silu(gc)) @ w_out
    return out, out_c

def _chunk_mixer(h, w_in, ln_g, ln_b, w_s, b_s, w_out):
    u, v, g = jnp.split(h @ w_in, 3, axis=-1)
    B, L, _ = v.shape
    v = _layernorm(v, ln_g, ln_b).reshape(B, L // CHUNK, CHUNK, CHUNK_GROUPS, CHUNK_GC)
    s = jnp.einsum('gpq,bnqgc->bnpgc', w_s, v) + b_s[:, :, None]
    y = u * s.reshape(B, L, BRANCH) * jax.nn.silu(g)
    return y @ w_out

def first_inputs(seed: int = 0) -> dict:
    key = jax.random.key(seed)
    ks = iter(jax.random.split(key, 40))

    def nrm(shape, s):
        return jax.random.normal(next(ks), shape, jnp.float32) * s

    nA, nB, nC, nD = (_n_layers_of(k) for k in range(N_MIXERS))
    D, E = D_MODEL, BRANCH
    HQK = MLA_HEADS * (MLA_NOPE + MLA_ROPE)
    HKV = MLA_HEADS * (MLA_NOPE + MLA_V)
    HV = MLA_HEADS * MLA_V
    return {
        'x': nrm((BATCH, SEQ, D), 1.0),
        'c': nrm((BATCH, D), 1.0),
        'ctx': nrm((BATCH, CTX_LEN, D), 1.0),
        'c_ctx': nrm((D,), 1.0),
        'norm_g': 1.0 + nrm((DEPTH, D), 0.05),
        'w_mod': nrm((DEPTH, D, 3 * D), 0.5 * D ** -0.5),
        'b_mod': nrm((DEPTH, 3 * D), 0.01),
        'cv_w_in': nrm((nA, D, 3 * E), D ** -0.5),
        'cv_dw': nrm((nA, CONV_WIDTH, E), CONV_WIDTH ** -0.5),
        'cv_db': nrm((nA, E), 0.01),
        'cv_ln_g': 1.0 + nrm((nA, E), 0.05),
        'cv_ln_b': nrm((nA, E), 0.01),
        'cv_w_out': nrm((nA, E, D), E ** -0.5),
        'pl_w_in': nrm((nB, D, 2 * E), D ** -0.5),
        'pl_w_grp': nrm((nB, len(POOL_WINDOWS), POOL_GROUP, POOL_GROUP), POOL_GROUP ** -0.5),
        'pl_scale': 1.0 + nrm((nB, E), 0.05),
        'pl_w_out': nrm((nB, E, D), E ** -0.5),
        'ml_w_in': nrm((nC, D, MLA_KVC + MLA_Q_RANK + HV), D ** -0.5),
        'ml_q_norm': 1.0 + nrm((nC, MLA_Q_RANK), 0.05),
        'ml_kv_norm': 1.0 + nrm((nC, MLA_KV_RANK), 0.05),
        'ml_w_uq': nrm((nC, MLA_Q_RANK, HQK), MLA_Q_RANK ** -0.5),
        'ml_w_ukv': nrm((nC, MLA_KV_RANK, HKV), MLA_KV_RANK ** -0.5),
        'ml_nope_norm': 1.0 + nrm((nC, 2, MLA_NOPE), 0.05),
        'ml_rope_norm': 1.0 + nrm((nC, 2, MLA_ROPE), 0.05),
        'ml_w_out': nrm((nC, HV, D), HV ** -0.5),
        'ch_w_in': nrm((nD, D, 3 * E), D ** -0.5),
        'ch_ln_g': 1.0 + nrm((nD, E), 0.05),
        'ch_ln_b': nrm((nD, E), 0.01),
        'ch_w_s': nrm((nD, CHUNK_GROUPS, CHUNK, CHUNK), CHUNK ** -0.5),
        'ch_b_s': 1.0 + nrm((nD, CHUNK, CHUNK_GROUPS), 0.05),
        'ch_w_out': nrm((nD, E, D), E ** -0.5),
    }

def first_block(x, c, ctx, c_ctx, norm_g, w_mod, b_mod,
              cv_w_in, cv_dw, cv_db, cv_ln_g, cv_ln_b, cv_w_out,
              pl_w_in, pl_w_grp, pl_scale, pl_w_out,
              ml_w_in, ml_q_norm, ml_kv_norm, ml_w_uq, ml_w_ukv, ml_nope_norm, ml_rope_norm, ml_w_out,
              ch_w_in, ch_ln_g, ch_ln_b, ch_w_s, ch_b_s, ch_w_out):
    L = x.shape[1]
    ROWS = L // GRID_W
    tabs = _rope_tables(ROWS)
    s_lat = jax.nn.silu(c)
    s_ctx = jax.nn.silu(c_ctx)
    cx = ctx
    for i in range(DEPTH):
        kind, j = i % N_MIXERS, i // N_MIXERS
        ctx_out = any(k % N_MIXERS == MIX_MLA for k in range(i + 1, DEPTH))
        ctx_in = ctx_out or kind == MIX_MLA
        sh, sc, gt = jnp.split((s_lat @ w_mod[i] + b_mod[i])[:, None, :], 3, axis=-1)
        h = _rms(x, norm_g[i]) * (1.0 + sc) + sh
        if ctx_in:
            shc, scc, gtc = jnp.split(s_ctx @ w_mod[i] + b_mod[i], 3, axis=-1)
            hc = _rms(cx, norm_g[i]) * (1.0 + scc) + shc
        if kind == MIX_CONV:
            args = (cv_w_in[j], cv_dw[j], cv_db[j], cv_ln_g[j], cv_ln_b[j], cv_w_out[j])
            o = _conv_mixer(h, *args)
            oc = _conv_mixer(hc, *args) if ctx_out else None
        elif kind == MIX_POOL:
            args = (pl_w_in[j], pl_w_grp[j], pl_scale[j], pl_w_out[j])
            o = _pool_mixer(h, *args)
            oc = _pool_mixer(hc, *args) if ctx_out else None
        elif kind == MIX_MLA:
            o, oc = _mla_mixer(h, hc, ctx_out, tabs, ml_w_in[j], ml_q_norm[j], ml_kv_norm[j],
                               ml_w_uq[j], ml_w_ukv[j], ml_nope_norm[j], ml_rope_norm[j], ml_w_out[j])
        else:
            args = (ch_w_in[j], ch_ln_g[j], ch_ln_b[j], ch_w_s[j], ch_b_s[j], ch_w_out[j])
            o = _chunk_mixer(h, *args)
            oc = _chunk_mixer(hc, *args) if ctx_out else None
        x = x + gt * o
        if ctx_out:
            cx = cx + gtc * oc
    return x


DEPTH_2 = 1

SB_HEADS = 16
SB_HEAD_DIM = 64
SB_WIDTH = SB_HEADS * SB_HEAD_DIM
RET_HEADS = 4
RET_QK_DIM = 256
RET_V_DIM = 2 * RET_QK_DIM
RET_QK_WIDTH = RET_HEADS * RET_QK_DIM
RET_V_WIDTH = RET_HEADS * RET_V_DIM
N_BRANCH = 2
BLOCK = 128
D_FF = -(-8 * D_MODEL // (3 * 256)) * 256
ROPE_BASE = 10000.0
N_MOD = 6
IN_SPLITS = (SB_WIDTH, 2 * SB_WIDTH, 3 * SB_WIDTH,
             3 * SB_WIDTH + RET_QK_WIDTH,
             3 * SB_WIDTH + 2 * RET_QK_WIDTH,
             3 * SB_WIDTH + 2 * RET_QK_WIDTH + RET_V_WIDTH,
             3 * SB_WIDTH + 2 * RET_QK_WIDTH + 2 * RET_V_WIDTH)
IN_WIDTH = 3 * SB_WIDTH + 2 * RET_QK_WIDTH + 2 * RET_V_WIDTH + N_BRANCH * D_MODEL


def rmsnorm(t, g):
    tf = t.astype(jnp.float32)
    y = tf * lax.rsqrt(jnp.mean(tf * tf, axis=-1, keepdims=True) + EPS)
    return (y * g.astype(jnp.float32)).astype(t.dtype)

def head_rmsnorm(t):
    tf = t.astype(jnp.float32)
    return (tf * lax.rsqrt(jnp.mean(tf * tf, axis=-1, keepdims=True) + EPS)).astype(t.dtype)

def modulate(h, shift, scale):
    return h * (1.0 + scale[:, None, :]) + shift[:, None, :]

def rotary(t):
    s, d = t.shape[1], t.shape[-1]
    inv_freq = ROPE_BASE ** (-jnp.arange(0, d, 2, dtype=jnp.float32) / d)
    ang = jnp.arange(s, dtype=jnp.float32)[:, None] * inv_freq[None, :]
    cos = jnp.cos(ang)[None, :, None, :]
    sin = jnp.sin(ang)[None, :, None, :]
    t1, t2 = jnp.split(t.astype(jnp.float32), 2, axis=-1)
    return jnp.concatenate([t1 * cos - t2 * sin, t1 * sin + t2 * cos], axis=-1).astype(t.dtype)

def stick_breaking_attention(q, k, v):
    s_len = q.shape[2]
    scale = SB_HEAD_DIM ** -0.5
    outs = []
    for i in range(s_len // BLOCK):
        end = (i + 1) * BLOCK
        qb = q[:, :, i * BLOCK:end]
        kb = k[:, :, :end]
        vb = v[:, :, :end]
        z = jnp.einsum('bhtd,bhsd->bhts', qb, kb).astype(jnp.float32) * scale
        t_pos = i * BLOCK + jnp.arange(BLOCK)
        s_pos = jnp.arange(end)
        mask = s_pos[None, :] < t_pos[:, None]
        log_1m_beta = jnp.where(mask, jax.nn.log_sigmoid(-z), 0.0)
        after = lax.cumsum(log_1m_beta, axis=3, reverse=True) - log_1m_beta
        log_a = jax.nn.log_sigmoid(z) + after
        a = jnp.where(mask, jnp.exp(log_a), 0.0)
        outs.append(jnp.einsum('bhts,bhsd->bhtd', a.astype(v.dtype), vb))
    return jnp.concatenate(outs, axis=2)

def retention(q, k, v):
    out_dtype = v.dtype
    q = q.astype(jnp.float32)
    k = k.astype(jnp.float32)
    v = v.astype(jnp.float32)
    b, h, s_len, dk = q.shape
    dv = v.shape[-1]
    n_chunks = s_len // BLOCK
    log_gamma = jnp.log(1.0 - 2.0 ** (-5.0 - jnp.arange(h, dtype=jnp.float32)))
    idx = jnp.arange(BLOCK, dtype=jnp.float32)
    diff = idx[:, None] - idx[None, :]
    decay_mask = jnp.where(diff >= 0, jnp.exp(jnp.maximum(diff, 0.0) * log_gamma[:, None, None]), 0.0)
    query_decay = jnp.exp((idx + 1.0) * log_gamma[:, None])
    key_decay = jnp.exp((BLOCK - 1.0 - idx) * log_gamma[:, None])
    chunk_decay = jnp.exp(BLOCK * log_gamma)
    qc = q.reshape(b, h, n_chunks, BLOCK, dk)
    kc = k.reshape(b, h, n_chunks, BLOCK, dk)
    vc = v.reshape(b, h, n_chunks, BLOCK, dv)
    scores = jnp.einsum('bhncd,bhnmd->bhncm', qc, kc) * decay_mask[None, :, None]
    intra = jnp.einsum('bhncm,bhnme->bhnce', scores, vc)
    k_dec = kc * key_decay[None, :, None, :, None]

    def step(state, xs):
        q_i, k_i, v_i = xs
        cross = jnp.einsum('bhcd,bhde->bhce', q_i, state) * query_decay[None, :, :, None]
        state = state * chunk_decay[None, :, None, None] + jnp.einsum('bhcd,bhce->bhde', k_i, v_i)
        return state, cross

    xs = (jnp.moveaxis(qc, 2, 0), jnp.moveaxis(k_dec, 2, 0), jnp.moveaxis(vc, 2, 0))
    init = jnp.zeros((b, h, dk, dv), jnp.float32)
    _, cross = lax.scan(step, init, xs)
    out = intra + jnp.moveaxis(cross, 0, 2)
    return out.reshape(b, h, s_len, dv).astype(out_dtype)

def second_inputs(seed: int = 0) -> dict:
    key = jax.random.key(seed)
    ks = jax.random.split(key, 14)

    def nrm(k, shape, fan_in):
        return jax.random.normal(k, shape, jnp.float32) * (fan_in ** -0.5)

    x = jax.random.normal(ks[0], (BATCH, SEQ, D_MODEL), jnp.float32)
    c = jax.random.normal(ks[1], (BATCH, D_MODEL), jnp.float32)
    w_ada = nrm(ks[2], (DEPTH_2, D_MODEL, N_MOD * D_MODEL), D_MODEL)
    b_ada = 0.02 * jax.random.normal(ks[3], (DEPTH_2, N_MOD * D_MODEL), jnp.float32)
    g_norm1 = 1.0 + 0.02 * jax.random.normal(ks[4], (DEPTH_2, D_MODEL), jnp.float32)
    w_in = nrm(ks[5], (DEPTH_2, D_MODEL, IN_WIDTH), D_MODEL)
    b_branch = 0.02 * jax.random.normal(ks[6], (DEPTH_2, N_BRANCH * D_MODEL), jnp.float32)
    w_proj_sb = nrm(ks[7], (DEPTH_2, SB_WIDTH, D_MODEL), SB_WIDTH)
    w_proj_ret = nrm(ks[8], (DEPTH_2, RET_V_WIDTH, D_MODEL), RET_V_WIDTH)
    w_out = nrm(ks[9], (DEPTH_2, D_MODEL, D_MODEL), D_MODEL)
    g_norm2 = 1.0 + 0.02 * jax.random.normal(ks[10], (DEPTH_2, D_MODEL), jnp.float32)
    w_ffn_in = nrm(ks[11], (DEPTH_2, D_MODEL, 2 * D_FF), D_MODEL)
    w_ffn_out = nrm(ks[12], (DEPTH_2, D_FF, D_MODEL), D_FF)
    g_final = 1.0 + 0.02 * jax.random.normal(ks[13], (D_MODEL,), jnp.float32)
    return {'x': x, 'c': c, 'w_ada': w_ada, 'b_ada': b_ada, 'g_norm1': g_norm1,
            'w_in': w_in, 'b_branch': b_branch, 'w_proj_sb': w_proj_sb,
            'w_proj_ret': w_proj_ret, 'w_out': w_out, 'g_norm2': g_norm2,
            'w_ffn_in': w_ffn_in, 'w_ffn_out': w_ffn_out, 'g_final': g_final}

def second_block(x, c, w_ada, b_ada, g_norm1, w_in, b_branch, w_proj_sb, w_proj_ret,
              w_out, g_norm2, w_ffn_in, w_ffn_out, g_final):
    b, s_len, _ = x.shape
    c_act = jax.nn.silu(c)
    for l in range(DEPTH_2):
        mod = jnp.einsum('bd,de->be', c_act, w_ada[l]) + b_ada[l]
        shift1, scale1, gate1, shift2, scale2, gate2 = jnp.split(mod, N_MOD, axis=-1)

        hmix = modulate(rmsnorm(x, g_norm1[l]), shift1, scale1)
        proj = jnp.einsum('bsd,de->bse', hmix, w_in[l])
        sb_q, sb_k, sb_v, r_q, r_k, r_v, r_g, br = jnp.split(proj, IN_SPLITS, axis=-1)

        def sb_heads(t):
            return t.reshape(b, s_len, SB_HEADS, SB_HEAD_DIM).transpose(0, 2, 1, 3)
        o_sb = stick_breaking_attention(sb_heads(sb_q), sb_heads(sb_k), sb_heads(sb_v))
        o_sb = o_sb.transpose(0, 2, 1, 3).reshape(b, s_len, SB_WIDTH)

        rq = rotary(r_q.reshape(b, s_len, RET_HEADS, RET_QK_DIM))
        rk = rotary(r_k.reshape(b, s_len, RET_HEADS, RET_QK_DIM)) * (RET_QK_DIM ** -0.5)
        rv = r_v.reshape(b, s_len, RET_HEADS, RET_V_DIM)
        o_ret = retention(rq.transpose(0, 2, 1, 3), rk.transpose(0, 2, 1, 3), rv.transpose(0, 2, 1, 3))
        o_ret = head_rmsnorm(o_ret.transpose(0, 2, 1, 3)).reshape(b, s_len, RET_V_WIDTH)
        o_ret = jax.nn.silu(r_g) * o_ret

        g_sb, g_ret = jnp.split(jax.nn.sigmoid(br + b_branch[l]), N_BRANCH, axis=-1)
        merged = (g_sb * jnp.einsum('bse,ed->bsd', o_sb, w_proj_sb[l])
                  + g_ret * jnp.einsum('bse,ed->bsd', o_ret, w_proj_ret[l]))
        x = x + gate1[:, None, :] * jnp.einsum('bsd,de->bse', merged, w_out[l])

        hffn = modulate(rmsnorm(x, g_norm2[l]), shift2, scale2)
        a, u = jnp.split(jnp.einsum('bsd,df->bsf', hffn, w_ffn_in[l]), 2, axis=-1)
        x = x + gate2[:, None, :] * jnp.einsum('bsf,fd->bsd', jax.nn.silu(a) * u, w_ffn_out[l])

    return rmsnorm(x, g_final)


def setup_inputs(seed=0):
    out = dict(first_inputs(seed))
    for name, value in second_inputs(seed + 1).items():
        if name != "x":
            out[name + "_2"] = value
    return out


def reference(
    x, c, ctx, c_ctx, norm_g, w_mod, b_mod, cv_w_in, cv_dw, cv_db, cv_ln_g, cv_ln_b, cv_w_out,
    pl_w_in, pl_w_grp, pl_scale, pl_w_out, ml_w_in, ml_q_norm, ml_kv_norm, ml_w_uq, ml_w_ukv,
    ml_nope_norm, ml_rope_norm, ml_w_out, ch_w_in, ch_ln_g, ch_ln_b, ch_w_s, ch_b_s, ch_w_out,
    c_2, w_ada_2, b_ada_2, g_norm1_2, w_in_2, b_branch_2, w_proj_sb_2, w_proj_ret_2, w_out_2,
    g_norm2_2, w_ffn_in_2, w_ffn_out_2, g_final_2,
):
    x = first_block(
        x, c, ctx, c_ctx, norm_g, w_mod, b_mod, cv_w_in, cv_dw, cv_db, cv_ln_g, cv_ln_b,
        cv_w_out, pl_w_in, pl_w_grp, pl_scale, pl_w_out, ml_w_in, ml_q_norm, ml_kv_norm,
        ml_w_uq, ml_w_ukv, ml_nope_norm, ml_rope_norm, ml_w_out, ch_w_in, ch_ln_g, ch_ln_b,
        ch_w_s, ch_b_s, ch_w_out,
    )
    return second_block(
        x, c_2, w_ada_2, b_ada_2, g_norm1_2, w_in_2, b_branch_2, w_proj_sb_2, w_proj_ret_2,
        w_out_2, g_norm2_2, w_ffn_in_2, w_ffn_out_2, g_final_2,
    )


_drawn_inputs = setup_inputs


def setup_inputs(seed=0):
    import zlib

    import numpy as np

    out = dict(_drawn_inputs(seed))
    spreads = {}
    factors = {'norm_g': 3.2,
     'b_mod': 5.792,
     'cv_db': 8.0,
     'cv_ln_g': 7.122,
     'cv_ln_b': 8.0,
     'pl_scale': 5.311,
     'g_norm1_2': 13.561,
     'b_branch_2': 62.926,
     'g_norm2_2': 13.07,
     'g_final_2': 8.145}
    for name, (base, spread) in spreads.items():
        noise = np.random.default_rng([zlib.crc32(name.encode()), seed]).standard_normal(out[name].shape)
        drawn = base * np.exp(spread * noise) if base else spread * noise
        out[name] = jnp.asarray(drawn.astype(out[name].dtype))
    for name, factor in factors.items():
        out[name] = (out[name] * factor).astype(out[name].dtype)
    return out
```

```python
from contextlib import ExitStack

import numpy as np

import concourse.bass as bass
from concourse import mybir

P = 128
D = 1024
T = 512
KB = D // P
TB = T // P
TILE_W = 256
CONV_W = 31
PAD = CONV_W // 2
POOL_PAD = 8
D_FF = 2816
FFB = D_FF // P
EPS = 1e-6
NEG_BIG = -1e30
SB_SCALE = 64 ** -0.5
RK_SCALE = 256 ** -0.5
RET_HEADS = 4

F32 = mybir.dt.float32
F32R = mybir.dt.float32r
ALU = mybir.AluOpType
ACT = mybir.ActivationFunctionType

N_CONV = 0
N_CONV_OUT = N_CONV + 12
N_POOL = N_CONV_OUT + 4
N_GRP = N_POOL + 8
N_POOL_OUT = N_GRP + 1
N_SB = N_POOL_OUT + 4
N_SB_OUT = N_SB + 12
N_RET1 = N_SB_OUT + 8
N_RETP = N_RET1 + 12
N_RET2 = N_RETP + 4
N_GATE = N_RET2 + 12
N_MERGE = N_GATE + 4
N_OUT = N_MERGE + 4
N_FFN = N_OUT + 4
N_FFN_OUT = N_FFN + 22
N_TILES = N_FFN_OUT + 12

MOD_G = 512
MOD_ROUND = 3 * D
ROUND_GROUPS = MOD_ROUND // MOD_G
N_MOD_GROUPS = 4 * ROUND_GROUPS
DVE_GROUPS = 4

COLS = {}
_at = 0
for _name, _n in (("norm_g", 16), ("b_mod", 48), ("b_ada", 48), ("cv_db", 8), ("cv_ln_g", 8),
                  ("cv_ln_b", 8), ("pl_scale", 8), ("g_norm1", 8), ("g_norm2", 8), ("g_final", 8),
                  ("b_branch", 16), ("c", 8), ("c_2", 8), ("dw", 8 * CONV_W)):
    COLS[_name] = _at
    _at += _n
N_COLS = _at

C_MEAN, C_EYE, C_NEG, C_NTRI, C_NONE, C_POOL = (P * i for i in range(6))
N_CONST = C_POOL + 4 * 16


def z_off(j):
    return {0: 0, 1: 512, 3: 896, 2: 1024}[j]


Z_W = 1280


def build_program(nc, w_stream, mod_stream, x_in, cols_in, const_in, rope_in, decay_in, x_spill, out):
    with ExitStack() as ctx:
        base = 16512

        def place(name, at, n, dt):
            assert at + 4 * n <= 229344 - base, (name, at + 4 * n)
            return nc.alloc_sbuf_tensor_at(name, [P, n], dt, offset=base + at)

        def blocks(t, w):
            return t[:, :].rearrange("p (b w) -> p b w", w=w)

        def sem(name):
            return ctx.enter_context(nc.semaphore(name))

        K = 1024
        w_raw = place("w_raw", 0, 4096, F32)[:, :].rearrange("p (s k c) -> p s k c", s=2, k=KB)
        w_hi = place("w_hi", 16 * K, 4096, F32R)[:, :].rearrange("p (s k c) -> p s k c", s=2, k=KB)
        w_lo = place("w_lo", 32 * K, 4096, F32R)[:, :].rearrange("p (s k c) -> p s k c", s=2, k=KB)
        h_hi = blocks(place("h_hi", 48 * K, 4096, F32R), T)
        h_lo = blocks(place("h_lo", 64 * K, 4096, F32R), T)
        x_flat = place("x_sb", 80 * K, 4096, F32)
        x_sb = blocks(x_flat, T)
        rs = place("rs", 96 * K, 512, F32)
        cols = place("cols", 98 * K, N_COLS, F32)
        at = (98 * K + 4 * N_COLS + 31) // 32 * 32
        mods = place("mods", at, 96, F32)
        gp = place("gp", at + 4 * 96, 8, F32)
        csil = place("csil", at + 4 * 104, 16, F32)
        at = at + 4 * 120
        mean_m = place("mean_m", at, P, F32)
        pool_edge = place("pool_edge", at + 512, 64, F32)
        eye_r = place("eye_r", at + 768, P, F32R)
        neg_r = place("neg_r", at + 1280, P, F32R)
        ntri_r = place("ntri_r", at + 1792, P, F32R)
        none_r = place("none_r", at + 2304, P, F32R)
        ones_c = place("ones_c", at + 2816, 2, F32)
        eps_c = place("eps_c", at + 2848, 1, F32)
        var = at + 2880

        g_hi = blocks(place("g_hi", var, 4096, F32R), T)
        g_lo = blocks(place("g_lo", var + 16 * K, 4096, F32R), T)
        v = var + 32 * K
        mod_acc = place("mod_acc", v, MOD_ROUND, F32)
        mod_chunk = place("mod_chunk", v + 12 * K, 2048, F32)[:, :].rearrange("p (s k c) -> p s k c", s=2, k=2)
        v1 = v + 20 * K
        y_flat = place("y_sb", v1, 4096, F32)
        y_sb = blocks(y_flat, T)
        gs_flat = place("gs_sb", v1 + 16 * K, 4096, F32)
        gs_sb = blocks(gs_flat, T)
        first_chunk = [t[:, :].rearrange("p (s k c) -> p s k c", s=4, k=2) for t in (y_flat, gs_flat)]
        sa = blocks(place("sa", v1 + 32 * K, 2048, F32), T)
        sq = blocks(place("sq", v1 + 40 * K, 1024, F32), T)
        ypad = place("ypad", var, 2 * (T + 2 * PAD), F32)[:, :].rearrange("p (m t) -> p m t", m=2)
        c_stage = place("c_stage", var + 8 * K, N_CONST, F32)
        PW = T + 2 * POOL_PAD
        vpad = place("vpad", v1, 2 * PW, F32)[:, :].rearrange("p (m t) -> p m t", m=2)
        pool_a = place("pool_a", v1 + 8 * PW, 2 * PW, F32)[:, :].rearrange("p (m t) -> p m t", m=2)
        pool_b = place("pool_b", v1 + 16 * PW, 2 * PW, F32)[:, :].rearrange("p (m t) -> p m t", m=2)

        names = ("q_hi", "q_lo", "k_hi", "k_lo", "v_hi", "v_lo")
        sbq_hi, sbq_lo, sbk_hi, sbk_lo, sbv_hi, sbv_lo = (
            place(f"sb{n}", v1 + 4 * K * i, 1024, F32R) for i, n in enumerate(names))
        sbq_hi, sbq_lo, sbk_hi, sbk_lo = (blocks(t, T) for t in (sbq_hi, sbq_lo, sbk_hi, sbk_lo))
        sbv_hi, sbv_lo = (blocks(t, TILE_W) for t in (sbv_hi, sbv_lo))
        att_hi = blocks(place("att_hi", v1 + 24 * K, 2 * Z_W, F32R), Z_W)
        att_lo = blocks(place("att_lo", v1 + 34 * K, 2 * Z_W, F32R), Z_W)
        z_tmp = x_flat[:, 0:2 * Z_W].rearrange("p (s z) -> p s z", s=2)
        mg = x_sb
        gate_t = blocks(place("gate_t", v1, 1024, F32), T)
        pr = blocks(place("pr", v, 4096, F32), T)
        rq_hi, rq_lo, rk_hi, rk_lo = (
            blocks(place(f"r{n}", v + (16 + 4 * i) * K, 1024, F32R), T) for i, n in enumerate(names[:4]))
        rv_hi, rv_lo = (blocks(place(f"r{n}", v + (32 + 8 * i) * K, 2048, F32R), T) for i, n in enumerate(names[4:]))
        s_hi, s_lo = (place(f"s_{n}", v + 48 * K + 5 * K * i, Z_W, F32R) for i, n in enumerate(("hi", "lo")))
        rope = blocks(place("rope", v + 58 * K, 1024, F32), T)
        decay = place("decay", v + 62 * K, T, F32)
        rt = blocks(place("rt", v + 64 * K, 2048, F32), T)
        gates = blocks(place("gates", v + 16 * K, 4096, F32), T)
        nt = blocks(place("nt", v + 48 * K, 2048, F32), T)
        nsq = blocks(place("nsq", v + 56 * K, 1024, F32), T)
        f_hi = blocks(place("f_hi", var, FFB * T, F32R), T)
        f_lo = blocks(place("f_lo", var + 2 * K * FFB, FFB * T, F32R), T)
        ft = blocks(place("ft", var + 4 * K * FFB, 2048, F32), T)
        fsq = blocks(place("fsq", var + 4 * K * FFB + 8 * K, 1024, F32), T)

        ps = ctx.enter_context(nc.psum_tensor("ps", [P, 2, 2, T], F32))
        at_ps = ctx.enter_context(nc.psum_tensor("at_ps", [P, 4, T], F32))
        ps_tok = ps[:, :, :, :].rearrange("p s m (h c) -> p s (m h) c", c=TILE_W)
        ps_flat = ps[:, :, :, :].rearrange("p s m t -> p (s m t)")
        at_flat = at_ps[:, :, :].rearrange("p b t -> p (b t)")
        z_ps = (at_flat, ps_flat)

        cols_in_s, x_in_s, const_in_s = sem("cols_loaded"), sem("x_loaded"), sem("consts_loaded")
        w_landed = [sem("w_landed_even"), sem("w_landed_odd")]
        first_in = [sem(f"first_chunk_loaded_{i}") for i in range(8)]
        chunk_in = [sem("mod_chunk_loaded_even"), sem("mod_chunk_loaded_odd")]
        w_hi_done, w_lo_done = sem("w_hi_done"), sem("w_lo_done")
        tile_done = sem("tile_done")
        csil_done, consts_done, pads_done = sem("csil_done"), sem("consts_done"), sem("pads_done")
        first_mod = sem("first_mod")
        mod_step = sem("mod_step")
        mod_summed, mods_ready, gp_ready = sem("mod_summed"), sem("mods_ready"), sem("gp_ready")
        x_updated = sem("x_updated")
        sq_ready, sq_used, root_ready, rs_ready = sem("sq_ready"), sem("sq_used"), sem("root_ready"), sem("rs_ready")
        t_ready, h_hi_ready, h_lo_ready = sem("t_ready"), sem("h_hi_ready"), sem("h_lo_ready")
        a_copied, sig_ready, y_ready, conv_step = sem("a_copied"), sem("sig_ready"), sem("y_ready"), sem("conv_step")
        conv_summed, centred, ln_z, ln_w = sem("conv_summed"), sem("centred"), sem("ln_z"), sem("ln_w")
        gs_ready = sem("gs_ready")
        v_copied, pool_step, pooled = sem("v_copied"), sem("pool_step"), sem("pooled")
        g_hi_ready, g_lo_ready = sem("g_hi_ready"), sem("g_lo_ready")
        grp_done, grp_y = sem("grp_done"), sem("grp_y")
        x_spilled, x_back = sem("x_spilled"), sem("x_back")
        qkv_hi, qkv_lo = sem("qkv_hi"), sem("qkv_lo")
        z_done, stick_step, stick_ln = sem("z_done"), sem("stick_step"), sem("stick_ln")
        sp_step, sp_split = sem("sp_step"), sem("sp_split")
        after_done, a_exp, a_step, a_split = sem("after_done"), sem("a_exp"), sem("a_step"), sem("a_split")
        o_done, o_hi_ready, o_lo_ready = sem("o_done"), sem("o_hi_ready"), sem("o_lo_ready")
        gate_ready, mg_ready = sem("gate_ready"), sem("mg_ready")
        rope_in_s, decay_in_s = sem("rope_loaded"), sem("decay_loaded")
        rot_step, rot_hi, rot_lo = sem("rot_step"), sem("rot_hi"), sem("rot_lo")
        rv_hi_ready, rv_lo_ready = sem("rv_hi_ready"), sem("rv_lo_ready")
        s_done, s_decayed, s_hi_ready, s_lo_ready = sem("s_done"), sem("s_decayed"), sem("s_hi_ready"), sem("s_lo_ready")
        ro_done, ro_sq, ro_stat, ro_root, ro_rs = sem("ro_done"), sem("ro_sq"), sem("ro_stat"), sem("ro_root"), sem("ro_rs")
        ro_norm, ro_silu, ro_w = sem("ro_norm"), sem("ro_silu"), sem("ro_w")
        pr_ready, merge_step = sem("pr_ready"), sem("merge_step")
        ff_silu, ff_prod, ff_hi, ff_lo = sem("ff_silu"), sem("ff_prod"), sem("ff_hi"), sem("ff_lo")
        out_stored = sem("out_stored")

        SQ_RING = 2

        def sq_buf(u):
            return {0: sq, 1: sq, 2: sq, 3: sq, 4: nsq, 5: fsq}[u]

        def t_buf(u):
            return {0: sa, 1: sa, 2: sa, 3: sa, 4: nt, 5: ft}[u]

        def x_count(u, k):
            return 8 * {2: 0, 3: 1, 4: 2, 5: 3}[u] + k + 1

        def mod_col(r, part, k):
            return 24 * r + 8 * part + k

        SHIFT = {0: (0, 0), 2: (1, 0), 3: (2, 0), 4: (3, 0)}
        GAIN = {0: "norm_g", 2: "norm_g", 3: "g_norm1", 4: "g_norm2"}
        GAIN_AT = {0: 0, 2: 8, 3: 0, 4: 0}
        FILL = {0: 0, 1: 1, 2: 2, 3: 4, 4: 6}
        GATE = {"conv": (0, 2), "pool": (1, 2), "out": (2, 2), "ffn": (3, 2)}

        block = ctx.enter_context(nc.Block())

        @block.sync
        def _(sp):
            sp.dma_start(cols[:, :], cols_in).then_inc(cols_in_s, 16)
            sp.dma_start(x_sb, x_in).then_inc(x_in_s, 16)
            sp.dma_start(c_stage[:, :], const_in).then_inc(const_in_s, 16)
            for n in range(2):
                sp.dma_start(w_raw[:, n], w_stream[n]).then_inc(w_landed[n], 16)

            def load(n, slot):
                sp.wait_ge(w_lo_done, n - 1)
                sp.dma_start(w_raw[:, slot], w_stream[n]).then_inc(w_landed[slot], 16)

            with sp.Fori(1, N_TILES // 2) as i:
                load(2 * i, 0)
                load(2 * i + 1, 1)
            load(N_TILES - 1, (N_TILES - 1) % 2)

        @block.gpsimd
        def _(pool):
            pool.wait_ge(csil_done, 2)

            def group(g, col, step0, seq0, c_at):
                for q in range(4):
                    slot = q % 2
                    if q >= 2:
                        pool.wait_ge(mod_step, step0 + 4 * (q - 1))
                    else:
                        pool.wait_ge(mod_step, step0)
                    pool.dma_start(mod_chunk[:, slot], mod_stream[g, q]).then_inc(chunk_in[slot], 16)
                    pool.wait_ge(chunk_in[slot], seq0 + 16 * (q // 2) + 16)
                    acc = mod_acc[:, col:col + MOD_G]
                    for b in range(2):
                        kb = 2 * q + b
                        c = csil[:, c_at + kb:c_at + kb + 1]
                        nc.gpsimd.tensor_scalar(mod_chunk[:, slot, b], mod_chunk[:, slot, b], c, 1.0,
                                                ALU.mult, ALU.mult).then_inc(mod_step, 1)
                        pool.wait_ge(mod_step, step0 + 2 * kb + 1)
                        if kb == 0:
                            nc.gpsimd.tensor_copy(acc, mod_chunk[:, slot, b]).then_inc(mod_step, 1)
                            continue
                        nc.gpsimd.tensor_tensor(acc, acc, mod_chunk[:, slot, b], ALU.add).then_inc(mod_step, 1)

            nc.gpsimd.memset(ones_c[:, :], 1.0).then_inc(mod_step, 1)
            before = 0
            for r in range(4):
                if r:
                    pool.wait_ge(mod_summed, r + 1)
                for i in range(0 if r else DVE_GROUPS, ROUND_GROUPS):
                    group(i + ROUND_GROUPS * r, i * MOD_G, 16 * before + 1, 32 * before, 0 if r < 2 else 8)
                    before += 1

        def mod_steps(r):
            return 16 * (ROUND_GROUPS * (r + 1) - DVE_GROUPS) + 1

        @block.tensor
        def _(pe):
            def three(out_ap, a_hi, a_lo, b_hi, b_lo, start, stop, inc=None):
                nc.tensor.matmul(out_ap, a_hi, b_hi, start=start, stop=False, skip_group_check=True)
                nc.tensor.matmul(out_ap, a_hi, b_lo, start=False, stop=False, skip_group_check=True)
                last = nc.tensor.matmul(out_ap, a_lo, b_hi, start=False, stop=stop, skip_group_check=True)
                if inc is not None:
                    last.then_inc(inc, 1)

            def split_ready(n):
                pe.wait_ge(w_hi_done, n + 1)
                pe.wait_ge(w_lo_done, n + 1)

            def tile(n, slot, src_hi, src_lo, before_block=None, kbs=KB, k0=0, first=True, last=True, bank=None):
                split_ready(n)
                bank = slot if bank is None else bank
                for m in range(2):
                    for k in range(kbs):
                        if m == 0 and before_block is not None:
                            before_block(k)
                        c = slice(P * m, P * m + P)
                        three(ps[:, bank, m, :], w_hi[:, slot, k, c], w_lo[:, slot, k, c],
                              src_hi[:, k0 + k, :], src_lo[:, k0 + k, :],
                              first and k == 0, last and k == kbs - 1,
                              tile_done if m == 1 and k == kbs - 1 else None)

            def tile_tokens(n, slot):
                split_ready(n)
                for tb in range(TB):
                    for k in range(KB):
                        c = slice(P * tb, P * tb + P)
                        three(ps_tok[:, slot, tb, :], h_hi[:, k, c], h_lo[:, k, c],
                              w_hi[:, slot, k, :], w_lo[:, slot, k, :], k == 0, k == KB - 1,
                              tile_done if tb == TB - 1 and k == KB - 1 else None)

            def h_block(fill):
                return lambda k: pe.wait_ge(h_lo_ready, 8 * fill + k + 1)

            def norm_stat(u, k):
                pe.wait_ge(sq_ready, 8 * u + k + 1)
                if u and k == 0:
                    pe.wait_ge(root_ready, u)
                nc.tensor.matmul(at_ps[:, 0, :], mean_m[:, :], sq_buf(u)[:, k % SQ_RING, :], start=(k == 0),
                                 stop=(k == KB - 1), skip_group_check=True).then_inc(sq_used, 1)

            def mod_sum(r, b0, nb, ready, count):
                pe.wait_ge(ready, count)
                for b in range(nb):
                    last = nc.tensor.matmul(at_ps[:, 3, b:b + 1], mod_acc[:, P * (b0 + b):P * (b0 + b + 1)],
                                            ones_c[:, 0:1], start=True, stop=True, skip_group_check=True)
                last.then_inc(mod_summed, 1)

            def update_tiles(n0, fill, u, src_hi=h_hi, src_lo=h_lo, ready=None):
                for j in range(4):
                    tile(n0 + j, (n0 + j) % 2, src_hi, src_lo, ready if j == 0 else None)
                    if j:
                        norm_stat(u, 2 * j - 2)
                        norm_stat(u, 2 * j - 1)
                norm_stat(u, 6)
                norm_stat(u, 7)

            pe.wait_ge(consts_done, 1)
            for k in range(KB):
                norm_stat(0, k)
            pe.wait_ge(mod_step, 1)
            mod_sum(0, 0, 16, first_mod, 4 * KB)

            for j in range(4):
                for i in range(3):
                    n = N_CONV + 3 * j + i
                    tile(n, n % 2, h_hi, h_lo, h_block(0) if n == 0 else None)
                if j == 1:
                    pe.wait_ge(mods_ready, 1)
                    mod_sum(0, 16, 8, mod_step, mod_steps(0))
            for k in range(KB):
                pe.wait_ge(conv_step, CONV_W * (k + 1))
                nc.tensor.matmul(at_ps[:, 1, :], mean_m[:, :], y_sb[:, k, :], start=(k == 0), stop=(k == KB - 1),
                                 skip_group_check=True).then_inc(conv_summed, 1)
            for k in range(KB):
                norm_stat(1, k)
            pe.wait_ge(mods_ready, 2)
            mod_sum(1, 0, 24, mod_step, mod_steps(1))
            update_tiles(N_CONV_OUT, 1, 2, ready=h_block(1))

            tile(N_POOL, 0, h_hi, h_lo, h_block(2))
            tile(N_POOL + 1, 1, h_hi, h_lo)
            with pe.Fori(1, 4) as i:
                tile(2 * i + N_POOL, 0, h_hi, h_lo)
                tile(2 * i + N_POOL + 1, 1, h_hi, h_lo)
            pe.wait_ge(mods_ready, 3)
            split_ready(N_GRP)
            for g in range(4):
                pe.wait_ge(g_lo_ready, 2 * g + 2)
                if g == 0:
                    pe.wait_ge(w_hi_done, N_GRP + 2)
                for m in range(2):
                    out_ap = (ps[:, 1, m, :], at_ps[:, m, :], at_ps[:, 2 + m, :], ps[:, 0, m, :])[g]
                    for k in range(2):
                        c = slice(P * m, P * m + P)
                        three(out_ap, w_hi[:, 0, 2 * g + k, c], w_lo[:, 0, 2 * g + k, c], g_hi[:, 2 * g + k, :],
                              g_lo[:, 2 * g + k, :], k == 0, k == 1,
                              (tile_done if g == 3 and m == 1 else grp_done) if k == 1 else None)
            update_tiles(N_POOL_OUT, 3, 3, ready=h_block(3))
            pe.wait_ge(mods_ready, 3)
            mod_sum(2, 0, 24, mod_step, mod_steps(2))

            def scores(hd, base_z):
                rows, zp = slice(64 * (hd % 2), 64 * (hd % 2) + 64), z_ps[hd % 2]
                blk = hd // 2
                for j in range(TB):
                    w = T - P * j
                    z = zp[:, z_off(j):z_off(j) + w]
                    three(z, sbk_hi[rows, blk, P * j:P * j + P], sbk_lo[rows, blk, P * j:P * j + P],
                          sbq_hi[rows, blk, P * j:T], sbq_lo[rows, blk, P * j:T], j < 3, False)
                    last = nc.tensor.matmul(z[:, 0:P], eye_r[:, :], neg_r[:, :], start=False, stop=False,
                                            skip_group_check=True)
                last.then_inc(z_done, 1)

            def subtract_after(hd, want):
                pe.wait_ge(sp_split, want)
                zp = z_ps[hd % 2]
                for part in (att_hi, att_lo):
                    for j in range(TB):
                        for j2 in range(j, TB):
                            w = T - P * j2
                            o = z_off(j) + P * (j2 - j)
                            last = nc.tensor.matmul(zp[:, o:o + w], (ntri_r if j2 == j else none_r)[:, :],
                                                    part[:, hd % 2, z_off(j2):z_off(j2) + w],
                                                    start=False, stop=False, skip_group_check=True)
                last.then_inc(after_done, 1)

            def attend(hd, want):
                pe.wait_ge(a_split, want)
                c = slice(P * (hd // 2), P * (hd // 2) + P)
                op = z_ps[hd % 2]
                for j in range(TB):
                    w = T - P * j
                    three(op[:, 1536 + P * j:2048], sbv_hi[:, j, c], sbv_lo[:, j, c],
                          att_hi[:, hd % 2, z_off(j):z_off(j) + w], att_lo[:, hd % 2, z_off(j):z_off(j) + w],
                          j == 0, j == TB - 1, o_done if j == TB - 1 else None)

            def stick_group(grp, n, parity, ready=None):
                tile(n, parity, h_hi, h_lo, ready)
                tile(n + 1, 1 - parity, h_hi, h_lo)
                tile_tokens(n + 2, parity)
                pe.wait_ge(qkv_hi, grp * 3 + 3)
                pe.wait_ge(qkv_lo, grp * 3 + 3)
                hd0 = grp * 4
                scores(0, hd0)
                scores(1, hd0)
                for pair in range(2):
                    subtract_after(0, hd0 + 2 * pair + 1)
                    subtract_after(1, hd0 + 2 * pair + 2)
                    for s in range(2):
                        attend(2 * pair + s, hd0 + 2 * pair + s + 1)
                        if pair == 0:
                            scores(2 + s, hd0)
                pe.wait_ge(o_lo_ready, hd0 + 4)

            stick_group(0, N_SB, N_SB % 2, h_block(4))
            stick_group(1, N_SB + 3, (N_SB + 3) % 2)
            with pe.Fori(1, 2) as i:
                stick_group(2 * i, 6 * i + N_SB, N_SB % 2)
                stick_group(2 * i + 1, 6 * i + N_SB + 3, (N_SB + 3) % 2)

            def gated(n, parity):
                tile(n, parity, h_hi, h_lo)
                tile(n + 1, 1 - parity, g_hi, g_lo)

            with pe.Fori(0, 4) as i:
                gated(2 * i + N_SB_OUT, N_SB_OUT % 2)
            pe.wait_ge(mods_ready, 4)
            mod_sum(3, 0, 24, mod_step, mod_steps(3))

            def head(hd, n, parity):
                tile(n, parity, h_hi, h_lo)
                tile(n + 1, 1 - parity, h_hi, h_lo)
                tile_tokens(n + 2, parity)
                pe.wait_ge(rot_lo, hd * 4 + 4)
                for j in range(TB):
                    w = T - P * j
                    for c in range(2):
                        three(at_ps[:, j, 0:w], rk_hi[:, c, P * j:P * j + P], rk_lo[:, c, P * j:P * j + P],
                              rq_hi[:, c, P * j:T], rq_lo[:, c, P * j:T], c == 0, c == 1, s_done if c == 1 else None)
                tile_tokens(n + 3, 1 - parity)
                pe.wait_ge(rv_lo_ready, hd * 2 + 2)
                pe.wait_ge(s_lo_ready, hd * 4 + 4)
                for e in range(4):
                    for j in range(TB):
                        w = T - P * j
                        three(at_ps[:, e, P * j:T], rv_hi[:, j, P * e:P * e + P], rv_lo[:, j, P * e:P * e + P],
                              s_hi[:, z_off(j):z_off(j) + w], s_lo[:, z_off(j):z_off(j) + w],
                              j == 0, j == TB - 1, ro_done if j == TB - 1 else None)
                tile(n + 4, parity, h_hi, h_lo)
                for e in range(4):
                    pe.wait_ge(ro_sq, hd * 4 + e + 1)
                    nc.tensor.matmul(ps[:, 1 - parity, 0, :], mean_m[:, :], rt[:, e % 2, :], start=(e == 0), stop=(e == 3),
                                     skip_group_check=True).then_inc(ro_stat, 1)
                pe.wait_ge(ro_root, hd + 1)
                tile(n + 5, 1 - parity, h_hi, h_lo)

            with pe.Fori(0, 2) as i:
                head(i, i * 6 + N_RET1, N_RET1 % 2)
            pe.wait_ge(o_lo_ready, 16 + 8)
            with pe.Fori(0, 2) as i:
                tile(2 * i + N_RETP, N_RETP % 2, g_hi, g_lo)
                tile(2 * i + N_RETP + 1, (N_RETP + 1) % 2, g_hi, g_lo)
            with pe.Fori(0, 2) as i:
                head(i + 2, i * 6 + N_RET2, N_RET2 % 2)
            with pe.Fori(0, 2) as i:
                tile(2 * i + N_GATE, N_GATE % 2, h_hi, h_lo)
                tile(2 * i + N_GATE + 1, (N_GATE + 1) % 2, h_hi, h_lo)
            pe.wait_ge(o_lo_ready, 16 + 16)
            with pe.Fori(0, 2) as i:
                tile(2 * i + N_MERGE, N_MERGE % 2, g_hi, g_lo)
                tile(2 * i + N_MERGE + 1, (N_MERGE + 1) % 2, g_hi, g_lo)
            update_tiles(N_OUT, 5, 4, ready=h_block(5))

            tile(N_FFN, N_FFN % 2, h_hi, h_lo, h_block(6))
            tile(N_FFN + 1, (N_FFN + 1) % 2, h_hi, h_lo)
            with pe.Fori(1, 11) as i:
                tile(2 * i + N_FFN, N_FFN % 2, h_hi, h_lo)
                tile(2 * i + N_FFN + 1, (N_FFN + 1) % 2, h_hi, h_lo)

            def ffn_out(n, parity, bank, ready=None):
                tile(n, parity, f_hi, f_lo, ready, first=True, last=False, bank=bank)
                tile(n + 1, 1 - parity, f_hi, f_lo, ready, k0=8, first=False, last=False, bank=bank)
                tile(n + 2, parity, f_hi, f_lo, ready, kbs=FFB - 16, k0=16, first=False, last=True, bank=bank)

            pe.wait_ge(ff_lo, FFB)
            for j in range(4):
                n = N_FFN_OUT + 3 * j
                ffn_out(n, n % 2, j % 2)
                if j:
                    norm_stat(5, 2 * j - 2)
                    norm_stat(5, 2 * j - 1)
            norm_stat(5, 6)
            norm_stat(5, 7)

        @block.scalar
        def _(act):
            def split(n, slot):
                act.wait_ge(w_landed[slot], (n - slot) * 8 + 16)
                nc.scalar.activation(w_hi[:, slot], w_raw[:, slot], ACT.Copy).then_inc(w_hi_done, 1)

            def done(n):
                act.wait_ge(tile_done, n + 1)

            def squares(u, k, src):
                if 8 * u + k >= SQ_RING:
                    act.wait_ge(sq_used, 8 * u + k - SQ_RING + 1)
                nc.scalar.activation(sq_buf(u)[:, k % SQ_RING, :], src, ACT.Square).then_inc(sq_ready, 1)

            def root(u):
                act.wait_ge(sq_used, 8 * u + 8)
                nc.scalar.activation(rs[:, :], at_ps[:, 0, :], ACT.Sqrt, bias=eps_c[:, 0:1]).then_inc(root_ready, 1)

            def norm_hi(u, n_free):
                r, part = SHIFT[u]
                idx = {0: 0, 2: 1, 3: 2, 4: 3}[u]
                if n_free:
                    done(n_free - 1)
                for k in range(KB):
                    act.wait_ge(t_ready, 8 * idx + k + 1)
                    c = mod_col(r, part, k)
                    nc.scalar.activation(h_hi[:, k, :], t_buf(u)[:, k % 4, :], ACT.Identity,
                                         bias=mods[:, c:c + 1]).then_inc(h_hi_ready, 1)

            def update_steps(n0, u):
                for j in range(4):
                    done(n0 + j)
                    split(n0 + j + 2, (n0 + j) % 2)
                    for m in range(2):
                        act.wait_ge(x_updated, x_count(u, 2 * j + m))
                        squares(u, 2 * j + m, x_sb[:, 2 * j + m, :])
                root(u)

            for i in range(8):
                act.dma_start(first_chunk[i // 4][:, i % 4], mod_stream[i // 4, i % 4]).then_inc(first_in[i], 16)
            act.wait_ge(cols_in_s, 16)
            for i, name in enumerate(("c", "c_2")):
                nc.scalar.activation(csil[:, 8 * i:8 * i + 8], cols[:, COLS[name]:COLS[name] + 8], ACT.Silu).then_inc(csil_done, 1)
            act.wait_ge(x_in_s, 16)
            act.wait_ge(pads_done, 1)
            for k in range(KB):
                squares(0, k, x_sb[:, k, :])
            for i in range(8):
                act.wait_ge(first_mod, 2 * i + 2)
                act.dma_start(first_chunk[i // 4][:, i % 4], mod_stream[2 + i // 4, i % 4]).then_inc(first_in[i], 16)
            root(0)
            for n in range(2):
                split(n, n)
            norm_hi(0, 0)

            for j in range(4):
                n = N_CONV + 3 * j
                done(n)
                if j:
                    act.wait_ge(y_ready, 2 * j)
                else:
                    act.wait_ge(h_lo_ready, 8)
                nc.scalar.activation(sa[:, 0:2, :], ps[:, n % 2], ACT.Copy).then_inc(a_copied, 1)
                split(n + 2, n % 2)
                done(n + 1)
                nc.scalar.activation(sa[:, 2:4, :], ps[:, (n + 1) % 2], ACT.Sigmoid).then_inc(sig_ready, 1)
                split(n + 3, (n + 1) % 2)
                done(n + 2)
                if j == 0:
                    act.wait_ge(first_mod, 4 * KB)
                nc.scalar.activation(gs_sb[:, 2 * j:2 * j + 2, :], ps[:, n % 2], ACT.Silu).then_inc(gs_ready, 1)
                split(n + 4, n % 2)
            for k in range(KB):
                act.wait_ge(centred, k + 1)
                squares(1, k, y_sb[:, k, :])
            root(1)
            done(N_CONV_OUT - 1)
            for k in range(KB):
                act.wait_ge(ln_z, 2 * k + 1)
                c = COLS["cv_ln_b"] + k
                nc.scalar.activation(sa[:, k % 4, :], sa[:, k % 4, :], ACT.Silu, bias=cols[:, c:c + 1]).then_inc(ln_w, 1)
                act.wait_ge(ln_z, 2 * k + 2)
                nc.scalar.activation(h_hi[:, k, :], y_sb[:, k, :], ACT.Copy).then_inc(h_hi_ready, 1)
            update_steps(N_CONV_OUT, 2)
            norm_hi(2, N_POOL)

            act.wait_ge(pads_done, 2)
            for j in range(4):
                n = N_POOL + j
                done(n)
                if j:
                    act.wait_ge(g_lo_ready, 2 * j)
                nc.scalar.activation(vpad[:, :, POOL_PAD:POOL_PAD + T], ps[:, n % 2], ACT.Copy).then_inc(v_copied, 1)
                split(n + 2, n % 2)
                for m in range(2):
                    act.wait_ge(pooled, 2 * j + m + 1)
                    nc.scalar.activation(g_hi[:, 2 * j + m, :], pool_b[:, m, 0:T], ACT.Copy).then_inc(g_hi_ready, 1)
            for j in range(4):
                n = N_POOL + 4 + j
                done(n)
                nc.scalar.activation(gs_sb[:, 2 * j:2 * j + 2, :], ps[:, n % 2], ACT.Silu).then_inc(gs_ready, 1)
                split(n + 2, n % 2)
            for k in range(KB):
                act.wait_ge(grp_y, k + 1)
                nc.scalar.activation(h_hi[:, k, :], sa[:, k % 4, :], ACT.Copy).then_inc(h_hi_ready, 1)
            done(N_GRP)
            split(N_GRP + 2, N_GRP % 2)
            update_steps(N_POOL_OUT, 3)
            norm_hi(3, N_SB)
            act.wait_ge(h_lo_ready, 8 * 4 + 8)
            act.dma_start(x_spill, x_sb).then_inc(x_spilled, 16)
            act.wait_ge(x_spilled, 16)

            def softplus_log(s, hd):
                act.wait_ge(z_done, hd + 1)
                if isinstance(hd, int) and hd < 2:
                    pass
                else:
                    act.wait_ge(a_split, hd - 1)
                zt = z_tmp[:, s, :]
                nc.scalar.activation(zt, z_ps[s][:, 0:Z_W], ACT.Abs).then_inc(stick_step, 1)
                act.wait_ge(stick_step, hd * 2 + 1)
                nc.scalar.activation(zt, zt, ACT.Exp, scale=-1.0).then_inc(stick_step, 1)
                act.wait_ge(stick_step, hd * 2 + 2)
                nc.scalar.activation(zt, zt, ACT.Ln, bias=1.0).then_inc(stick_ln, 1)

            def weights(s, hd):
                act.wait_ge(after_done, hd + 1)
                nc.scalar.activation(z_tmp[:, s, :], z_ps[s][:, 0:Z_W], ACT.Exp).then_inc(a_exp, 1)

            def output_hi(s, hd, blk):
                act.wait_ge(o_done, hd + 1)
                rows = slice(64 * s, 64 * s + 64)
                nc.scalar.activation(g_hi[rows, blk, :], z_ps[s][rows, 1536:2048], ACT.Copy).then_inc(o_hi_ready, 1)

            def stick_group(grp, n, parity):
                for i, (dst, scale) in enumerate(((sbq_hi, SB_SCALE), (sbk_hi, 1.0), (sbv_hi, 1.0))):
                    slot = (parity + i) % 2
                    done(n + i)
                    src = ps_tok[:, slot] if i == 2 else ps[:, slot]
                    nc.scalar.activation(dst, src, ACT.Copy, scale=scale).then_inc(qkv_hi, 1)
                    split(n + i + 2, slot)
                hd = grp * 4
                softplus_log(0, hd)
                softplus_log(1, hd + 1)
                weights(0, hd)
                weights(1, hd + 1)
                for s in range(2):
                    output_hi(s, hd + s, grp * 2)
                    softplus_log(s, hd + 2 + s)
                for s in range(2):
                    weights(s, hd + 2 + s)
                for s in range(2):
                    output_hi(s, hd + 2 + s, grp * 2 + 1)

            stick_group(0, N_SB, N_SB % 2)
            stick_group(1, N_SB + 3, (N_SB + 3) % 2)
            with act.Fori(1, 2) as i:
                stick_group(2 * i, 6 * i + N_SB, N_SB % 2)
                stick_group(2 * i + 1, 6 * i + N_SB + 3, (N_SB + 3) % 2)

            for j in range(4):
                n = N_SB_OUT + 2 * j
                done(n)
                if j:
                    act.wait_ge(mg_ready, 2 * j)
                for m in range(2):
                    c = COLS["b_branch"] + 2 * j + m
                    nc.scalar.activation(gate_t[:, m, :], ps[:, n % 2, m, :], ACT.Sigmoid, bias=cols[:, c:c + 1]).then_inc(gate_ready, 1)
                split(n + 2, n % 2)
                done(n + 1)
                split(n + 3, (n + 1) % 2)
            act.wait_ge(mg_ready, 8)
            act.wait_ge(mods_ready, 5)
            act.dma_start(rope, rope_in).then_inc(rope_in_s, 16)

            def head(hd, n, parity, g_at):
                if not (isinstance(hd, int) and hd == 0):
                    act.wait_ge(s_decayed, hd * 4)
                act.dma_start(decay[:, :], decay_in[hd]).then_inc(decay_in_s, 16)
                for i, (dst, scale) in enumerate(((rq_hi, 1.0), (rk_hi, RK_SCALE))):
                    slot = (parity + i) % 2
                    done(n + i)
                    for m in range(2):
                        act.wait_ge(rot_step, hd * 4 + 2 * i + m + 1)
                        nc.scalar.activation(dst[:, m, :], rt[:, m, :], ACT.Copy, scale=scale).then_inc(rot_hi, 1)
                    split(n + i + 2, slot)
                for i in range(2):
                    slot = (parity + i) % 2
                    done(n + 2 + i)
                    nc.scalar.activation(rv_hi[:, :, TILE_W * i:TILE_W * (i + 1)], ps_tok[:, slot], ACT.Copy).then_inc(rv_hi_ready, 1)
                    split(n + i + 4, slot)
                    if i == 0:
                        for j in range(TB):
                            w = T - P * j
                            act.wait_ge(s_decayed, hd * 4 + j + 1)
                            nc.scalar.activation(s_hi[:, z_off(j):z_off(j) + w], rt[:, j % 2, 0:w], ACT.Copy).then_inc(s_hi_ready, 1)
                for e in range(4):
                    act.wait_ge(ro_done, hd * 4 + e + 1)
                    if e >= 2:
                        act.wait_ge(ro_stat, hd * 4 + e - 1)
                    nc.scalar.activation(rt[:, e % 2, :], at_ps[:, e, :], ACT.Square).then_inc(ro_sq, 1)
                act.wait_ge(ro_stat, hd * 4 + 4)
                nc.scalar.activation(rs[:, :], ps[:, 1 - parity, 0, :], ACT.Sqrt, scale=2.0, bias=eps_c[:, 0:1]).then_inc(ro_root, 1)
                for i in range(2):
                    slot = (parity + i) % 2
                    done(n + 4 + i)
                    if i:
                        act.wait_ge(ro_w, hd * 4 + 2)
                    nc.scalar.activation(rt[:, 2:4, :], ps[:, slot], ACT.Silu).then_inc(ro_silu, 1)
                    split(n + 6 + i, slot)
                    for m in range(2):
                        e = 2 * i + m
                        act.wait_ge(ro_w, hd * 4 + e + 1)
                        nc.scalar.activation(g_hi[:, g_at + e, :], rt[:, m, :], ACT.Copy).then_inc(o_hi_ready, 1)

            for i in range(2):
                head(i, i * 6 + N_RET1, N_RET1 % 2, i * 4)
            for j in range(4):
                n = N_RETP + j
                done(n)
                nc.scalar.activation(pr[:, 2 * j:2 * j + 2, :], ps[:, n % 2], ACT.Copy).then_inc(pr_ready, 1)
                split(n + 2, n % 2)
            for i in range(2):
                head(i + 2, i * 6 + N_RET2, N_RET2 % 2, i * 4)
            for j in range(4):
                n = N_GATE + j
                done(n)
                if j == 0:
                    act.wait_ge(o_lo_ready, 16 + 16)
                for m in range(2):
                    c = COLS["b_branch"] + 8 + 2 * j + m
                    nc.scalar.activation(gates[:, 2 * j + m, :], ps[:, n % 2, m, :], ACT.Sigmoid, bias=cols[:, c:c + 1]).then_inc(gate_ready, 1)
                split(n + 2, n % 2)
            for j in range(4):
                n = N_MERGE + j
                done(n)
                for m in range(2):
                    act.wait_ge(merge_step, 3 * (2 * j + m) + 3)
                    nc.scalar.activation(h_hi[:, 2 * j + m, :], mg[:, 2 * j + m, :], ACT.Copy).then_inc(h_hi_ready, 1)
                split(n + 2, n % 2)
            act.wait_ge(h_lo_ready, 8 * 5 + 8)
            act.dma_start(x_sb, x_spill).then_inc(x_back, 16)
            update_steps(N_OUT, 4)
            norm_hi(4, N_FFN)

            def ffn_pair(j, n, parity):
                done(n)
                if not (isinstance(j, int) and j == 0):
                    act.wait_ge(ff_prod, j * 2)
                nc.scalar.activation(ft[:, 0:2, :], ps[:, parity], ACT.Silu).then_inc(ff_silu, 1)
                split(n + 2, parity)
                done(n + 1)
                for m in range(2):
                    act.wait_ge(ff_prod, j * 2 + m + 1)
                    nc.scalar.activation(f_hi[:, j * 2 + m, :], ft[:, 2 + m, :], ACT.Copy).then_inc(ff_hi, 1)
                split(n + 3, 1 - parity)

            act.wait_ge(h_lo_ready, 8 * 6 + 8)
            ffn_pair(0, N_FFN, N_FFN % 2)
            with act.Fori(1, 11) as i:
                ffn_pair(i, 2 * i + N_FFN, N_FFN % 2)
            for j in range(4):
                for i in range(3):
                    n = N_FFN_OUT + 3 * j + i
                    done(n)
                    if n + 2 < N_TILES:
                        split(n + 2, n % 2)
                for m in range(2):
                    act.wait_ge(x_updated, x_count(5, 2 * j + m))
                    squares(5, 2 * j + m, x_sb[:, 2 * j + m, :])
            root(5)
            for k in range(KB):
                act.wait_ge(t_ready, 8 * 4 + k + 1)
                act.dma_start(out[:, k, :], x_sb[:, k, :]).then_inc(out_stored, 16)
            act.wait_ge(out_stored, 16 * KB)

        @block.vector
        def _(dve):
            def split(n, slot):
                dve.wait_ge(w_hi_done, n + 1)
                nc.vector.tensor_tensor(w_lo[:, slot], w_raw[:, slot], w_hi[:, slot].bitcast(F32),
                                        ALU.subtract).then_inc(w_lo_done, 1)

            def done(n):
                dve.wait_ge(tile_done, n + 1)

            def low(dst, src, hi, inc, scale=None):
                if scale is None:
                    nc.vector.tensor_tensor(dst, src, hi.bitcast(F32), ALU.subtract).then_inc(inc, 1)
                else:
                    nc.vector.scalar_tensor_tensor(dst, src, scale, hi.bitcast(F32), ALU.mult, ALU.subtract).then_inc(inc, 1)

            def take_mods(r, b0, nb, count):
                dve.wait_ge(mod_summed, count)
                src = COLS["b_mod"] + 24 * r + b0 if r < 2 else COLS["b_ada"] + 24 * (r - 2) + b0
                dst = 24 * r + b0
                nc.vector.tensor_tensor(mods[:, dst:dst + nb], at_ps[:, 3, 0:nb], cols[:, src:src + nb],
                                        ALU.add).then_inc(mods_ready, 1)
                dve.wait_ge(mods_ready, count)

            def gain(u):
                idx = {0: 0, 2: 1, 3: 2, 4: 3}[u]
                r, part = SHIFT[u]
                c, g = mod_col(r, part + 1, 0), COLS[GAIN[u]] + GAIN_AT[u]
                nc.vector.scalar_tensor_tensor(gp[:, :], mods[:, c:c + 8], 1.0, cols[:, g:g + 8], ALU.add,
                                               ALU.mult).then_inc(gp_ready, 1)
                dve.wait_ge(gp_ready, idx + 1)

            def invert(u):
                dve.wait_ge(root_ready, u + 1)
                nc.vector.reciprocal(rs[:, :], rs[:, :]).then_inc(rs_ready, 1)
                dve.wait_ge(rs_ready, u + 1)

            def norm(u):
                idx = {0: 0, 2: 1, 3: 2, 4: 3}[u]
                r, part = SHIFT[u]
                tb = t_buf(u)

                def lows(k):
                    dve.wait_ge(h_hi_ready, 8 * FILL[u] + k + 1)
                    c = mod_col(r, part, k)
                    nc.vector.scalar_tensor_tensor(h_lo[:, k, :], tb[:, k % 4, :], mods[:, c:c + 1],
                                                   h_hi[:, k, :].bitcast(F32), ALU.add, ALU.subtract).then_inc(h_lo_ready, 1)

                for k in range(KB):
                    if k >= 4:
                        dve.wait_ge(h_lo_ready, 8 * FILL[u] + k - 3)
                    nc.vector.scalar_tensor_tensor(tb[:, k % 4, :], x_sb[:, k, :], gp[:, k:k + 1], rs[:, :], ALU.mult,
                                                   ALU.mult).then_inc(t_ready, 1)
                    if k:
                        lows(k - 1)
                lows(KB - 1)

            def update_steps(n0, u, gate, x0):
                r, part = GATE[gate]
                for j in range(4):
                    n = n0 + j
                    done(n)
                    for m in range(2):
                        k = 2 * j + m
                        c = mod_col(r, part, k)
                        nc.vector.scalar_tensor_tensor(x_sb[:, k, :], ps[:, n % 2, m, :], mods[:, c:c + 1], x_sb[:, k, :],
                                                       ALU.mult, ALU.add).then_inc(x_updated, 1)
                    split(n + 2, n % 2)

            nc.vector.memset(eps_c[:, :], EPS)
            nc.vector.memset(ypad[:, :, :], 0.0).then_inc(pads_done, 1)
            dve.wait_ge(const_in_s, 16)
            nc.vector.tensor_copy(pool_edge[:, :], c_stage[:, C_POOL:C_POOL + 64])
            for dst, c in ((eye_r, C_EYE), (neg_r, C_NEG), (ntri_r, C_NTRI), (none_r, C_NONE)):
                nc.vector.tensor_copy(dst[:, :], c_stage[:, c:c + P])
            nc.vector.tensor_copy(mean_m[:, :], c_stage[:, C_MEAN:C_MEAN + P]).then_inc(consts_done, 1)
            dve.wait_ge(csil_done, 2)
            for g in range(DVE_GROUPS):
                acc = mod_acc[:, MOD_G * g:MOD_G * (g + 1)]
                for kb in range(KB):
                    i = 4 * g + kb // 2
                    if kb % 2 == 0:
                        dve.wait_ge(first_in[i % 8], 16 * (i // 8) + 16)
                    src = first_chunk[(i % 8) // 4][:, i % 4, kb % 2]
                    c = csil[:, kb:kb + 1]
                    if kb == 0:
                        nc.vector.tensor_scalar(acc, src, c, None, ALU.mult).then_inc(first_mod, 1)
                    else:
                        dve.wait_ge(first_mod, 8 * g + kb)
                        nc.vector.scalar_tensor_tensor(acc, src, c, acc, ALU.mult, ALU.add).then_inc(first_mod, 1)
            for n in range(2):
                split(n, n)
            take_mods(0, 0, 16, 1)
            gain(0)
            invert(0)
            norm(0)

            def convolve(k):
                w, db = COLS["dw"] + CONV_W * k, COLS["cv_db"] + k
                src = ypad[:, k % 2, :]
                nc.vector.tensor_scalar(y_sb[:, k, :], src[:, 0:T], cols[:, w:w + 1], cols[:, db:db + 1], ALU.mult,
                                        ALU.add).then_inc(conv_step, 1)
                for t in range(1, CONV_W):
                    dve.wait_ge(conv_step, CONV_W * k + t)
                    nc.vector.scalar_tensor_tensor(y_sb[:, k, :], src[:, t:t + T], cols[:, w + t:w + t + 1], y_sb[:, k, :],
                                                   ALU.mult, ALU.add).then_inc(conv_step, 1)

            for j in range(4):
                n = N_CONV + 3 * j
                done(n)
                split(n + 2, n % 2)
                done(n + 1)
                dve.wait_ge(a_copied, j + 1)
                dve.wait_ge(sig_ready, j + 1)
                if j:
                    dve.wait_ge(conv_step, CONV_W * 2 * j)
                for m in range(2):
                    nc.vector.tensor_tensor(ypad[:, m, PAD:PAD + T], sa[:, m, :], sa[:, 2 + m, :], ALU.mult).then_inc(y_ready, 1)
                split(n + 3, (n + 1) % 2)
                dve.wait_ge(y_ready, 2 * j + 2)
                convolve(2 * j)
                done(n + 2)
                split(n + 4, n % 2)
                convolve(2 * j + 1)
                if j == 1:
                    take_mods(0, 16, 8, 2)
            dve.wait_ge(conv_summed, KB)
            for k in range(KB):
                nc.vector.tensor_tensor(y_sb[:, k, :], y_sb[:, k, :], at_ps[:, 1, :], ALU.subtract).then_inc(centred, 1)
            take_mods(1, 0, 24, 3)
            invert(1)

            def gate_conv(k):
                dve.wait_ge(ln_w, k + 1)
                nc.vector.tensor_tensor(y_sb[:, k, :], sa[:, k % 4, :], gs_sb[:, k, :], ALU.mult).then_inc(ln_z, 1)

            for k in range(KB):
                c = COLS["cv_ln_g"] + k
                nc.vector.scalar_tensor_tensor(sa[:, k % 4, :], y_sb[:, k, :], cols[:, c:c + 1], rs[:, :], ALU.mult,
                                               ALU.mult).then_inc(ln_z, 1)
                gate_conv(k)
                dve.wait_ge(h_hi_ready, 8 + k + 1)
                low(h_lo[:, k, :], y_sb[:, k, :], h_hi[:, k, :], h_lo_ready)
            update_steps(N_CONV_OUT, 2, "conv", 0)
            gain(2)
            invert(2)
            norm(2)

            nc.vector.memset(vpad[:, :, 0:POOL_PAD], 0.0)
            nc.vector.memset(vpad[:, :, POOL_PAD + T:PW], 0.0).then_inc(pads_done, 1)
            steps = 0
            for j in range(4):
                n = N_POOL + j
                win = 2 << j
                done(n)
                dve.wait_ge(v_copied, j + 1)
                src, ln = vpad, PW
                for lvl in range(j + 1):
                    d = 1 << lvl
                    dst = pool_a if (j - lvl) % 2 == 0 else pool_b
                    ln -= d
                    nc.vector.tensor_tensor(dst[:, :, 0:ln], src[:, :, 0:ln], src[:, :, d:d + ln], ALU.add).then_inc(pool_step, 1)
                    steps += 1
                    dve.wait_ge(pool_step, steps)
                    src = dst
                assert src is pool_a
                o = POOL_PAD - win // 2
                tok = vpad[:, :, POOL_PAD:POOL_PAD + T]
                nc.vector.scalar_tensor_tensor(pool_b[:, :, 0:T], pool_a[:, :, o:o + T], 1.0 / win, tok, ALU.mult,
                                               ALU.subtract).then_inc(pool_step, 1)
                dve.wait_ge(pool_step, steps + 1)
                for m in range(2):
                    for side, e in ((0, 0), (T - 8, 8)):
                        nc.vector.tensor_tensor(pool_a[:, m, o + side:o + side + 8], pool_a[:, m, o + side:o + side + 8],
                                                pool_edge[:, 16 * j + e:16 * j + e + 8], ALU.mult).then_inc(pool_step, 1)
                steps += 5
                dve.wait_ge(pool_step, steps)
                for m in range(2):
                    nc.vector.tensor_tensor(pool_b[:, m, 0:8], pool_a[:, m, o:o + 8], tok[:, m, 0:8],
                                            ALU.subtract).then_inc(pool_step, 1)
                    nc.vector.tensor_tensor(pool_b[:, m, T - 8:T], pool_a[:, m, o + T - 8:o + T], tok[:, m, T - 8:T],
                                            ALU.subtract).then_inc(pooled, 1)
                steps += 2
                split(n + 2, n % 2)
                for m in range(2):
                    dve.wait_ge(g_hi_ready, 2 * j + m + 1)
                    low(g_lo[:, 2 * j + m, :], pool_b[:, m, 0:T], g_hi[:, 2 * j + m, :], g_lo_ready)
            for j in range(4):
                n = N_POOL + 4 + j
                done(n)
                if n + 2 < N_GRP + 2:
                    split(n + 2, n % 2)
            dve.wait_ge(gs_ready, 8)

            def group_y(k):
                if k == 7:
                    done(N_GRP)
                else:
                    dve.wait_ge(grp_done, k + 1)
                if k >= 4:
                    dve.wait_ge(h_lo_ready, 24 + k - 3)
                src = (ps[:, 1, k % 2, :], at_ps[:, k % 2, :], at_ps[:, 2 + k % 2, :], ps[:, 0, k % 2, :])[k // 2]
                c = COLS["pl_scale"] + k
                nc.vector.scalar_tensor_tensor(sa[:, k % 4, :], src, cols[:, c:c + 1], gs_sb[:, k, :], ALU.mult,
                                               ALU.mult).then_inc(grp_y, 1)

            def group_low(k):
                dve.wait_ge(h_hi_ready, 24 + k + 1)
                low(h_lo[:, k, :], sa[:, k % 4, :], h_hi[:, k, :], h_lo_ready)

            done(N_GRP - 1)
            for k in range(KB):
                group_y(k)
                if k:
                    group_low(k - 1)
            group_low(KB - 1)
            split(N_GRP + 2, N_GRP % 2)
            update_steps(N_POOL_OUT, 3, "pool", 8)
            take_mods(2, 0, 24, 4)
            gain(3)
            invert(3)
            norm(3)

            def softplus_split(s, hd):
                dve.wait_ge(stick_ln, hd + 1)
                zt = z_tmp[:, s, :]
                nc.vector.scalar_tensor_tensor(zt, z_ps[s][:, 0:Z_W], 0.0, zt, ALU.max, ALU.add).then_inc(sp_step, 1)
                dve.wait_ge(sp_step, hd * 2 + 1)
                nc.vector.tensor_copy(att_hi[:, s, :], zt).then_inc(sp_step, 1)
                dve.wait_ge(sp_step, hd * 2 + 2)
                low(att_lo[:, s, :], zt, att_hi[:, s, :], sp_split)

            def weights_split(s, hd):
                dve.wait_ge(a_exp, hd + 1)
                zt = z_tmp[:, s, :]
                nc.vector.tensor_copy(att_hi[:, s, :], zt).then_inc(a_step, 1)
                dve.wait_ge(a_step, hd + 1)
                low(att_lo[:, s, :], zt, att_hi[:, s, :], a_split)

            def output_low(s, hd, blk):
                dve.wait_ge(o_hi_ready, hd + 1)
                rows = slice(64 * s, 64 * s + 64)
                low(g_lo[rows, blk, :], z_ps[s][rows, 1536:2048], g_hi[rows, blk, :], o_lo_ready)

            def stick_group(grp, n, parity):
                for i, (dst, hi, scale) in enumerate(((sbq_lo, sbq_hi, SB_SCALE), (sbk_lo, sbk_hi, None), (sbv_lo, sbv_hi, None))):
                    slot = (parity + i) % 2
                    dve.wait_ge(qkv_hi, grp * 3 + i + 1)
                    low(dst, ps_tok[:, slot] if i == 2 else ps[:, slot], hi, qkv_lo, scale)
                    split(n + i + 2, slot)
                hd = grp * 4
                softplus_split(0, hd)
                softplus_split(1, hd + 1)
                weights_split(0, hd)
                weights_split(1, hd + 1)
                for s in range(2):
                    output_low(s, hd + s, grp * 2)
                    softplus_split(s, hd + 2 + s)
                for s in range(2):
                    weights_split(s, hd + 2 + s)
                for s in range(2):
                    output_low(s, hd + 2 + s, grp * 2 + 1)

            stick_group(0, N_SB, N_SB % 2)
            stick_group(1, N_SB + 3, (N_SB + 3) % 2)
            with dve.Fori(1, 2) as i:
                stick_group(2 * i, 6 * i + N_SB, N_SB % 2)
                stick_group(2 * i + 1, 6 * i + N_SB + 3, (N_SB + 3) % 2)

            for j in range(4):
                n = N_SB_OUT + 2 * j
                done(n)
                split(n + 2, n % 2)
                done(n + 1)
                for m in range(2):
                    dve.wait_ge(gate_ready, 2 * j + m + 1)
                    nc.vector.tensor_tensor(mg[:, 2 * j + m, :], ps[:, (n + 1) % 2, m, :], gate_t[:, m, :],
                                            ALU.mult).then_inc(mg_ready, 1)
                split(n + 3, (n + 1) % 2)
            take_mods(3, 0, 24, 5)

            dve.wait_ge(rope_in_s, 16)
            cos, sin = rope[:, 0, :], rope[:, 1, :]

            def rotate(i, slot, hd):
                a, b = ps[:, slot, 0, :], ps[:, slot, 1, :]
                for half, (p, q, op) in enumerate(((cos, sin, ALU.subtract), (sin, cos, ALU.add))):
                    nc.vector.tensor_tensor(rt[:, half, :], a, p, ALU.mult).then_inc(ro_norm, 1)
                    nc.vector.tensor_tensor(rt[:, 2 + half, :], b, q, ALU.mult).then_inc(ro_norm, 1)
                    dve.wait_ge(ro_norm, hd * 12 + 4 * i + 2 * half + 2)
                    nc.vector.tensor_tensor(rt[:, half, :], rt[:, half, :], rt[:, 2 + half, :], op).then_inc(rot_step, 1)

            def head(hd, n, parity, g_at):
                for i, (dst, hi, scale) in enumerate(((rq_lo, rq_hi, None), (rk_lo, rk_hi, RK_SCALE))):
                    slot = (parity + i) % 2
                    done(n + i)
                    rotate(i, slot, hd)
                    for m in range(2):
                        dve.wait_ge(rot_hi, hd * 4 + 2 * i + m + 1)
                        low(dst[:, m, :], rt[:, m, :], hi[:, m, :], rot_lo, scale)
                    dve.wait_ge(rot_lo, hd * 4 + 2 * i + 2)
                    split(n + i + 2, slot)
                dve.wait_ge(decay_in_s, hd * 16 + 16)
                for i in range(2):
                    slot = (parity + i) % 2
                    done(n + 2 + i)
                    dve.wait_ge(rv_hi_ready, hd * 2 + i + 1)
                    low(rv_lo[:, :, TILE_W * i:TILE_W * (i + 1)], ps_tok[:, slot], rv_hi[:, :, TILE_W * i:TILE_W * (i + 1)], rv_lo_ready)
                    split(n + i + 4, slot)
                    if i == 0:
                        def s_low(j):
                            w = T - P * j
                            dve.wait_ge(s_hi_ready, hd * 4 + j + 1)
                            low(s_lo[:, z_off(j):z_off(j) + w], rt[:, j % 2, 0:w], s_hi[:, z_off(j):z_off(j) + w], s_lo_ready)

                        for j in range(TB):
                            w = T - P * j
                            dve.wait_ge(s_done, hd * 4 + j + 1)
                            if j >= 2:
                                dve.wait_ge(s_lo_ready, hd * 4 + j - 1)
                            nc.vector.tensor_tensor(rt[:, j % 2, 0:w], at_ps[:, j, 0:w], decay[:, 0:w], ALU.mult).then_inc(s_decayed, 1)
                            if j:
                                s_low(j - 1)
                        s_low(TB - 1)
                dve.wait_ge(ro_root, hd + 1)
                nc.vector.reciprocal(rs[:, :], rs[:, :]).then_inc(ro_rs, 1)
                dve.wait_ge(ro_rs, hd + 1)
                for i in range(2):
                    slot = (parity + i) % 2
                    done(n + 4 + i)
                    dve.wait_ge(ro_silu, hd * 2 + i + 1)
                    for m in range(2):
                        e = 2 * i + m
                        if i:
                            dve.wait_ge(o_lo_ready, hd * 4 + 16 + m + 1)
                        nc.vector.tensor_tensor(rt[:, m, :], at_ps[:, e, :], rs[:, :], ALU.mult).then_inc(ro_norm, 1)
                        dve.wait_ge(ro_norm, hd * 12 + 8 + e + 1)
                        nc.vector.tensor_tensor(rt[:, m, :], rt[:, m, :], rt[:, 2 + m, :], ALU.mult).then_inc(ro_w, 1)
                    for m in range(2):
                        e = 2 * i + m
                        dve.wait_ge(o_hi_ready, hd * 4 + 16 + e + 1)
                        low(g_lo[:, g_at + e, :], rt[:, m, :], g_hi[:, g_at + e, :], o_lo_ready)
                    split(n + 6 + i, slot)
                dve.wait_ge(o_lo_ready, hd * 4 + 20)

            for i in range(2):
                head(i, i * 6 + N_RET1, N_RET1 % 2, i * 4)
            for j in range(4):
                n = N_RETP + j
                done(n)
                split(n + 2, n % 2)
            for i in range(2):
                head(i + 2, i * 6 + N_RET2, N_RET2 % 2, i * 4)
            for j in range(4):
                n = N_GATE + j
                done(n)
                split(n + 2, n % 2)
            dve.wait_ge(gate_ready, 16)
            for j in range(4):
                n = N_MERGE + j
                done(n)
                for m in range(2):
                    k = 2 * j + m
                    nc.vector.tensor_tensor(pr[:, k, :], ps[:, n % 2, m, :], pr[:, k, :], ALU.add).then_inc(merge_step, 1)
                    dve.wait_ge(merge_step, 3 * k + 1)
                    nc.vector.tensor_tensor(pr[:, k, :], pr[:, k, :], gates[:, k, :], ALU.mult).then_inc(merge_step, 1)
                    dve.wait_ge(merge_step, 3 * k + 2)
                    nc.vector.tensor_tensor(mg[:, k, :], pr[:, k, :], mg[:, k, :], ALU.add).then_inc(merge_step, 1)
                    dve.wait_ge(h_hi_ready, 8 * 5 + k + 1)
                    low(h_lo[:, k, :], mg[:, k, :], h_hi[:, k, :], h_lo_ready)
                split(n + 2, n % 2)
            dve.wait_ge(x_back, 16)
            update_steps(N_OUT, 4, "out", 16)
            gain(4)
            invert(4)
            norm(4)

            def ffn_pair(j, n, parity):
                done(n)
                split(n + 2, parity)
                done(n + 1)
                dve.wait_ge(ff_silu, j + 1)
                for m in range(2):
                    nc.vector.tensor_tensor(ft[:, 2 + m, :], ps[:, 1 - parity, m, :], ft[:, m, :], ALU.mult).then_inc(ff_prod, 1)
                for m in range(2):
                    dve.wait_ge(ff_hi, j * 2 + m + 1)
                    low(f_lo[:, j * 2 + m, :], ft[:, 2 + m, :], f_hi[:, j * 2 + m, :], ff_lo)
                split(n + 3, 1 - parity)
                dve.wait_ge(ff_lo, j * 2 + 2)

            ffn_pair(0, N_FFN, N_FFN % 2)
            with dve.Fori(1, 11) as i:
                ffn_pair(i, 2 * i + N_FFN, N_FFN % 2)
            r, part = GATE["ffn"]
            for j in range(4):
                for i in range(3):
                    n = N_FFN_OUT + 3 * j + i
                    done(n)
                    if i == 2:
                        for m in range(2):
                            k = 2 * j + m
                            c = mod_col(r, part, k)
                            nc.vector.scalar_tensor_tensor(x_sb[:, k, :], ps[:, j % 2, m, :], mods[:, c:c + 1], x_sb[:, k, :],
                                                           ALU.mult, ALU.add).then_inc(x_updated, 1)
                    if n + 2 < N_TILES:
                        split(n + 2, n % 2)
            invert(5)
            for k in range(KB):
                c = COLS["g_final"] + k
                nc.vector.scalar_tensor_tensor(x_sb[:, k, :], x_sb[:, k, :], cols[:, c:c + 1], rs[:, :], ALU.mult,
                                               ALU.mult).then_inc(t_ready, 1)


def _columns(v):
    return np.asarray(v).reshape(-1, P).T


def _weight_tiles(w):
    w = np.asarray(w)
    if w.shape[0] < D:
        w = np.concatenate([w, np.zeros((D - w.shape[0], w.shape[1]), w.dtype)])
    return list(w.reshape(KB, P, -1, TILE_W).transpose(2, 1, 0, 3))


def _shape_constants():
    f = np.float32
    const = np.zeros((P, N_CONST), f)
    const[:, C_MEAN:C_MEAN + P] = 1.0 / D
    const[:, C_EYE:C_EYE + P] = np.eye(P)
    s, t = np.arange(P)[:, None], np.arange(P)[None, :]
    const[:, C_NEG:C_NEG + P] = np.where(s >= t, f(NEG_BIG), f(0))
    const[:, C_NTRI:C_NTRI + P] = np.where(s >= t, f(-1), f(0))
    const[:, C_NONE:C_NONE + P] = -1
    tok = np.arange(T)
    for j in range(4):
        win = 2 << j
        cnt = (np.clip(tok + win - win // 2, 0, T) - np.clip(tok - win // 2, 0, T)).astype(f)
        const[:, C_POOL + 16 * j:C_POOL + 16 * j + 16] = (1 / cnt)[np.r_[0:8, T - 8:T]]
    ang_freq = f(10000.0) ** (-np.arange(0, 256, 2, dtype=f) / f(256))
    ang = ang_freq[:, None] * tok.astype(f)[None, :]
    rope = np.stack([np.cos(ang), np.sin(ang)], axis=1).astype(f)
    log_gamma = np.log(f(1) - f(2) ** (f(-5) - np.arange(RET_HEADS, dtype=f)))
    diff = (tok[None, :] - np.arange(P)[:, None]).astype(f)
    decay = np.where(diff >= 0, np.exp(np.maximum(diff, 0)[None] * log_gamma[:, None, None]), 0).astype(f)
    return const, rope, decay


def kernel(**inputs):
    import concourse.bacc as bacc
    from concourse.bass_utils import run_bass_kernel_spmd

    a = {k: np.asarray(v) for k, v in inputs.items()}

    def pick(groups, order):
        return [groups[g][j] for g, j in order]

    conv = _weight_tiles(a["cv_w_in"][0])
    w_in = a["w_in_2"][0]
    cuts = np.cumsum([0, 1024, 1024, 1024, 1024, 1024, 2048, 2048, 1024, 1024])
    parts = [_weight_tiles(w_in[:, p:q]) for p, q in zip(cuts[:-1], cuts[1:])]
    sq, sk, sv, rq, rk, rv, rg, b_sb, b_ret = parts
    proj_sb = _weight_tiles(a["w_proj_sb_2"][0])
    proj_ret = [_weight_tiles(a["w_proj_ret_2"][0][D * i:D * (i + 1)]) for i in range(2)]
    ffn = _weight_tiles(a["w_ffn_in_2"][0])
    ffn_out = [_weight_tiles(a["w_ffn_out_2"][0][D * i:D * (i + 1)]) for i in range(3)]
    tiles = []
    for j in range(4):
        tiles += [conv[j], conv[4 + j], conv[8 + j]]
    tiles += _weight_tiles(a["cv_w_out"][0])
    tiles += _weight_tiles(a["pl_w_in"][0])
    tiles += _weight_tiles(a["pl_w_grp"][0].reshape(D, TILE_W))
    tiles += _weight_tiles(a["pl_w_out"][0])
    for j in range(4):
        tiles += [sq[j], sk[j], sv[j]]
    for j in range(4):
        tiles += [b_sb[j], proj_sb[j]]
    for h in range(RET_HEADS):
        tiles += [rq[h], rk[h], rv[2 * h], rv[2 * h + 1], rg[2 * h], rg[2 * h + 1]]
        if h == 1:
            tiles += proj_ret[0]
    tiles += b_ret + proj_ret[1]
    tiles += _weight_tiles(a["w_out_2"][0])
    for j in range(11):
        tiles += [ffn[j], ffn[11 + j]]
    for j in range(4):
        tiles += [ffn_out[i][j] for i in range(3)]
    assert len(tiles) == N_TILES
    w_stream = np.stack(tiles)

    mod = np.concatenate([a["w_mod"][0], a["w_mod"][1], a["w_ada_2"][0]], axis=1)
    mod_stream = np.ascontiguousarray(mod.reshape(4, 2, P, N_MOD_GROUPS, MOD_G).transpose(3, 0, 2, 1, 4))
    vectors = {
        "norm_g": a["norm_g"], "b_mod": a["b_mod"], "b_ada": a["b_ada_2"], "cv_db": a["cv_db"], "cv_ln_g": a["cv_ln_g"],
        "cv_ln_b": a["cv_ln_b"], "pl_scale": a["pl_scale"], "g_norm1": a["g_norm1_2"], "g_norm2": a["g_norm2_2"],
        "g_final": a["g_final_2"], "b_branch": a["b_branch_2"], "c": a["c"], "c_2": a["c_2"],
        "dw": a["cv_dw"][0].reshape(CONV_W, KB, P).transpose(1, 0, 2),
    }
    cols = np.ascontiguousarray(np.concatenate([_columns(vectors[n]) for n in COLS], axis=1))
    assert cols.shape == (P, N_COLS)
    x_t = np.ascontiguousarray(a["x"][0].T.reshape(KB, P, T).transpose(1, 0, 2))
    const, rope, decay = _shape_constants()

    arrays = {"w_stream": w_stream, "mod_stream": mod_stream, "x_t": x_t, "cols_in": cols, "const_in": const,
              "rope_in": rope, "decay_in": decay}
    nc = bacc.Bacc("TRN2", target_bir_lowering=False, num_devices=1)
    aps = {k: nc.dram_tensor(k, v.shape, F32, kind="ExternalInput").ap() for k, v in arrays.items()}
    x_spill = nc.dram_tensor("x_spill", (P, KB, T), F32).ap()
    out = nc.dram_tensor("out_t", (P, KB, T), F32, kind="ExternalOutput").ap()
    build_program(nc, aps["w_stream"], aps["mod_stream"], aps["x_t"], aps["cols_in"], aps["const_in"],
                  aps["rope_in"], aps["decay_in"], x_spill, out)
    got = run_bass_kernel_spmd(nc, [arrays], core_ids=[0]).results[0]["out_t"]
    return np.ascontiguousarray(got.transpose(1, 0, 2).reshape(D, T).T)[None]
```

```python
from contextlib import ExitStack

import numpy as np

import concourse.bass as bass
from concourse import mybir

P = 128
D = 1024
T = 512
KB = D // P
TB = T // P
TILE_W = 256
CONV_W = 31
PAD = CONV_W // 2
POOL_PAD = 8
D_FF = 2816
FFB = D_FF // P
EPS = 1e-6
NEG_BIG = -1e30
SB_SCALE = 64 ** -0.5
RK_SCALE = 256 ** -0.5
RET_HEADS = 4

F32 = mybir.dt.float32
F32R = mybir.dt.float32r
ALU = mybir.AluOpType
ACT = mybir.ActivationFunctionType

N_CONV = 0
N_CONV_OUT = N_CONV + 12
N_POOL = N_CONV_OUT + 4
N_GRP = N_POOL + 8
N_POOL_OUT = N_GRP + 1
N_SB = N_POOL_OUT + 4
N_SB_GATE = N_SB + 12
N_SB_OUT = N_SB_GATE + 4
N_RET1 = N_SB_OUT + 4
N_RETP = N_RET1 + 12
N_RET2 = N_RETP + 4
N_GATE = N_RET2 + 12
N_MERGE = N_GATE + 4
N_OUT = N_MERGE + 4
N_FFN = N_OUT + 4
N_FFN_OUT = N_FFN + 22
N_TILES = N_FFN_OUT + 12

MOD_G = 512
MOD_ROUND = 3 * D
ROUND_GROUPS = MOD_ROUND // MOD_G
N_MOD_GROUPS = 4 * ROUND_GROUPS
DVE_GROUPS = 4

COLS = {}
_at = 0
for _name, _n in (("norm_g", 16), ("b_mod", 48), ("b_ada", 48), ("cv_db", 8), ("cv_ln_g", 8),
                  ("cv_ln_b", 8), ("pl_scale", 8), ("g_norm1", 8), ("g_norm2", 8), ("g_final", 8),
                  ("b_branch", 16), ("c", 8), ("c_2", 8), ("dw", 8 * CONV_W)):
    COLS[_name] = _at
    _at += _n
N_COLS = _at

C_MEAN, C_EYE, C_NEG, C_NTRI, C_NONE, C_POOL = (P * i for i in range(6))
N_CONST = C_POOL + 4 * 16


def z_off(j):
    return {0: 0, 1: 512, 3: 896, 2: 1024}[j]


Z_W = 1280


def build_program(nc, w_stream, mod_stream, x_in, cols_in, const_in, rope_in, decay_in, x_spill, out):
    with ExitStack() as ctx:
        base = 16512

        def place(name, at, n, dt):
            assert at + 4 * n <= 229344 - base, (name, at + 4 * n)
            return nc.alloc_sbuf_tensor_at(name, [P, n], dt, offset=base + at)

        def blocks(t, w):
            return t[:, :].rearrange("p (b w) -> p b w", w=w)

        def sem(name):
            return ctx.enter_context(nc.semaphore(name))

        K = 1024
        w_raw = place("w_raw", 0, 4096, F32)[:, :].rearrange("p (s k c) -> p s k c", s=2, k=KB)
        w_hi = place("w_hi", 16 * K, 4096, F32R)[:, :].rearrange("p (s k c) -> p s k c", s=2, k=KB)
        w_lo = place("w_lo", 32 * K, 4096, F32R)[:, :].rearrange("p (s k c) -> p s k c", s=2, k=KB)
        h_hi = blocks(place("h_hi", 48 * K, 4096, F32R), T)
        h_lo = blocks(place("h_lo", 64 * K, 4096, F32R), T)
        x_flat = place("x_sb", 80 * K, 4096, F32)
        x_sb = blocks(x_flat, T)
        rs = place("rs", 96 * K, 512, F32)
        cols = place("cols", 98 * K, N_COLS, F32)
        at = (98 * K + 4 * N_COLS + 31) // 32 * 32
        mods = place("mods", at, 96, F32)
        gp = place("gp", at + 4 * 96, 8, F32)
        csil = place("csil", at + 4 * 104, 16, F32)
        at = at + 4 * 120
        mean_m = place("mean_m", at, P, F32)
        pool_edge = place("pool_edge", at + 512, 64, F32)
        eye_r = place("eye_r", at + 768, P, F32R)
        neg_r = place("neg_r", at + 1280, P, F32R)
        ntri_r = place("ntri_r", at + 1792, P, F32R)
        none_r = place("none_r", at + 2304, P, F32R)
        ones_c = place("ones_c", at + 2816, 2, F32)
        eps_c = place("eps_c", at + 2848, 1, F32)
        var = at + 2880

        g_hi = blocks(place("g_hi", var, 4096, F32R), T)
        g_lo = blocks(place("g_lo", var + 16 * K, 4096, F32R), T)
        v = var + 32 * K
        mod_acc = place("mod_acc", v, MOD_ROUND, F32)
        mod_chunk = place("mod_chunk", v + 12 * K, 2048, F32)[:, :].rearrange("p (s k c) -> p s k c", s=2, k=2)
        v1 = v + 20 * K
        y_flat = place("y_sb", v1, 4096, F32)
        y_sb = blocks(y_flat, T)
        gs_flat = place("gs_sb", v1 + 16 * K, 4096, F32)
        gs_sb = blocks(gs_flat, T)
        first_chunk = [t[:, :].rearrange("p (s k c) -> p s k c", s=4, k=2) for t in (y_flat, gs_flat)]
        sa = blocks(place("sa", v1 + 32 * K, 2048, F32), T)
        sq = blocks(place("sq", v1 + 40 * K, 1024, F32), T)
        ypad = place("ypad", var, 2 * (T + 2 * PAD), F32)[:, :].rearrange("p (m t) -> p m t", m=2)
        c_stage = place("c_stage", var + 8 * K, N_CONST, F32)
        PW = T + 2 * POOL_PAD
        vpad = place("vpad", v1, 2 * PW, F32)[:, :].rearrange("p (m t) -> p m t", m=2)
        pool_a = place("pool_a", v1 + 8 * PW, 2 * PW, F32)[:, :].rearrange("p (m t) -> p m t", m=2)
        pool_b = place("pool_b", v1 + 16 * PW, 2 * PW, F32)[:, :].rearrange("p (m t) -> p m t", m=2)

        names = ("q_hi", "q_lo", "k_hi", "k_lo", "v_hi", "v_lo")
        qkv_at = ([v1 + 4 * K * i for i in range(6)], [v + 4 * K * i for i in range(5)] + [v1 + 44 * K])
        sbq_hi, sbq_lo, sbk_hi, sbk_lo, sbv_hi, sbv_lo = (
            [blocks(place(f"sb{name}_{s}", qkv_at[s][i], 1024, F32R), TILE_W if i >= 4 else T) for s in range(2)]
            for i, name in enumerate(names))
        att_hi = blocks(place("att_hi", v1 + 24 * K, 2 * Z_W, F32R), Z_W)
        att_lo = blocks(place("att_lo", v1 + 34 * K, 2 * Z_W, F32R), Z_W)
        z_tmp = x_flat[:, 0:2 * Z_W].rearrange("p (s z) -> p s z", s=2)
        mg = x_sb
        sb_gates = blocks(place("sb_gates", v1, 4096, F32), T)
        pr = blocks(place("pr", v, 4096, F32), T)
        rq_hi, rq_lo, rk_hi, rk_lo = (
            blocks(place(f"r{n}", v + (16 + 4 * i) * K, 1024, F32R), T) for i, n in enumerate(names[:4]))
        rv_hi, rv_lo = (blocks(place(f"r{n}", v + (32 + 8 * i) * K, 2048, F32R), T) for i, n in enumerate(names[4:]))
        s_hi, s_lo = (place(f"s_{n}", v + 48 * K + 5 * K * i, Z_W, F32R) for i, n in enumerate(("hi", "lo")))
        rope = blocks(place("rope", v + 58 * K, 1024, F32), T)
        decay = place("decay", v + 62 * K, T, F32)
        rt = blocks(place("rt", v + 64 * K, 2048, F32), T)
        gates = blocks(place("gates", v + 16 * K, 4096, F32), T)
        nt = blocks(place("nt", v + 48 * K, 2048, F32), T)
        nsq = blocks(place("nsq", v + 56 * K, 1024, F32), T)
        f_hi = blocks(place("f_hi", var, FFB * T, F32R), T)
        f_lo = blocks(place("f_lo", var + 2 * K * FFB, FFB * T, F32R), T)
        ft = blocks(place("ft", var + 4 * K * FFB, 2048, F32), T)
        fsq = blocks(place("fsq", var + 4 * K * FFB + 8 * K, 1024, F32), T)

        ps = ctx.enter_context(nc.psum_tensor("ps", [P, 2, 2, T], F32))
        at_ps = ctx.enter_context(nc.psum_tensor("at_ps", [P, 4, T], F32))
        ps_tok = ps[:, :, :, :].rearrange("p s m (h c) -> p s (m h) c", c=TILE_W)
        ps_flat = ps[:, :, :, :].rearrange("p s m t -> p (s m t)")
        at_flat = at_ps[:, :, :].rearrange("p b t -> p (b t)")
        z_ps = (at_flat[:, 0:3 * T], ps_flat[:, T:4 * T])
        o_ps = at_flat[:, 3 * T:4 * T]

        cols_in_s, x_in_s, const_in_s = sem("cols_loaded"), sem("x_loaded"), sem("consts_loaded")
        w_landed = [sem("w_landed_even"), sem("w_landed_odd")]
        first_in = [sem(f"first_chunk_loaded_{i}") for i in range(8)]
        chunk_in = [sem("mod_chunk_loaded_even"), sem("mod_chunk_loaded_odd")]
        w_hi_done, w_lo_done = sem("w_hi_done"), sem("w_lo_done")
        tile_done = sem("tile_done")
        ones_done = sem("ones_done")
        csil_done, consts_done, pads_done = sem("csil_done"), sem("consts_done"), sem("pads_done")
        first_mod = sem("first_mod")
        mod_step = sem("mod_step")
        mod_summed, mods_ready, gp_ready = sem("mod_summed"), sem("mods_ready"), sem("gp_ready")
        x_updated = sem("x_updated")
        sq_ready, sq_used, root_ready, rs_ready = sem("sq_ready"), sem("sq_used"), sem("root_ready"), sem("rs_ready")
        t_ready, h_hi_ready, h_lo_ready = sem("t_ready"), sem("h_hi_ready"), sem("h_lo_ready")
        a_copied, sig_ready, y_ready, conv_step = sem("a_copied"), sem("sig_ready"), sem("y_ready"), sem("conv_step")
        conv_summed, centred = sem("conv_summed"), sem("centred")
        ln_t, ln_silu, ln_y = sem("ln_t"), sem("ln_silu"), sem("ln_y")
        gs_ready = sem("gs_ready")
        v_copied, pool_step, pooled = sem("v_copied"), sem("pool_step"), sem("pooled")
        g_hi_ready, g_lo_ready = sem("g_hi_ready"), sem("g_lo_ready")
        grp_done, grp_y = sem("grp_done"), sem("grp_y")
        x_spilled, x_back = sem("x_spilled"), sem("x_back")
        block_done = sem("block_done")
        qkv_hi, qkv_lo = sem("qkv_hi"), sem("qkv_lo")
        gate_raw = sem("gate_raw")
        z_done, stick_step, stick_ln = sem("z_done"), sem("stick_step"), sem("stick_ln")
        sp_step, sp_split = sem("sp_step"), sem("sp_split")
        after_done, a_exp, a_step, a_split = sem("after_done"), sem("a_exp"), sem("a_step"), sem("a_split")
        o_done, o_hi_ready, o_lo_ready = sem("o_done"), sem("o_hi_ready"), sem("o_lo_ready")
        gate_ready, mg_ready = sem("gate_ready"), sem("mg_ready")
        rope_in_s, decay_in_s = sem("rope_loaded"), sem("decay_loaded")
        rot_step, rot_hi, rot_lo = sem("rot_step"), sem("rot_hi"), sem("rot_lo")
        rv_hi_ready, rv_lo_ready = sem("rv_hi_ready"), sem("rv_lo_ready")
        s_done, s_decayed, s_hi_ready, s_lo_ready = sem("s_done"), sem("s_decayed"), sem("s_hi_ready"), sem("s_lo_ready")
        ro_done, ro_sq, ro_stat, ro_root, ro_rs = sem("ro_done"), sem("ro_sq"), sem("ro_stat"), sem("ro_root"), sem("ro_rs")
        ro_norm, ro_silu, ro_w = sem("ro_norm"), sem("ro_silu"), sem("ro_w")
        pr_ready, merge_step = sem("pr_ready"), sem("merge_step")
        ff_silu, ff_prod, ff_hi, ff_lo = sem("ff_silu"), sem("ff_prod"), sem("ff_hi"), sem("ff_lo")
        out_stored = sem("out_stored")

        SQ_RING = 2

        def sq_buf(u):
            return {0: sq, 1: sq, 2: sq, 3: sq, 4: nsq, 5: fsq}[u]

        def t_buf(u):
            return {0: sa, 1: sa, 2: sa, 3: sa, 4: nt, 5: ft}[u]

        def x_count(u, k):
            return 8 * {2: 0, 3: 1, 4: 2, 5: 3}[u] + k + 1

        def mod_col(r, part, k):
            return 24 * r + 8 * part + k

        SHIFT = {0: (0, 0), 2: (1, 0), 3: (2, 0), 4: (3, 0)}
        GAIN = {0: "norm_g", 2: "norm_g", 3: "g_norm1", 4: "g_norm2"}
        GAIN_AT = {0: 0, 2: 8, 3: 0, 4: 0}
        FILL = {0: 0, 1: 1, 2: 2, 3: 4, 4: 6}
        GATE = {"conv": (0, 2), "pool": (1, 2), "out": (2, 2), "ffn": (3, 2)}

        block = ctx.enter_context(nc.Block())

        @block.sync
        def _(sp):
            sp.dma_start(cols[:, :], cols_in).then_inc(cols_in_s, 16)
            sp.dma_start(x_sb, x_in).then_inc(x_in_s, 16)
            sp.dma_start(c_stage[:, :], const_in).then_inc(const_in_s, 16)
            for n in range(2):
                sp.dma_start(w_raw[:, n], w_stream[n]).then_inc(w_landed[n], 16)

            def load(n, slot):
                sp.wait_ge(w_lo_done, n - 1)
                sp.dma_start(w_raw[:, slot], w_stream[n]).then_inc(w_landed[slot], 16)

            with sp.Fori(1, N_TILES // 2) as i:
                load(2 * i, 0)
                load(2 * i + 1, 1)
            load(N_TILES - 1, (N_TILES - 1) % 2)

        @block.gpsimd
        def _(pool):
            nc.gpsimd.memset(ones_c[:, :], 1.0).then_inc(ones_done, 1)
            pool.wait_ge(csil_done, 2)

            chunks = [(r, i, q) for r in range(4) for i in range(0 if r else DVE_GROUPS, ROUND_GROUPS) for q in range(4)]

            def load(c):
                r, i, q = chunks[c]
                if c >= 2:
                    pool.wait_ge(mod_step, 4 * (c - 1))
                pool.dma_start(mod_chunk[:, c % 2], mod_stream[i + ROUND_GROUPS * r, q]).then_inc(chunk_in[c % 2], 16)

            load(0)
            for c, (r, i, q) in enumerate(chunks):
                if c + 1 < len(chunks):
                    load(c + 1)
                pool.wait_ge(chunk_in[c % 2], 16 * (c // 2) + 16)
                acc = mod_acc[:, i * MOD_G:(i + 1) * MOD_G]
                if r and q == 0:
                    pool.wait_ge(mod_summed, 1 if r == 1 and i < DVE_GROUPS else r + 1)
                for b in range(2):
                    kb = 2 * q + b
                    col = kb + (0 if r < 2 else 8)
                    part, scalar = mod_chunk[:, c % 2, b], csil[:, col:col + 1]
                    nc.gpsimd.tensor_scalar(part, part, scalar, 1.0, ALU.mult, ALU.mult).then_inc(mod_step, 1)
                    pool.wait_ge(mod_step, 4 * c + 2 * b + 1)
                    if kb == 0:
                        nc.gpsimd.tensor_copy(acc, part).then_inc(mod_step, 1)
                    else:
                        nc.gpsimd.tensor_tensor(acc, acc, part, ALU.add).then_inc(mod_step, 1)

        def mod_steps(r):
            return 16 * (ROUND_GROUPS * (r + 1) - DVE_GROUPS)

        @block.tensor
        def _(pe):
            def three(out_ap, a_hi, a_lo, b_hi, b_lo, start, stop, inc=None):
                nc.tensor.matmul(out_ap, a_hi, b_hi, start=start, stop=False, skip_group_check=True)
                nc.tensor.matmul(out_ap, a_hi, b_lo, start=False, stop=False, skip_group_check=True)
                last = nc.tensor.matmul(out_ap, a_lo, b_hi, start=False, stop=stop, skip_group_check=True)
                if inc is not None:
                    last.then_inc(inc, 1)

            def split_ready(n):
                pe.wait_ge(w_hi_done, n + 1)
                pe.wait_ge(w_lo_done, n + 1)

            def tile(n, slot, src_hi, src_lo, before_block=None, kbs=KB, k0=0, first=True, last=True, bank=None):
                split_ready(n)
                bank = slot if bank is None else bank
                for m in range(2):
                    for k in range(kbs):
                        if m == 0 and before_block is not None:
                            before_block(k)
                        c = slice(P * m, P * m + P)
                        three(ps[:, bank, m, :], w_hi[:, slot, k, c], w_lo[:, slot, k, c],
                              src_hi[:, k0 + k, :], src_lo[:, k0 + k, :],
                              first and k == 0, last and k == kbs - 1,
                              tile_done if m == 1 and k == kbs - 1 else None)

            def tile_tokens(n, slot):
                split_ready(n)
                for tb in range(TB):
                    for k in range(KB):
                        c = slice(P * tb, P * tb + P)
                        three(ps_tok[:, slot, tb, :], h_hi[:, k, c], h_lo[:, k, c],
                              w_hi[:, slot, k, :], w_lo[:, slot, k, :], k == 0, k == KB - 1,
                              tile_done if tb == TB - 1 and k == KB - 1 else None)

            def h_block(fill):
                return lambda k: pe.wait_ge(h_lo_ready, 8 * fill + k + 1)

            def norm_stat(u, k):
                pe.wait_ge(sq_ready, 8 * u + k + 1)
                if u and k == 0:
                    pe.wait_ge(root_ready, u)
                nc.tensor.matmul(at_ps[:, 0, :], mean_m[:, :], sq_buf(u)[:, k % SQ_RING, :], start=(k == 0),
                                 stop=(k == KB - 1), skip_group_check=True).then_inc(sq_used, 1)

            def mod_sum(r, b0, nb, ready, count):
                pe.wait_ge(ready, count)
                for b in range(nb):
                    last = nc.tensor.matmul(at_ps[:, 3, b:b + 1], mod_acc[:, P * (b0 + b):P * (b0 + b + 1)],
                                            ones_c[:, 0:1], start=True, stop=True, skip_group_check=True)
                last.then_inc(mod_summed, 1)

            def update_tiles(n0, fill, u, src_hi=h_hi, src_lo=h_lo, ready=None):
                for j in range(4):
                    tile(n0 + j, (n0 + j) % 2, src_hi, src_lo, ready if j == 0 else None)
                    if j:
                        norm_stat(u, 2 * j - 2)
                        norm_stat(u, 2 * j - 1)
                norm_stat(u, 6)
                norm_stat(u, 7)

            pe.wait_ge(consts_done, 1)
            for k in range(KB):
                norm_stat(0, k)
            pe.wait_ge(ones_done, 1)
            mod_sum(0, 0, 16, first_mod, 4 * KB)

            for j in range(4):
                for i in range(3):
                    n = N_CONV + 3 * j + i
                    tile(n, n % 2, h_hi, h_lo, h_block(0) if n == 0 else None)
                if j == 0:
                    pe.wait_ge(mods_ready, 1)
                    mod_sum(0, 16, 8, mod_step, mod_steps(0))
                if j == 2:
                    pe.wait_ge(mods_ready, 2)
                    mod_sum(1, 0, 24, mod_step, mod_steps(1))
            for k in range(KB):
                pe.wait_ge(conv_step, CONV_W * (k + 1))
                nc.tensor.matmul(at_ps[:, 1, :], mean_m[:, :], y_sb[:, k, :], start=(k == 0), stop=(k == KB - 1),
                                 skip_group_check=True).then_inc(conv_summed, 1)
            for k in range(KB):
                norm_stat(1, k)
            update_tiles(N_CONV_OUT, 1, 2, ready=h_block(1))

            tile(N_POOL, 0, h_hi, h_lo, h_block(2))
            tile(N_POOL + 1, 1, h_hi, h_lo)
            tile(N_POOL + 2, 0, h_hi, h_lo)
            tile(N_POOL + 3, 1, h_hi, h_lo)
            pe.wait_ge(mods_ready, 3)
            mod_sum(2, 0, 24, mod_step, mod_steps(2))
            with pe.Fori(2, 4) as i:
                tile(2 * i + N_POOL, 0, h_hi, h_lo)
                tile(2 * i + N_POOL + 1, 1, h_hi, h_lo)
            pe.wait_ge(mods_ready, 4)
            split_ready(N_GRP)
            for g in range(4):
                pe.wait_ge(g_lo_ready, 2 * g + 2)
                if g == 0:
                    pe.wait_ge(w_hi_done, N_GRP + 2)
                for m in range(2):
                    out_ap = (ps[:, 1, m, :], at_ps[:, m, :], at_ps[:, 2 + m, :], ps[:, 0, m, :])[g]
                    for k in range(2):
                        c = slice(P * m, P * m + P)
                        three(out_ap, w_hi[:, 0, 2 * g + k, c], w_lo[:, 0, 2 * g + k, c], g_hi[:, 2 * g + k, :],
                              g_lo[:, 2 * g + k, :], k == 0, k == 1,
                              (tile_done if g == 3 and m == 1 else grp_done) if k == 1 else None)
            update_tiles(N_POOL_OUT, 3, 3, ready=h_block(3))
            mod_sum(3, 0, 24, mod_step, mod_steps(3))

            def scores(hd):
                rows, zp = slice(64 * (hd % 2), 64 * (hd % 2) + 64), z_ps[hd % 2]
                blk, s = hd % 4 // 2, hd // 4 % 2
                for j in range(TB):
                    w = T - P * j
                    z = zp[:, z_off(j):z_off(j) + w]
                    three(z, sbk_hi[s][rows, blk, P * j:P * j + P], sbk_lo[s][rows, blk, P * j:P * j + P],
                          sbq_hi[s][rows, blk, P * j:T], sbq_lo[s][rows, blk, P * j:T], j < 3, False)
                    last = nc.tensor.matmul(z[:, 0:P], eye_r[:, :], neg_r[:, :], start=False, stop=False,
                                            skip_group_check=True)
                last.then_inc(z_done, 1)

            def subtract_after(hd):
                pe.wait_ge(sp_split, hd + 1)
                zp = z_ps[hd % 2]
                for part in (att_hi, att_lo):
                    for j in range(TB):
                        for j2 in range(j, TB):
                            w = T - P * j2
                            o = z_off(j) + P * (j2 - j)
                            last = nc.tensor.matmul(zp[:, o:o + w], (ntri_r if j2 == j else none_r)[:, :],
                                                    part[:, hd % 2, z_off(j2):z_off(j2) + w],
                                                    start=False, stop=False, skip_group_check=True)
                last.then_inc(after_done, 1)

            def attend(hd):
                pe.wait_ge(a_split, hd + 1)
                if hd:
                    pe.wait_ge(o_lo_ready, hd)
                s = hd // 4 % 2
                c = slice(P * (hd % 4 // 2), P * (hd % 4 // 2) + P)
                for j in range(TB):
                    w = T - P * j
                    three(o_ps[:, P * j:T], sbv_hi[s][:, j, c], sbv_lo[s][:, j, c],
                          att_hi[:, hd % 2, z_off(j):z_off(j) + w], att_lo[:, hd % 2, z_off(j):z_off(j) + w],
                          j == 0, j == TB - 1, o_done if j == TB - 1 else None)

            def half_tile(n, m, bank, before_block=None):
                if m == 0:
                    split_ready(n)
                for k in range(KB):
                    if before_block is not None:
                        before_block(k)
                    c = slice(P * m, P * m + P)
                    three(ps_flat[:, T * bank:T * bank + T], w_hi[:, n % 2, k, c], w_lo[:, n % 2, k, c],
                          h_hi[:, k, :], h_lo[:, k, :], k == 0, k == KB - 1,
                          (tile_done if m else block_done) if k == KB - 1 else None)

            def quarter_tokens(n, tb, bank):
                if tb == 0:
                    split_ready(n)
                o = T * bank + TILE_W * (tb % 2)
                inc = {0: None, 1: block_done, 2: None, 3: tile_done}[tb]
                for k in range(KB):
                    c = slice(P * tb, P * tb + P)
                    three(ps_flat[:, o:o + TILE_W], h_hi[:, k, c], h_lo[:, k, c], w_hi[:, n % 2, k, :], w_lo[:, n % 2, k, :],
                          k == 0, k == KB - 1, inc if k == KB - 1 else None)

            def qkv_block(grp, b, bank, behind):
                n = N_SB + 3 * grp
                if 6 * grp + b - behind > 0:
                    pe.wait_ge(qkv_lo, 6 * grp + b - behind)
                half_tile(n + b // 2, b % 2, bank, h_block(4) if (grp, b) == (0, 0) else None)

            def v_block(grp, tb, bank, behind):
                b = 4 + tb // 2
                if tb % 2 == 0:
                    pe.wait_ge(qkv_lo, 6 * grp + b - behind)
                quarter_tokens(N_SB + 3 * grp + 2, tb, bank)

            def gate_block(b):
                if b:
                    pe.wait_ge(gate_raw, b)
                else:
                    pe.wait_ge(qkv_lo, 24)
                half_tile(N_SB_GATE + b // 2, b % 2, 0)

            for b in range(4):
                qkv_block(0, b, b, 4)
            for tb in range(TB):
                v_block(0, tb, tb // 2, 4)
            for grp in range(4):
                hd = 4 * grp

                def block(b):
                    if grp < 3:
                        qkv_block(grp + 1, b, 0, 0)
                    else:
                        gate_block(b)

                pe.wait_ge(qkv_lo, 6 * grp + 4)
                scores(hd)
                block(0)
                if grp == 0:
                    pe.wait_ge(qkv_lo, 6)
                scores(hd + 1)
                block(1)
                subtract_after(hd)
                block(2)
                subtract_after(hd + 1)
                pe.wait_ge(qkv_lo, 6 * grp + 6)
                attend(hd)
                block(3)
                scores(hd + 2)
                attend(hd + 1)
                scores(hd + 3)
                if grp < 3:
                    v_block(grp + 1, 0, 0, 0)
                    v_block(grp + 1, 1, 0, 0)
                    subtract_after(hd + 2)
                    v_block(grp + 1, 2, 0, 0)
                    subtract_after(hd + 3)
                    attend(hd + 2)
                    v_block(grp + 1, 3, 0, 0)
                    attend(hd + 3)
                else:
                    gate_block(4)
                    subtract_after(hd + 2)
                    gate_block(5)
                    subtract_after(hd + 3)
                    attend(hd + 2)
                    gate_block(6)
                    attend(hd + 3)
                    gate_block(7)

            pe.wait_ge(o_lo_ready, 16)
            pe.wait_ge(gate_raw, 8)
            with pe.Fori(0, 2) as i:
                tile(2 * i + N_SB_OUT, N_SB_OUT % 2, g_hi, g_lo)
                tile(2 * i + N_SB_OUT + 1, (N_SB_OUT + 1) % 2, g_hi, g_lo)

            def head(hd, n, parity):
                tile(n, parity, h_hi, h_lo)
                tile(n + 1, 1 - parity, h_hi, h_lo)
                tile_tokens(n + 2, parity)
                pe.wait_ge(rot_lo, hd * 4 + 4)
                for j in range(TB):
                    w = T - P * j
                    for c in range(2):
                        three(at_ps[:, j, 0:w], rk_hi[:, c, P * j:P * j + P], rk_lo[:, c, P * j:P * j + P],
                              rq_hi[:, c, P * j:T], rq_lo[:, c, P * j:T], c == 0, c == 1, s_done if c == 1 else None)
                tile_tokens(n + 3, 1 - parity)
                pe.wait_ge(rv_lo_ready, hd * 2 + 2)
                pe.wait_ge(s_lo_ready, hd * 4 + 4)
                for e in range(4):
                    for j in range(TB):
                        w = T - P * j
                        three(at_ps[:, e, P * j:T], rv_hi[:, j, P * e:P * e + P], rv_lo[:, j, P * e:P * e + P],
                              s_hi[:, z_off(j):z_off(j) + w], s_lo[:, z_off(j):z_off(j) + w],
                              j == 0, j == TB - 1, ro_done if j == TB - 1 else None)
                tile(n + 4, parity, h_hi, h_lo)
                for e in range(4):
                    pe.wait_ge(ro_sq, hd * 4 + e + 1)
                    nc.tensor.matmul(ps[:, 1 - parity, 0, :], mean_m[:, :], rt[:, e % 2, :], start=(e == 0), stop=(e == 3),
                                     skip_group_check=True).then_inc(ro_stat, 1)
                pe.wait_ge(ro_root, hd + 1)
                tile(n + 5, 1 - parity, h_hi, h_lo)

            with pe.Fori(0, 2) as i:
                head(i, i * 6 + N_RET1, N_RET1 % 2)
            pe.wait_ge(o_lo_ready, 16 + 8)
            with pe.Fori(0, 2) as i:
                tile(2 * i + N_RETP, N_RETP % 2, g_hi, g_lo)
                tile(2 * i + N_RETP + 1, (N_RETP + 1) % 2, g_hi, g_lo)
            with pe.Fori(0, 2) as i:
                head(i + 2, i * 6 + N_RET2, N_RET2 % 2)
            with pe.Fori(0, 2) as i:
                tile(2 * i + N_GATE, N_GATE % 2, h_hi, h_lo)
                tile(2 * i + N_GATE + 1, (N_GATE + 1) % 2, h_hi, h_lo)
            pe.wait_ge(o_lo_ready, 16 + 16)
            with pe.Fori(0, 2) as i:
                tile(2 * i + N_MERGE, N_MERGE % 2, g_hi, g_lo)
                tile(2 * i + N_MERGE + 1, (N_MERGE + 1) % 2, g_hi, g_lo)
            update_tiles(N_OUT, 5, 4, ready=h_block(5))

            tile(N_FFN, N_FFN % 2, h_hi, h_lo, h_block(6))
            tile(N_FFN + 1, (N_FFN + 1) % 2, h_hi, h_lo)
            with pe.Fori(1, 11) as i:
                tile(2 * i + N_FFN, N_FFN % 2, h_hi, h_lo)
                tile(2 * i + N_FFN + 1, (N_FFN + 1) % 2, h_hi, h_lo)

            def ffn_out(n, parity, bank, ready=None):
                tile(n, parity, f_hi, f_lo, ready, first=True, last=False, bank=bank)
                tile(n + 1, 1 - parity, f_hi, f_lo, ready, k0=8, first=False, last=False, bank=bank)
                tile(n + 2, parity, f_hi, f_lo, ready, kbs=FFB - 16, k0=16, first=False, last=True, bank=bank)

            pe.wait_ge(ff_lo, FFB)
            for j in range(4):
                n = N_FFN_OUT + 3 * j
                ffn_out(n, n % 2, j % 2)
                if j:
                    norm_stat(5, 2 * j - 2)
                    norm_stat(5, 2 * j - 1)
            norm_stat(5, 6)
            norm_stat(5, 7)

        @block.scalar
        def _(act):
            def split(n, slot):
                act.wait_ge(w_landed[slot], (n - slot) * 8 + 16)
                nc.scalar.activation(w_hi[:, slot], w_raw[:, slot], ACT.Copy).then_inc(w_hi_done, 1)

            def done(n):
                act.wait_ge(tile_done, n + 1)

            def squares(u, k, src):
                if 8 * u + k >= SQ_RING:
                    act.wait_ge(sq_used, 8 * u + k - SQ_RING + 1)
                nc.scalar.activation(sq_buf(u)[:, k % SQ_RING, :], src, ACT.Square).then_inc(sq_ready, 1)

            def root(u):
                act.wait_ge(sq_used, 8 * u + 8)
                nc.scalar.activation(rs[:, :], at_ps[:, 0, :], ACT.Sqrt, bias=eps_c[:, 0:1]).then_inc(root_ready, 1)

            def norm_hi(u, n_free):
                r, part = SHIFT[u]
                idx = {0: 0, 2: 1, 3: 2, 4: 3}[u]
                if n_free:
                    done(n_free - 1)
                for k in range(KB):
                    act.wait_ge(t_ready, 8 * idx + k + 1)
                    c = mod_col(r, part, k)
                    nc.scalar.activation(h_hi[:, k, :], t_buf(u)[:, k % 4, :], ACT.Identity,
                                         bias=mods[:, c:c + 1]).then_inc(h_hi_ready, 1)

            def update_steps(n0, u):
                for j in range(4):
                    done(n0 + j)
                    split(n0 + j + 2, (n0 + j) % 2)
                    for m in range(2):
                        act.wait_ge(x_updated, x_count(u, 2 * j + m))
                        squares(u, 2 * j + m, x_sb[:, 2 * j + m, :])
                root(u)

            for i in range(8):
                act.dma_start(first_chunk[i // 4][:, i % 4], mod_stream[i // 4, i % 4]).then_inc(first_in[i], 16)
            act.wait_ge(cols_in_s, 16)
            for i, name in enumerate(("c", "c_2")):
                nc.scalar.activation(csil[:, 8 * i:8 * i + 8], cols[:, COLS[name]:COLS[name] + 8], ACT.Silu).then_inc(csil_done, 1)
            act.wait_ge(x_in_s, 16)
            act.wait_ge(pads_done, 1)
            for k in range(KB):
                squares(0, k, x_sb[:, k, :])
            for i in range(8):
                act.wait_ge(first_mod, 2 * i + 2)
                act.dma_start(first_chunk[i // 4][:, i % 4], mod_stream[2 + i // 4, i % 4]).then_inc(first_in[i], 16)
            root(0)
            for n in range(2):
                split(n, n)
            norm_hi(0, 0)

            for j in range(4):
                n = N_CONV + 3 * j
                done(n)
                if j:
                    act.wait_ge(y_ready, 2 * j)
                else:
                    act.wait_ge(h_lo_ready, 8)
                nc.scalar.activation(sa[:, 0:2, :], ps[:, n % 2], ACT.Copy).then_inc(a_copied, 1)
                split(n + 2, n % 2)
                done(n + 1)
                nc.scalar.activation(sa[:, 2:4, :], ps[:, (n + 1) % 2], ACT.Sigmoid).then_inc(sig_ready, 1)
                split(n + 3, (n + 1) % 2)
                done(n + 2)
                if j == 0:
                    act.wait_ge(first_mod, 4 * KB)
                nc.scalar.activation(gs_sb[:, 2 * j:2 * j + 2, :], ps[:, n % 2], ACT.Silu).then_inc(gs_ready, 1)
                split(n + 4, n % 2)
            for k in range(KB):
                act.wait_ge(centred, k + 1)
                squares(1, k, y_sb[:, k, :])
            root(1)
            done(N_CONV_OUT - 1)

            def ln_activate(k):
                act.wait_ge(ln_t, k + 1)
                c = COLS["cv_ln_b"] + k
                nc.scalar.activation(sa[:, k % 4, :], sa[:, k % 4, :], ACT.Silu, bias=cols[:, c:c + 1]).then_inc(ln_silu, 1)

            ln_activate(0)
            for k in range(KB):
                if k + 1 < KB:
                    ln_activate(k + 1)
                act.wait_ge(ln_y, k + 1)
                nc.scalar.activation(h_hi[:, k, :], y_sb[:, k, :], ACT.Copy).then_inc(h_hi_ready, 1)
            update_steps(N_CONV_OUT, 2)
            norm_hi(2, N_POOL)

            act.wait_ge(pads_done, 2)
            for j in range(4):
                n = N_POOL + j
                done(n)
                if j:
                    act.wait_ge(g_lo_ready, 2 * j)
                nc.scalar.activation(vpad[:, :, POOL_PAD:POOL_PAD + T], ps[:, n % 2], ACT.Copy).then_inc(v_copied, 1)
                split(n + 2, n % 2)
                for m in range(2):
                    act.wait_ge(pooled, 2 * j + m + 1)
                    nc.scalar.activation(g_hi[:, 2 * j + m, :], pool_b[:, m, 0:T], ACT.Copy).then_inc(g_hi_ready, 1)
            for j in range(4):
                n = N_POOL + 4 + j
                done(n)
                nc.scalar.activation(gs_sb[:, 2 * j:2 * j + 2, :], ps[:, n % 2], ACT.Silu).then_inc(gs_ready, 1)
                split(n + 2, n % 2)
            for k in range(KB):
                act.wait_ge(grp_y, k + 1)
                nc.scalar.activation(h_hi[:, k, :], sa[:, k % 4, :], ACT.Copy).then_inc(h_hi_ready, 1)
            done(N_GRP)
            split(N_GRP + 2, N_GRP % 2)
            update_steps(N_POOL_OUT, 3)
            norm_hi(3, N_SB)
            act.wait_ge(h_lo_ready, 8 * 4 + 8)
            act.dma_start(x_spill, x_sb).then_inc(x_spilled, 16)

            def softplus_log(hd):
                s = hd % 2
                act.wait_ge(z_done, hd + 1)
                if hd >= 2:
                    act.wait_ge(a_split, hd - 1)
                zt = z_tmp[:, s, :]
                nc.scalar.activation(zt, z_ps[s][:, 0:Z_W], ACT.Abs).then_inc(stick_step, 1)
                act.wait_ge(stick_step, hd * 2 + 1)
                nc.scalar.activation(zt, zt, ACT.Exp, scale=-1.0).then_inc(stick_step, 1)
                act.wait_ge(stick_step, hd * 2 + 2)
                nc.scalar.activation(zt, zt, ACT.Ln, bias=1.0).then_inc(stick_ln, 1)

            def weights(hd):
                act.wait_ge(after_done, hd + 1)
                nc.scalar.activation(z_tmp[:, hd % 2, :], z_ps[hd % 2][:, 0:Z_W], ACT.Exp).then_inc(a_exp, 1)

            def output_hi(hd):
                act.wait_ge(o_done, hd + 1)
                rows = slice(64 * (hd % 2), 64 * (hd % 2) + 64)
                nc.scalar.activation(g_hi[rows, hd // 2, :], o_ps[rows, :], ACT.Copy).then_inc(o_hi_ready, 1)

            def half_done(n, b):
                if b % 2:
                    done(n)
                else:
                    act.wait_ge(block_done, (n - N_SB) + 1)

            def qkv_high(grp, b, bank):
                half_done(N_SB + 3 * grp + b // 2, b)
                kind, m, s = b // 2, b % 2, grp % 2
                src = ps_flat[:, T * bank:T * bank + T]
                if kind == 2:
                    dst, src = sbv_hi[s][:, 2 * m:2 * m + 2, :], src.rearrange("p (b c) -> p b c", c=TILE_W)
                else:
                    dst = (sbq_hi, sbk_hi)[kind][s][:, m, :]
                nc.scalar.activation(dst, src, ACT.Copy, scale=SB_SCALE if kind == 0 else 1.0).then_inc(qkv_hi, 1)

            def gate_high(b):
                half_done(N_SB_GATE + b // 2, b)
                if b == 0:
                    act.wait_ge(o_done, 12)
                c = COLS["b_branch"] + b
                nc.scalar.activation(sb_gates[:, b, :], ps_flat[:, 0:T], ACT.Identity, bias=cols[:, c:c + 1]).then_inc(gate_raw, 1)

            nc.scalar.preload_act_table_set("natural_log_exp_and_others")
            for b in range(6):
                qkv_high(0, b, b % 4)
                if b % 2:
                    split(N_SB + b // 2 + 2, (N_SB + b // 2) % 2)
            act.wait_ge(x_spilled, 16)
            for grp in range(4):
                hd, n = 4 * grp, N_SB + 3 * grp + 3

                def high(b):
                    if grp < 3:
                        qkv_high(grp + 1, b, 0)
                    else:
                        gate_high(b)

                softplus_log(hd)
                high(0)
                softplus_log(hd + 1)
                high(1)
                split(n + 2, n % 2)
                weights(hd)
                high(2)
                weights(hd + 1)
                output_hi(hd)
                high(3)
                softplus_log(hd + 2)
                output_hi(hd + 1)
                softplus_log(hd + 3)
                split(n + 3, (n + 1) % 2)
                high(4)
                weights(hd + 2)
                if grp == 3:
                    high(5)
                weights(hd + 3)
                output_hi(hd + 2)
                high(5 if grp < 3 else 6)
                output_hi(hd + 3)
                split(n + 4, n % 2)
            gate_high(7)

            for half in range(2):
                act.wait_ge(gate_raw, 8)
                part = sb_gates[:, 4 * half:4 * half + 4, :]
                nc.scalar.activation(part, part, ACT.Sigmoid).then_inc(gate_ready, 1)
                if half == 0:
                    split(N_SB_OUT + 1, (N_SB_OUT + 1) % 2)
            for j in range(4):
                n = N_SB_OUT + j
                done(n)
                split(n + 2, n % 2)
            act.wait_ge(mg_ready, 4)
            act.wait_ge(mods_ready, 5)
            act.dma_start(rope, rope_in).then_inc(rope_in_s, 16)

            def head(hd, n, parity, g_at):
                if not (isinstance(hd, int) and hd == 0):
                    act.wait_ge(s_decayed, hd * 4)
                act.dma_start(decay[:, :], decay_in[hd]).then_inc(decay_in_s, 16)
                for i, (dst, scale) in enumerate(((rq_hi, 1.0), (rk_hi, RK_SCALE))):
                    slot = (parity + i) % 2
                    done(n + i)
                    for m in range(2):
                        act.wait_ge(rot_step, hd * 4 + 2 * i + m + 1)
                        nc.scalar.activation(dst[:, m, :], rt[:, m, :], ACT.Copy, scale=scale).then_inc(rot_hi, 1)
                    split(n + i + 2, slot)
                for i in range(2):
                    slot = (parity + i) % 2
                    done(n + 2 + i)
                    nc.scalar.activation(rv_hi[:, :, TILE_W * i:TILE_W * (i + 1)], ps_tok[:, slot], ACT.Copy).then_inc(rv_hi_ready, 1)
                    split(n + i + 4, slot)
                    if i == 0:
                        for j in range(TB):
                            w = T - P * j
                            act.wait_ge(s_decayed, hd * 4 + j + 1)
                            nc.scalar.activation(s_hi[:, z_off(j):z_off(j) + w], rt[:, j % 2, 0:w], ACT.Copy).then_inc(s_hi_ready, 1)
                for e in range(4):
                    act.wait_ge(ro_done, hd * 4 + e + 1)
                    if e >= 2:
                        act.wait_ge(ro_stat, hd * 4 + e - 1)
                    nc.scalar.activation(rt[:, e % 2, :], at_ps[:, e, :], ACT.Square).then_inc(ro_sq, 1)
                act.wait_ge(ro_stat, hd * 4 + 4)
                nc.scalar.activation(rs[:, :], ps[:, 1 - parity, 0, :], ACT.Sqrt, scale=2.0, bias=eps_c[:, 0:1]).then_inc(ro_root, 1)
                for i in range(2):
                    slot = (parity + i) % 2
                    done(n + 4 + i)
                    if i:
                        act.wait_ge(ro_w, hd * 4 + 2)
                    nc.scalar.activation(rt[:, 2:4, :], ps[:, slot], ACT.Silu).then_inc(ro_silu, 1)
                    split(n + 6 + i, slot)
                    for m in range(2):
                        e = 2 * i + m
                        act.wait_ge(ro_w, hd * 4 + e + 1)
                        nc.scalar.activation(g_hi[:, g_at + e, :], rt[:, m, :], ACT.Copy).then_inc(o_hi_ready, 1)

            for i in range(2):
                head(i, i * 6 + N_RET1, N_RET1 % 2, i * 4)
            for j in range(4):
                n = N_RETP + j
                done(n)
                nc.scalar.activation(pr[:, 2 * j:2 * j + 2, :], ps[:, n % 2], ACT.Copy).then_inc(pr_ready, 1)
                split(n + 2, n % 2)
            for i in range(2):
                head(i + 2, i * 6 + N_RET2, N_RET2 % 2, i * 4)
            for j in range(4):
                n = N_GATE + j
                done(n)
                if j == 0:
                    act.wait_ge(o_lo_ready, 16 + 16)
                for m in range(2):
                    c = COLS["b_branch"] + 8 + 2 * j + m
                    nc.scalar.activation(gates[:, 2 * j + m, :], ps[:, n % 2, m, :], ACT.Sigmoid, bias=cols[:, c:c + 1]).then_inc(gate_ready, 1)
                split(n + 2, n % 2)
            for j in range(4):
                n = N_MERGE + j
                done(n)
                for m in range(2):
                    act.wait_ge(merge_step, 3 * (2 * j + m) + 3)
                    nc.scalar.activation(h_hi[:, 2 * j + m, :], mg[:, 2 * j + m, :], ACT.Copy).then_inc(h_hi_ready, 1)
                split(n + 2, n % 2)
            act.wait_ge(h_lo_ready, 8 * 5 + 8)
            act.dma_start(x_sb, x_spill).then_inc(x_back, 16)
            update_steps(N_OUT, 4)
            norm_hi(4, N_FFN)

            def ffn_pair(j, n, parity):
                done(n)
                if not (isinstance(j, int) and j == 0):
                    act.wait_ge(ff_prod, j * 2)
                nc.scalar.activation(ft[:, 0:2, :], ps[:, parity], ACT.Silu).then_inc(ff_silu, 1)
                split(n + 2, parity)
                done(n + 1)
                for m in range(2):
                    act.wait_ge(ff_prod, j * 2 + m + 1)
                    nc.scalar.activation(f_hi[:, j * 2 + m, :], ft[:, 2 + m, :], ACT.Copy).then_inc(ff_hi, 1)
                split(n + 3, 1 - parity)

            act.wait_ge(h_lo_ready, 8 * 6 + 8)
            ffn_pair(0, N_FFN, N_FFN % 2)
            with act.Fori(1, 11) as i:
                ffn_pair(i, 2 * i + N_FFN, N_FFN % 2)
            for j in range(4):
                for i in range(3):
                    n = N_FFN_OUT + 3 * j + i
                    done(n)
                    if n + 2 < N_TILES:
                        split(n + 2, n % 2)
                for m in range(2):
                    act.wait_ge(x_updated, x_count(5, 2 * j + m))
                    squares(5, 2 * j + m, x_sb[:, 2 * j + m, :])
            root(5)
            for k in range(KB):
                act.wait_ge(t_ready, 8 * 4 + k + 1)
                act.dma_start(out[:, k, :], x_sb[:, k, :]).then_inc(out_stored, 16)
            act.wait_ge(out_stored, 16 * KB)

        @block.vector
        def _(dve):
            def split(n, slot):
                dve.wait_ge(w_hi_done, n + 1)
                nc.vector.tensor_tensor(w_lo[:, slot], w_raw[:, slot], w_hi[:, slot].bitcast(F32),
                                        ALU.subtract).then_inc(w_lo_done, 1)

            def done(n):
                dve.wait_ge(tile_done, n + 1)

            def low(dst, src, hi, inc, scale=None):
                if scale is None:
                    nc.vector.tensor_tensor(dst, src, hi.bitcast(F32), ALU.subtract).then_inc(inc, 1)
                else:
                    nc.vector.scalar_tensor_tensor(dst, src, scale, hi.bitcast(F32), ALU.mult, ALU.subtract).then_inc(inc, 1)

            def take_mods(r, b0, nb, count):
                dve.wait_ge(mod_summed, count)
                src = COLS["b_mod"] + 24 * r + b0 if r < 2 else COLS["b_ada"] + 24 * (r - 2) + b0
                dst = 24 * r + b0
                nc.vector.tensor_tensor(mods[:, dst:dst + nb], at_ps[:, 3, 0:nb], cols[:, src:src + nb],
                                        ALU.add).then_inc(mods_ready, 1)
                dve.wait_ge(mods_ready, count)

            def gain(u):
                idx = {0: 0, 2: 1, 3: 2, 4: 3}[u]
                r, part = SHIFT[u]
                c, g = mod_col(r, part + 1, 0), COLS[GAIN[u]] + GAIN_AT[u]
                nc.vector.scalar_tensor_tensor(gp[:, :], mods[:, c:c + 8], 1.0, cols[:, g:g + 8], ALU.add,
                                               ALU.mult).then_inc(gp_ready, 1)
                dve.wait_ge(gp_ready, idx + 1)

            def invert(u):
                dve.wait_ge(root_ready, u + 1)
                nc.vector.reciprocal(rs[:, :], rs[:, :]).then_inc(rs_ready, 1)
                dve.wait_ge(rs_ready, u + 1)

            def norm(u):
                idx = {0: 0, 2: 1, 3: 2, 4: 3}[u]
                r, part = SHIFT[u]
                tb = t_buf(u)

                def lows(k):
                    dve.wait_ge(h_hi_ready, 8 * FILL[u] + k + 1)
                    c = mod_col(r, part, k)
                    nc.vector.scalar_tensor_tensor(h_lo[:, k, :], tb[:, k % 4, :], mods[:, c:c + 1],
                                                   h_hi[:, k, :].bitcast(F32), ALU.add, ALU.subtract).then_inc(h_lo_ready, 1)

                for k in range(KB):
                    if k >= 4:
                        dve.wait_ge(h_lo_ready, 8 * FILL[u] + k - 3)
                    nc.vector.scalar_tensor_tensor(tb[:, k % 4, :], x_sb[:, k, :], gp[:, k:k + 1], rs[:, :], ALU.mult,
                                                   ALU.mult).then_inc(t_ready, 1)
                    if k:
                        lows(k - 1)
                lows(KB - 1)

            def update_steps(n0, u, gate, x0):
                r, part = GATE[gate]
                for j in range(4):
                    n = n0 + j
                    done(n)
                    for m in range(2):
                        k = 2 * j + m
                        c = mod_col(r, part, k)
                        nc.vector.scalar_tensor_tensor(x_sb[:, k, :], ps[:, n % 2, m, :], mods[:, c:c + 1], x_sb[:, k, :],
                                                       ALU.mult, ALU.add).then_inc(x_updated, 1)
                    split(n + 2, n % 2)

            nc.vector.memset(eps_c[:, :], EPS)
            nc.vector.memset(ypad[:, :, :], 0.0).then_inc(pads_done, 1)
            dve.wait_ge(const_in_s, 16)
            nc.vector.tensor_copy(pool_edge[:, :], c_stage[:, C_POOL:C_POOL + 64])
            for dst, c in ((eye_r, C_EYE), (neg_r, C_NEG), (ntri_r, C_NTRI), (none_r, C_NONE)):
                nc.vector.tensor_copy(dst[:, :], c_stage[:, c:c + P])
            nc.vector.tensor_copy(mean_m[:, :], c_stage[:, C_MEAN:C_MEAN + P]).then_inc(consts_done, 1)
            dve.wait_ge(csil_done, 2)
            for g in range(DVE_GROUPS):
                acc = mod_acc[:, MOD_G * g:MOD_G * (g + 1)]
                for kb in range(KB):
                    i = 4 * g + kb // 2
                    if kb % 2 == 0:
                        dve.wait_ge(first_in[i % 8], 16 * (i // 8) + 16)
                    src = first_chunk[(i % 8) // 4][:, i % 4, kb % 2]
                    c = csil[:, kb:kb + 1]
                    if kb == 0:
                        nc.vector.tensor_scalar(acc, src, c, None, ALU.mult).then_inc(first_mod, 1)
                    else:
                        dve.wait_ge(first_mod, 8 * g + kb)
                        nc.vector.scalar_tensor_tensor(acc, src, c, acc, ALU.mult, ALU.add).then_inc(first_mod, 1)
            for n in range(2):
                split(n, n)
            take_mods(0, 0, 16, 1)
            gain(0)
            invert(0)
            norm(0)

            def convolve(k):
                w, db = COLS["dw"] + CONV_W * k, COLS["cv_db"] + k
                src = ypad[:, k % 2, :]
                nc.vector.tensor_scalar(y_sb[:, k, :], src[:, 0:T], cols[:, w:w + 1], cols[:, db:db + 1], ALU.mult,
                                        ALU.add).then_inc(conv_step, 1)
                for t in range(1, CONV_W):
                    dve.wait_ge(conv_step, CONV_W * k + t)
                    nc.vector.scalar_tensor_tensor(y_sb[:, k, :], src[:, t:t + T], cols[:, w + t:w + t + 1], y_sb[:, k, :],
                                                   ALU.mult, ALU.add).then_inc(conv_step, 1)

            for j in range(4):
                n = N_CONV + 3 * j
                done(n)
                split(n + 2, n % 2)
                done(n + 1)
                dve.wait_ge(a_copied, j + 1)
                dve.wait_ge(sig_ready, j + 1)
                if j:
                    dve.wait_ge(conv_step, CONV_W * 2 * j)
                for m in range(2):
                    nc.vector.tensor_tensor(ypad[:, m, PAD:PAD + T], sa[:, m, :], sa[:, 2 + m, :], ALU.mult).then_inc(y_ready, 1)
                split(n + 3, (n + 1) % 2)
                dve.wait_ge(y_ready, 2 * j + 2)
                convolve(2 * j)
                done(n + 2)
                split(n + 4, n % 2)
                convolve(2 * j + 1)
                if j == 1:
                    take_mods(0, 16, 8, 2)
                if j == 3:
                    take_mods(1, 0, 24, 3)
            dve.wait_ge(conv_summed, KB)
            for k in range(KB):
                nc.vector.tensor_tensor(y_sb[:, k, :], y_sb[:, k, :], at_ps[:, 1, :], ALU.subtract).then_inc(centred, 1)
            invert(1)

            def scaled(k):
                if k >= 4:
                    dve.wait_ge(ln_y, k - 3)
                c = COLS["cv_ln_g"] + k
                nc.vector.scalar_tensor_tensor(sa[:, k % 4, :], y_sb[:, k, :], cols[:, c:c + 1], rs[:, :], ALU.mult,
                                               ALU.mult).then_inc(ln_t, 1)

            def gated(k):
                dve.wait_ge(ln_silu, k + 1)
                nc.vector.tensor_tensor(y_sb[:, k, :], sa[:, k % 4, :], gs_sb[:, k, :], ALU.mult).then_inc(ln_y, 1)

            def gated_low(k):
                dve.wait_ge(h_hi_ready, 8 + k + 1)
                low(h_lo[:, k, :], y_sb[:, k, :], h_hi[:, k, :], h_lo_ready)

            scaled(0)
            scaled(1)
            for k in range(KB):
                gated(k)
                if k + 2 < KB:
                    scaled(k + 2)
                if k:
                    gated_low(k - 1)
            gated_low(KB - 1)
            update_steps(N_CONV_OUT, 2, "conv", 0)
            gain(2)
            invert(2)
            norm(2)

            nc.vector.memset(vpad[:, :, 0:POOL_PAD], 0.0)
            nc.vector.memset(vpad[:, :, POOL_PAD + T:PW], 0.0).then_inc(pads_done, 1)
            steps = 0
            for j in range(4):
                n = N_POOL + j
                win = 2 << j
                done(n)
                dve.wait_ge(v_copied, j + 1)
                src, ln = vpad, PW
                for lvl in range(j + 1):
                    d = 1 << lvl
                    dst = pool_a if (j - lvl) % 2 == 0 else pool_b
                    ln -= d
                    nc.vector.tensor_tensor(dst[:, :, 0:ln], src[:, :, 0:ln], src[:, :, d:d + ln], ALU.add).then_inc(pool_step, 1)
                    steps += 1
                    dve.wait_ge(pool_step, steps)
                    src = dst
                assert src is pool_a
                o = POOL_PAD - win // 2
                tok = vpad[:, :, POOL_PAD:POOL_PAD + T]
                nc.vector.scalar_tensor_tensor(pool_b[:, :, 0:T], pool_a[:, :, o:o + T], 1.0 / win, tok, ALU.mult,
                                               ALU.subtract).then_inc(pool_step, 1)
                dve.wait_ge(pool_step, steps + 1)
                for m in range(2):
                    for side, e in ((0, 0), (T - 8, 8)):
                        nc.vector.tensor_tensor(pool_a[:, m, o + side:o + side + 8], pool_a[:, m, o + side:o + side + 8],
                                                pool_edge[:, 16 * j + e:16 * j + e + 8], ALU.mult).then_inc(pool_step, 1)
                steps += 5
                dve.wait_ge(pool_step, steps)
                for m in range(2):
                    nc.vector.tensor_tensor(pool_b[:, m, 0:8], pool_a[:, m, o:o + 8], tok[:, m, 0:8],
                                            ALU.subtract).then_inc(pool_step, 1)
                    nc.vector.tensor_tensor(pool_b[:, m, T - 8:T], pool_a[:, m, o + T - 8:o + T], tok[:, m, T - 8:T],
                                            ALU.subtract).then_inc(pooled, 1)
                steps += 2
                split(n + 2, n % 2)
                for m in range(2):
                    dve.wait_ge(g_hi_ready, 2 * j + m + 1)
                    low(g_lo[:, 2 * j + m, :], pool_b[:, m, 0:T], g_hi[:, 2 * j + m, :], g_lo_ready)
            for j in range(4):
                n = N_POOL + 4 + j
                done(n)
                if n + 2 < N_GRP + 2:
                    split(n + 2, n % 2)
            take_mods(2, 0, 24, 4)
            dve.wait_ge(gs_ready, 8)

            def group_y(k):
                if k == 7:
                    done(N_GRP)
                else:
                    dve.wait_ge(grp_done, k + 1)
                if k >= 4:
                    dve.wait_ge(h_lo_ready, 24 + k - 3)
                src = (ps[:, 1, k % 2, :], at_ps[:, k % 2, :], at_ps[:, 2 + k % 2, :], ps[:, 0, k % 2, :])[k // 2]
                c = COLS["pl_scale"] + k
                nc.vector.scalar_tensor_tensor(sa[:, k % 4, :], src, cols[:, c:c + 1], gs_sb[:, k, :], ALU.mult,
                                               ALU.mult).then_inc(grp_y, 1)

            def group_low(k):
                dve.wait_ge(h_hi_ready, 24 + k + 1)
                low(h_lo[:, k, :], sa[:, k % 4, :], h_hi[:, k, :], h_lo_ready)

            done(N_GRP - 1)
            for k in range(KB):
                group_y(k)
                if k:
                    group_low(k - 1)
            group_low(KB - 1)
            split(N_GRP + 2, N_GRP % 2)
            update_steps(N_POOL_OUT, 3, "pool", 8)
            take_mods(3, 0, 24, 5)
            gain(3)
            invert(3)
            norm(3)

            def softplus_high(hd):
                s = hd % 2
                dve.wait_ge(stick_ln, hd + 1)
                zt = z_tmp[:, s, :]
                nc.vector.scalar_tensor_tensor(zt, z_ps[s][:, 0:Z_W], 0.0, zt, ALU.max, ALU.add).then_inc(sp_step, 1)
                dve.wait_ge(sp_step, hd * 2 + 1)
                nc.vector.tensor_copy(att_hi[:, s, :], zt).then_inc(sp_step, 1)

            def softplus_low(hd):
                s = hd % 2
                dve.wait_ge(sp_step, hd * 2 + 2)
                low(att_lo[:, s, :], z_tmp[:, s, :], att_hi[:, s, :], sp_split)

            def weights_split(hd):
                s = hd % 2
                dve.wait_ge(a_exp, hd + 1)
                zt = z_tmp[:, s, :]
                nc.vector.tensor_copy(att_hi[:, s, :], zt).then_inc(a_step, 1)
                dve.wait_ge(a_step, hd + 1)
                low(att_lo[:, s, :], zt, att_hi[:, s, :], a_split)

            def output_low(hd):
                dve.wait_ge(o_hi_ready, hd + 1)
                rows = slice(64 * (hd % 2), 64 * (hd % 2) + 64)
                low(g_lo[rows, hd // 2, :], o_ps[rows, :], g_hi[rows, hd // 2, :], o_lo_ready)

            def qkv_low_part(grp, b, bank):
                dve.wait_ge(qkv_hi, 6 * grp + b + 1)
                kind, m, s = b // 2, b % 2, grp % 2
                src = ps_flat[:, T * bank:T * bank + T]
                if kind == 2:
                    c = slice(2 * m, 2 * m + 2)
                    low(sbv_lo[s][:, c, :], src.rearrange("p (b c) -> p b c", c=TILE_W), sbv_hi[s][:, c, :], qkv_lo)
                else:
                    dst, hi = ((sbq_lo, sbq_hi), (sbk_lo, sbk_hi))[kind]
                    low(dst[s][:, m, :], src, hi[s][:, m, :], qkv_lo, SB_SCALE if kind == 0 else None)

            for b in range(6):
                qkv_low_part(0, b, b % 4)
                if b % 2:
                    split(N_SB + b // 2 + 2, (N_SB + b // 2) % 2)
            for grp in range(4):
                hd, n = 4 * grp, N_SB + 3 * grp + 3

                def lows(b):
                    if grp < 3:
                        qkv_low_part(grp + 1, b, 0)

                softplus_high(hd)
                lows(0)
                softplus_low(hd)
                softplus_high(hd + 1)
                lows(1)
                softplus_low(hd + 1)
                split(n + 2, n % 2)
                weights_split(hd)
                lows(2)
                weights_split(hd + 1)
                output_low(hd)
                lows(3)
                softplus_high(hd + 2)
                softplus_low(hd + 2)
                output_low(hd + 1)
                softplus_high(hd + 3)
                lows(4)
                softplus_low(hd + 3)
                weights_split(hd + 2)
                split(n + 3, (n + 1) % 2)
                weights_split(hd + 3)
                output_low(hd + 2)
                lows(5)
                output_low(hd + 3)
                split(n + 4, n % 2)

            split(N_SB_OUT + 1, (N_SB_OUT + 1) % 2)
            for j in range(4):
                n = N_SB_OUT + j
                done(n)
                dve.wait_ge(gate_ready, j // 2 + 1)
                nc.vector.tensor_tensor(mg[:, 2 * j:2 * j + 2, :], ps[:, n % 2], sb_gates[:, 2 * j:2 * j + 2, :],
                                        ALU.mult).then_inc(mg_ready, 1)
                split(n + 2, n % 2)

            dve.wait_ge(rope_in_s, 16)
            cos, sin = rope[:, 0, :], rope[:, 1, :]

            def rotate(i, slot, hd):
                a, b = ps[:, slot, 0, :], ps[:, slot, 1, :]
                for half, (p, q, op) in enumerate(((cos, sin, ALU.subtract), (sin, cos, ALU.add))):
                    nc.vector.tensor_tensor(rt[:, half, :], a, p, ALU.mult).then_inc(ro_norm, 1)
                    nc.vector.tensor_tensor(rt[:, 2 + half, :], b, q, ALU.mult).then_inc(ro_norm, 1)
                    dve.wait_ge(ro_norm, hd * 12 + 4 * i + 2 * half + 2)
                    nc.vector.tensor_tensor(rt[:, half, :], rt[:, half, :], rt[:, 2 + half, :], op).then_inc(rot_step, 1)

            def head(hd, n, parity, g_at):
                for i, (dst, hi, scale) in enumerate(((rq_lo, rq_hi, None), (rk_lo, rk_hi, RK_SCALE))):
                    slot = (parity + i) % 2
                    done(n + i)
                    rotate(i, slot, hd)
                    for m in range(2):
                        dve.wait_ge(rot_hi, hd * 4 + 2 * i + m + 1)
                        low(dst[:, m, :], rt[:, m, :], hi[:, m, :], rot_lo, scale)
                    dve.wait_ge(rot_lo, hd * 4 + 2 * i + 2)
                    split(n + i + 2, slot)
                dve.wait_ge(decay_in_s, hd * 16 + 16)
                for i in range(2):
                    slot = (parity + i) % 2
                    done(n + 2 + i)
                    dve.wait_ge(rv_hi_ready, hd * 2 + i + 1)
                    low(rv_lo[:, :, TILE_W * i:TILE_W * (i + 1)], ps_tok[:, slot], rv_hi[:, :, TILE_W * i:TILE_W * (i + 1)], rv_lo_ready)
                    split(n + i + 4, slot)
                    if i == 0:
                        def s_low(j):
                            w = T - P * j
                            dve.wait_ge(s_hi_ready, hd * 4 + j + 1)
                            low(s_lo[:, z_off(j):z_off(j) + w], rt[:, j % 2, 0:w], s_hi[:, z_off(j):z_off(j) + w], s_lo_ready)

                        for j in range(TB):
                            w = T - P * j
                            dve.wait_ge(s_done, hd * 4 + j + 1)
                            if j >= 2:
                                dve.wait_ge(s_lo_ready, hd * 4 + j - 1)
                            nc.vector.tensor_tensor(rt[:, j % 2, 0:w], at_ps[:, j, 0:w], decay[:, 0:w], ALU.mult).then_inc(s_decayed, 1)
                            if j:
                                s_low(j - 1)
                        s_low(TB - 1)
                dve.wait_ge(ro_root, hd + 1)
                nc.vector.reciprocal(rs[:, :], rs[:, :]).then_inc(ro_rs, 1)
                dve.wait_ge(ro_rs, hd + 1)
                for i in range(2):
                    slot = (parity + i) % 2
                    done(n + 4 + i)
                    dve.wait_ge(ro_silu, hd * 2 + i + 1)
                    for m in range(2):
                        e = 2 * i + m
                        if i:
                            dve.wait_ge(o_lo_ready, hd * 4 + 16 + m + 1)
                        nc.vector.tensor_tensor(rt[:, m, :], at_ps[:, e, :], rs[:, :], ALU.mult).then_inc(ro_norm, 1)
                        dve.wait_ge(ro_norm, hd * 12 + 8 + e + 1)
                        nc.vector.tensor_tensor(rt[:, m, :], rt[:, m, :], rt[:, 2 + m, :], ALU.mult).then_inc(ro_w, 1)
                    for m in range(2):
                        e = 2 * i + m
                        dve.wait_ge(o_hi_ready, hd * 4 + 16 + e + 1)
                        low(g_lo[:, g_at + e, :], rt[:, m, :], g_hi[:, g_at + e, :], o_lo_ready)
                    split(n + 6 + i, slot)
                dve.wait_ge(o_lo_ready, hd * 4 + 20)

            for i in range(2):
                head(i, i * 6 + N_RET1, N_RET1 % 2, i * 4)
            for j in range(4):
                n = N_RETP + j
                done(n)
                split(n + 2, n % 2)
            for i in range(2):
                head(i + 2, i * 6 + N_RET2, N_RET2 % 2, i * 4)
            for j in range(4):
                n = N_GATE + j
                done(n)
                split(n + 2, n % 2)
            dve.wait_ge(gate_ready, 10)
            for j in range(4):
                n = N_MERGE + j
                done(n)
                for m in range(2):
                    k = 2 * j + m
                    nc.vector.tensor_tensor(pr[:, k, :], ps[:, n % 2, m, :], pr[:, k, :], ALU.add).then_inc(merge_step, 1)
                    dve.wait_ge(merge_step, 3 * k + 1)
                    nc.vector.tensor_tensor(pr[:, k, :], pr[:, k, :], gates[:, k, :], ALU.mult).then_inc(merge_step, 1)
                    dve.wait_ge(merge_step, 3 * k + 2)
                    nc.vector.tensor_tensor(mg[:, k, :], pr[:, k, :], mg[:, k, :], ALU.add).then_inc(merge_step, 1)
                    dve.wait_ge(h_hi_ready, 8 * 5 + k + 1)
                    low(h_lo[:, k, :], mg[:, k, :], h_hi[:, k, :], h_lo_ready)
                split(n + 2, n % 2)
            dve.wait_ge(x_back, 16)
            update_steps(N_OUT, 4, "out", 16)
            gain(4)
            invert(4)
            norm(4)

            def ffn_pair(j, n, parity):
                done(n)
                split(n + 2, parity)
                done(n + 1)
                dve.wait_ge(ff_silu, j + 1)
                for m in range(2):
                    nc.vector.tensor_tensor(ft[:, 2 + m, :], ps[:, 1 - parity, m, :], ft[:, m, :], ALU.mult).then_inc(ff_prod, 1)
                for m in range(2):
                    dve.wait_ge(ff_hi, j * 2 + m + 1)
                    low(f_lo[:, j * 2 + m, :], ft[:, 2 + m, :], f_hi[:, j * 2 + m, :], ff_lo)
                split(n + 3, 1 - parity)
                dve.wait_ge(ff_lo, j * 2 + 2)

            ffn_pair(0, N_FFN, N_FFN % 2)
            with dve.Fori(1, 11) as i:
                ffn_pair(i, 2 * i + N_FFN, N_FFN % 2)
            r, part = GATE["ffn"]
            for j in range(4):
                for i in range(3):
                    n = N_FFN_OUT + 3 * j + i
                    done(n)
                    if i == 2:
                        for m in range(2):
                            k = 2 * j + m
                            c = mod_col(r, part, k)
                            nc.vector.scalar_tensor_tensor(x_sb[:, k, :], ps[:, j % 2, m, :], mods[:, c:c + 1], x_sb[:, k, :],
                                                           ALU.mult, ALU.add).then_inc(x_updated, 1)
                    if n + 2 < N_TILES:
                        split(n + 2, n % 2)
            invert(5)
            for k in range(KB):
                c = COLS["g_final"] + k
                nc.vector.scalar_tensor_tensor(x_sb[:, k, :], x_sb[:, k, :], cols[:, c:c + 1], rs[:, :], ALU.mult,
                                               ALU.mult).then_inc(t_ready, 1)


def _columns(v):
    return np.asarray(v).reshape(-1, P).T


def _weight_tiles(w):
    w = np.asarray(w)
    if w.shape[0] < D:
        w = np.concatenate([w, np.zeros((D - w.shape[0], w.shape[1]), w.dtype)])
    return list(w.reshape(KB, P, -1, TILE_W).transpose(2, 1, 0, 3))


def _shape_constants():
    f = np.float32
    const = np.zeros((P, N_CONST), f)
    const[:, C_MEAN:C_MEAN + P] = 1.0 / D
    const[:, C_EYE:C_EYE + P] = np.eye(P)
    s, t = np.arange(P)[:, None], np.arange(P)[None, :]
    const[:, C_NEG:C_NEG + P] = np.where(s >= t, f(NEG_BIG), f(0))
    const[:, C_NTRI:C_NTRI + P] = np.where(s >= t, f(-1), f(0))
    const[:, C_NONE:C_NONE + P] = -1
    tok = np.arange(T)
    for j in range(4):
        win = 2 << j
        cnt = (np.clip(tok + win - win // 2, 0, T) - np.clip(tok - win // 2, 0, T)).astype(f)
        const[:, C_POOL + 16 * j:C_POOL + 16 * j + 16] = (1 / cnt)[np.r_[0:8, T - 8:T]]
    ang_freq = f(10000.0) ** (-np.arange(0, 256, 2, dtype=f) / f(256))
    ang = ang_freq[:, None] * tok.astype(f)[None, :]
    rope = np.stack([np.cos(ang), np.sin(ang)], axis=1).astype(f)
    log_gamma = np.log(f(1) - f(2) ** (f(-5) - np.arange(RET_HEADS, dtype=f)))
    diff = (tok[None, :] - np.arange(P)[:, None]).astype(f)
    decay = np.where(diff >= 0, np.exp(np.maximum(diff, 0)[None] * log_gamma[:, None, None]), 0).astype(f)
    return const, rope, decay


def kernel(**inputs):
    import concourse.bacc as bacc
    from concourse.bass_utils import run_bass_kernel_spmd

    a = {k: np.asarray(v) for k, v in inputs.items()}

    def pick(groups, order):
        return [groups[g][j] for g, j in order]

    conv = _weight_tiles(a["cv_w_in"][0])
    w_in = a["w_in_2"][0]
    cuts = np.cumsum([0, 1024, 1024, 1024, 1024, 1024, 2048, 2048, 1024, 1024])
    parts = [_weight_tiles(w_in[:, p:q]) for p, q in zip(cuts[:-1], cuts[1:])]
    sq, sk, sv, rq, rk, rv, rg, b_sb, b_ret = parts
    proj_sb = _weight_tiles(a["w_proj_sb_2"][0])
    proj_ret = [_weight_tiles(a["w_proj_ret_2"][0][D * i:D * (i + 1)]) for i in range(2)]
    ffn = _weight_tiles(a["w_ffn_in_2"][0])
    ffn_out = [_weight_tiles(a["w_ffn_out_2"][0][D * i:D * (i + 1)]) for i in range(3)]
    tiles = []
    for j in range(4):
        tiles += [conv[j], conv[4 + j], conv[8 + j]]
    tiles += _weight_tiles(a["cv_w_out"][0])
    tiles += _weight_tiles(a["pl_w_in"][0])
    tiles += _weight_tiles(a["pl_w_grp"][0].reshape(D, TILE_W))
    tiles += _weight_tiles(a["pl_w_out"][0])
    for j in range(4):
        tiles += [sq[j], sk[j], sv[j]]
    tiles += b_sb + proj_sb
    for h in range(RET_HEADS):
        tiles += [rq[h], rk[h], rv[2 * h], rv[2 * h + 1], rg[2 * h], rg[2 * h + 1]]
        if h == 1:
            tiles += proj_ret[0]
    tiles += b_ret + proj_ret[1]
    tiles += _weight_tiles(a["w_out_2"][0])
    for j in range(11):
        tiles += [ffn[j], ffn[11 + j]]
    for j in range(4):
        tiles += [ffn_out[i][j] for i in range(3)]
    assert len(tiles) == N_TILES
    w_stream = np.stack(tiles)

    mod = np.concatenate([a["w_mod"][0], a["w_mod"][1], a["w_ada_2"][0]], axis=1)
    mod_stream = np.ascontiguousarray(mod.reshape(4, 2, P, N_MOD_GROUPS, MOD_G).transpose(3, 0, 2, 1, 4))
    vectors = {
        "norm_g": a["norm_g"], "b_mod": a["b_mod"], "b_ada": a["b_ada_2"], "cv_db": a["cv_db"], "cv_ln_g": a["cv_ln_g"],
        "cv_ln_b": a["cv_ln_b"], "pl_scale": a["pl_scale"], "g_norm1": a["g_norm1_2"], "g_norm2": a["g_norm2_2"],
        "g_final": a["g_final_2"], "b_branch": a["b_branch_2"], "c": a["c"], "c_2": a["c_2"],
        "dw": a["cv_dw"][0].reshape(CONV_W, KB, P).transpose(1, 0, 2),
    }
    cols = np.ascontiguousarray(np.concatenate([_columns(vectors[n]) for n in COLS], axis=1))
    assert cols.shape == (P, N_COLS)
    x_t = np.ascontiguousarray(a["x"][0].T.reshape(KB, P, T).transpose(1, 0, 2))
    const, rope, decay = _shape_constants()

    arrays = {"w_stream": w_stream, "mod_stream": mod_stream, "x_t": x_t, "cols_in": cols, "const_in": const,
              "rope_in": rope, "decay_in": decay}
    nc = bacc.Bacc("TRN2", target_bir_lowering=False, num_devices=1)
    aps = {k: nc.dram_tensor(k, v.shape, F32, kind="ExternalInput").ap() for k, v in arrays.items()}
    x_spill = nc.dram_tensor("x_spill", (P, KB, T), F32).ap()
    out = nc.dram_tensor("out_t", (P, KB, T), F32, kind="ExternalOutput").ap()
    build_program(nc, aps["w_stream"], aps["mod_stream"], aps["x_t"], aps["cols_in"], aps["const_in"],
                  aps["rope_in"], aps["decay_in"], x_spill, out)
    got = run_bass_kernel_spmd(nc, [arrays], core_ids=[0]).results[0]["out_t"]
    return np.ascontiguousarray(got.transpose(1, 0, 2).reshape(D, T).T)[None]
```

```python
from contextlib import ExitStack

import numpy as np

import concourse.bass as bass
from concourse import mybir

P = 128
D = 1024
T = 512
KB = D // P
TB = T // P
TILE_W = 256
CONV_W = 31
PAD = CONV_W // 2
PE_TAPS = (6, 6, 6, 11)
CONV_STEPS = [2 * (CONV_W - n + 1) for n in PE_TAPS]
CONV_BEFORE = [sum(CONV_STEPS[:j]) for j in range(5)]
POOL_PAD = 8
D_FF = 2816
FFB = D_FF // P
EPS = 1e-6
NEG_BIG = -1e30
SB_SCALE = 64 ** -0.5
RK_SCALE = 256 ** -0.5
RET_HEADS = 4

F32 = mybir.dt.float32
F32R = mybir.dt.float32r
ALU = mybir.AluOpType
ACT = mybir.ActivationFunctionType

N_CONV = 0
N_CONV_OUT = N_CONV + 12
N_POOL = N_CONV_OUT + 4
N_GRP = N_POOL + 8
N_POOL_OUT = N_GRP + 1
N_SB = N_POOL_OUT + 4
N_SB_GATE = N_SB + 12
N_SB_OUT = N_SB_GATE + 4
N_RET1 = N_SB_OUT + 4
N_RETP = N_RET1 + 12
N_RET2 = N_RETP + 4
N_GATE = N_RET2 + 12
N_MERGE = N_GATE + 4
N_OUT = N_MERGE + 4
N_FFN = N_OUT + 4
N_FFN_OUT = N_FFN + 22
N_TILES = N_FFN_OUT + 12

MOD_G = 512
MOD_ROUND = 3 * D
ROUND_GROUPS = MOD_ROUND // MOD_G
N_MOD_GROUPS = 4 * ROUND_GROUPS
DVE_GROUPS = 4

COLS = {}
_at = 0
for _name, _n in (("norm_g", 16), ("b_mod", 48), ("b_ada", 48), ("cv_db", 8), ("cv_ln_g", 8),
                  ("cv_ln_b", 8), ("pl_scale", 8), ("g_norm1", 8), ("g_norm2", 8), ("g_final", 8),
                  ("b_branch", 16), ("c", 8), ("c_2", 8), ("dw", 8 * CONV_W)):
    COLS[_name] = _at
    _at += _n
N_COLS = _at

C_MEAN, C_EYE, C_NEG, C_NTRI, C_NONE, C_POOL = (P * i for i in range(6))
N_CONST = C_POOL + 4 * 16


def z_off(j):
    return {0: 0, 1: 512, 3: 896, 2: 1024}[j]


Z_W = 1280


def build_program(nc, w_stream, mod_stream, x_in, cols_in, const_in, rope_in, decay_in, x_spill, out):
    with ExitStack() as ctx:
        base = 16512

        def place(name, at, n, dt):
            assert at + 4 * n <= 229344 - base, (name, at + 4 * n)
            return nc.alloc_sbuf_tensor_at(name, [P, n], dt, offset=base + at)

        def blocks(t, w):
            return t[:, :].rearrange("p (b w) -> p b w", w=w)

        def sem(name):
            return ctx.enter_context(nc.semaphore(name))

        K = 1024
        w_raw = place("w_raw", 0, 4096, F32)[:, :].rearrange("p (s k c) -> p s k c", s=2, k=KB)
        w_hi = place("w_hi", 16 * K, 4096, F32R)[:, :].rearrange("p (s k c) -> p s k c", s=2, k=KB)
        w_lo = place("w_lo", 32 * K, 4096, F32R)[:, :].rearrange("p (s k c) -> p s k c", s=2, k=KB)
        h_hi = blocks(place("h_hi", 48 * K, 4096, F32R), T)
        h_lo = blocks(place("h_lo", 64 * K, 4096, F32R), T)
        x_flat = place("x_sb", 80 * K, 4096, F32)
        x_sb = blocks(x_flat, T)
        rs = place("rs", 96 * K, 512, F32)
        cols = place("cols", 98 * K, N_COLS, F32)
        at = (98 * K + 4 * N_COLS + 31) // 32 * 32
        mods = place("mods", at, 96, F32)
        gp = place("gp", at + 4 * 96, 8, F32)
        csil = place("csil", at + 4 * 104, 16, F32)
        at = at + 4 * 120
        mean_m = place("mean_m", at, P, F32)
        pool_edge = place("pool_edge", at + 512, 64, F32)
        eye_r = place("eye_r", at + 768, P, F32R)
        neg_r = place("neg_r", at + 1280, P, F32R)
        ntri_r = place("ntri_r", at + 1792, P, F32R)
        none_r = place("none_r", at + 2304, P, F32R)
        ones_c = place("ones_c", at + 2816, 2, F32)
        eps_c = place("eps_c", at + 2848, 1, F32)
        var = at + 2880

        g_hi = blocks(place("g_hi", var, 4096, F32R), T)
        g_lo = blocks(place("g_lo", var + 16 * K, 4096, F32R), T)
        v = var + 32 * K
        mod_acc = place("mod_acc", v, MOD_ROUND, F32)
        mod_chunk = place("mod_chunk", v + 12 * K, 2048, F32)[:, :].rearrange("p (s k c) -> p s k c", s=2, k=2)
        v1 = v + 20 * K
        y_flat = place("y_sb", v1, 4096, F32)
        y_sb = blocks(y_flat, T)
        gs_flat = place("gs_sb", v1 + 16 * K, 4096, F32)
        gs_sb = blocks(gs_flat, T)
        first_chunk = [t[:, :].rearrange("p (s k c) -> p s k c", s=4, k=2) for t in (y_flat, gs_flat)]
        sa = blocks(place("sa", v1 + 32 * K, 2048, F32), T)
        sq = blocks(place("sq", v1 + 40 * K, 2048, F32), T)
        ypad = place("ypad", var, 2 * (T + 2 * PAD), F32)[:, :].rearrange("p (m t) -> p m t", m=2)
        c_stage = place("c_stage", var + 8 * K, N_CONST, F32)
        diag_at = (0, 2 * max(PE_TAPS[0], PE_TAPS[2]))
        assert diag_at[1] + 2 * max(PE_TAPS[1], PE_TAPS[3]) <= 40
        diag = blocks(place("diag", var + 12 * K, 40 * P, F32), P)
        PW = T + 2 * POOL_PAD
        vpad = place("vpad", v1, 2 * PW, F32)[:, :].rearrange("p (m t) -> p m t", m=2)
        pool_a = place("pool_a", v1 + 8 * PW, 2 * PW, F32)[:, :].rearrange("p (m t) -> p m t", m=2)
        pool_b = place("pool_b", v1 + 16 * PW, 2 * PW, F32)[:, :].rearrange("p (m t) -> p m t", m=2)

        names = ("q_hi", "q_lo", "k_hi", "k_lo", "v_hi", "v_lo")
        qkv_at = ([v1 + 4 * K * i for i in range(6)], [v1 + 44 * K, v1 + 48 * K, 90 * K, 94 * K, v, v + 4 * K])
        sbq_hi, sbq_lo, sbk_hi, sbk_lo, sbv_hi, sbv_lo = (
            [blocks(place(f"sb{name}_{s}", qkv_at[s][i], 1024, F32R), TILE_W if i >= 4 else T) for s in range(2)]
            for i, name in enumerate(names))
        att_hi = blocks(place("att_hi", v1 + 24 * K, 2 * Z_W, F32R), Z_W)
        att_lo = blocks(place("att_lo", v1 + 34 * K, 2 * Z_W, F32R), Z_W)
        z_tmp = x_flat[:, 0:2 * Z_W].rearrange("p (s z) -> p s z", s=2)
        mg = x_sb
        sb_gates = blocks(place("sb_gates", v1, 4096, F32), T)
        pr = blocks(place("pr", v, 4096, F32), T)
        rq_hi, rq_lo, rk_hi, rk_lo = (
            blocks(place(f"r{n}", v + (16 + 4 * i) * K, 1024, F32R), T) for i, n in enumerate(names[:4]))
        rv_hi, rv_lo = (blocks(place(f"r{n}", v + (32 + 8 * i) * K, 2048, F32R), T) for i, n in enumerate(names[4:]))
        s_hi, s_lo = (place(f"s_{n}", v + 48 * K + 5 * K * i, Z_W, F32R) for i, n in enumerate(("hi", "lo")))
        rope = blocks(place("rope", v + 58 * K, 1024, F32), T)
        decay = place("decay", v + 62 * K, T, F32)
        rt = blocks(place("rt", v + 64 * K, 2048, F32), T)
        gates = blocks(place("gates", v + 16 * K, 4096, F32), T)
        nt = blocks(place("nt", v + 48 * K, 2048, F32), T)
        nsq = blocks(place("nsq", v + 56 * K, 2048, F32), T)
        f_hi = blocks(place("f_hi", var, FFB * T, F32R), T)
        f_lo = blocks(place("f_lo", var + 2 * K * FFB, FFB * T, F32R), T)
        ft = blocks(place("ft", var + 4 * K * FFB, 2048, F32), T)
        fsq = blocks(place("fsq", var + 4 * K * FFB + 8 * K, 2048, F32), T)

        ps = ctx.enter_context(nc.psum_tensor("ps", [P, 2, 2, T], F32))
        at_ps = ctx.enter_context(nc.psum_tensor("at_ps", [P, 4, T], F32))
        ps_tok = ps[:, :, :, :].rearrange("p s m (h c) -> p s (m h) c", c=TILE_W)
        ps_flat = ps[:, :, :, :].rearrange("p s m t -> p (s m t)")
        at_flat = at_ps[:, :, :].rearrange("p b t -> p (b t)")
        z_ps = (at_flat[:, 0:3 * T], ps_flat[:, T:4 * T])
        o_ps = at_flat[:, 3 * T:4 * T]

        cols_in_s, x_in_s, const_in_s = sem("cols_loaded"), sem("x_loaded"), sem("consts_loaded")
        w_landed = [sem("w_landed_even"), sem("w_landed_odd")]
        first_in = [sem(f"first_chunk_loaded_{i}") for i in range(8)]
        chunk_in = [sem("mod_chunk_loaded_even"), sem("mod_chunk_loaded_odd")]
        w_hi_done, w_lo_done = sem("w_hi_done"), sem("w_lo_done")
        tile_done = sem("tile_done")
        half_ready = sem("half_ready")
        ones_done = sem("ones_done")
        csil_done, consts_done, pads_done = sem("csil_done"), sem("consts_done"), sem("pads_done")
        first_mod = sem("first_mod")
        mod_step = sem("mod_step")
        mod_summed, mods_ready, gp_ready = sem("mod_summed"), sem("mods_ready"), sem("gp_ready")
        x_updated = sem("x_updated")
        sq_ready, sq_used, sq_added, root_ready, rs_ready = sem("sq_ready"), sem("sq_used"), sem("sq_added"), sem("root_ready"), sem("rs_ready")
        t_ready, h_hi_ready, h_lo_ready = sem("t_ready"), sem("h_hi_ready"), sem("h_lo_ready")
        a_copied, sig_ready, y_ready, conv_step = sem("a_copied"), sem("sig_ready"), sem("y_ready"), sem("conv_step")
        diag_ready, pe_taps_done = sem("diag_ready"), sem("pe_taps_done")
        conv_summed, centred = sem("conv_summed"), sem("centred")
        ln_t, ln_silu, ln_y = sem("ln_t"), sem("ln_silu"), sem("ln_y")
        gs_ready = sem("gs_ready")
        v_copied, pool_step, pooled = sem("v_copied"), sem("pool_step"), sem("pooled")
        g_hi_ready, g_lo_ready = sem("g_hi_ready"), sem("g_lo_ready")
        grp_done, grp_y = sem("grp_done"), sem("grp_y")
        x_spilled, x_back = sem("x_spilled"), sem("x_back")
        block_done = sem("block_done")
        qkv_hi, qkv_lo = sem("qkv_hi"), sem("qkv_lo")
        gate_raw = sem("gate_raw")
        z_done, stick_step, stick_ln = sem("z_done"), sem("stick_step"), sem("stick_ln")
        sp_step, sp_split = sem("sp_step"), sem("sp_split")
        after_done, a_exp, a_step, a_split = sem("after_done"), sem("a_exp"), sem("a_step"), sem("a_split")
        o_done, o_hi_ready, o_lo_ready = sem("o_done"), sem("o_hi_ready"), sem("o_lo_ready")
        gate_ready, mg_ready = sem("gate_ready"), sem("mg_ready")
        rope_in_s, decay_in_s = sem("rope_loaded"), sem("decay_loaded")
        rot_step, rot_hi, rot_lo = sem("rot_step"), sem("rot_hi"), sem("rot_lo")
        rv_hi_ready, rv_lo_ready = sem("rv_hi_ready"), sem("rv_lo_ready")
        s_done, s_decayed, s_hi_ready, s_lo_ready = sem("s_done"), sem("s_decayed"), sem("s_hi_ready"), sem("s_lo_ready")
        ro_done, ro_sq, ro_added, ro_stat, ro_root, ro_rs = sem("ro_done"), sem("ro_sq"), sem("ro_added"), sem("ro_stat"), sem("ro_root"), sem("ro_rs")
        ro_norm, ro_silu, ro_w = sem("ro_norm"), sem("ro_silu"), sem("ro_w")
        pr_ready, merge_step = sem("pr_ready"), sem("merge_step")
        ff_silu, ff_prod, ff_hi, ff_lo = sem("ff_silu"), sem("ff_prod"), sem("ff_hi"), sem("ff_lo")
        out_stored = sem("out_stored")

        FFN_BANK = [(N_FFN + j) % 2 for j in range(4)]
        SQ_RING = 4
        STAT_BANK = (0, 1, 0, 0, 0, 0)

        def sq_buf(u):
            return {0: sq, 1: sq, 2: sq, 3: sq, 4: nsq, 5: fsq}[u]

        def t_buf(u):
            return {0: sa, 1: sa, 2: sa, 3: sa, 4: nt, 5: ft}[u]

        def x_count(u, k):
            return 8 * {2: 0, 3: 1, 4: 2, 5: 3}[u] + k + 1

        def mod_col(r, part, k):
            return 24 * r + 8 * part + k

        SHIFT = {0: (0, 0), 2: (1, 0), 3: (2, 0), 4: (3, 0)}
        GAIN = {0: "norm_g", 2: "norm_g", 3: "g_norm1", 4: "g_norm2"}
        GAIN_AT = {0: 0, 2: 8, 3: 0, 4: 0}
        FILL = {0: 0, 1: 1, 2: 2, 3: 4, 4: 6}
        GATE = {"conv": (0, 2), "pool": (1, 2), "out": (2, 2), "ffn": (3, 2)}

        block = ctx.enter_context(nc.Block())

        @block.sync
        def _(sp):
            sp.dma_start(cols[:, :], cols_in).then_inc(cols_in_s, 16)
            sp.dma_start(c_stage[:, :], const_in).then_inc(const_in_s, 16)
            sp.dma_start(x_sb, x_in).then_inc(x_in_s, 16)
            sp.wait_ge(first_in[2], 16)
            for n in range(2):
                sp.dma_start(w_raw[:, n], w_stream[n]).then_inc(w_landed[n], 16)
            for i in range(8):
                sp.wait_ge(first_mod, 4 * (i // 2) + 3 + i % 2)
                sp.dma_start(first_chunk[i // 4][:, i % 4], mod_stream[2 * (i % 2) + 1, i // 2]).then_inc(first_in[i], 16)

            def load(n, slot):
                sp.wait_ge(w_lo_done, n - 1)
                sp.dma_start(w_raw[:, slot], w_stream[n]).then_inc(w_landed[slot], 16)

            with sp.Fori(1, N_TILES // 2) as i:
                load(2 * i, 0)
                load(2 * i + 1, 1)
            load(N_TILES - 1, (N_TILES - 1) % 2)

        @block.gpsimd
        def _(pool):
            nc.gpsimd.memset(ones_c[:, :], 1.0).then_inc(ones_done, 1)
            pool.wait_ge(csil_done, 2)
            pool.wait_ge(first_mod, 8)

            chunks = [(r, i, q) for r in range(4) for i in range(0 if r else DVE_GROUPS, ROUND_GROUPS) for q in range(4)]

            def steps_after(c):
                return 15 * (c // 4) + 4 * (c % 4) + 3

            def load(c):
                r, i, q = chunks[c]
                if c >= 2:
                    pool.wait_ge(mod_step, steps_after(c - 2))
                pool.dma_start(mod_chunk[:, c % 2], mod_stream[i + ROUND_GROUPS * r, q]).then_inc(chunk_in[c % 2], 16)

            load(0)
            for c, (r, i, q) in enumerate(chunks):
                if c + 1 < len(chunks):
                    load(c + 1)
                pool.wait_ge(chunk_in[c % 2], 16 * (c // 2) + 16)
                acc = mod_acc[:, i * MOD_G:(i + 1) * MOD_G]
                if r and q == 0:
                    pool.wait_ge(mod_summed, 2 if r == 1 and i < DVE_GROUPS else r + 2)
                for b in range(2):
                    kb = 2 * q + b
                    col = kb + (0 if r < 2 else 8)
                    part, scalar = mod_chunk[:, c % 2, b], csil[:, col:col + 1]
                    if kb == 0:
                        nc.gpsimd.tensor_scalar(acc, part, scalar, 1.0, ALU.mult, ALU.mult).then_inc(mod_step, 1)
                    else:
                        nc.gpsimd.tensor_scalar(part, part, scalar, 1.0, ALU.mult, ALU.mult).then_inc(mod_step, 1)
                        pool.wait_ge(mod_step, steps_after(c) - 2 * (1 - b) - 1)
                        nc.gpsimd.tensor_tensor(acc, acc, part, ALU.add).then_inc(mod_step, 1)

        def mod_steps(r):
            return 15 * (ROUND_GROUPS * (r + 1) - DVE_GROUPS)

        @block.tensor
        def _(pe):
            def three(out_ap, a_hi, a_lo, b_hi, b_lo, start, stop, inc=None):
                nc.tensor.matmul(out_ap, a_hi, b_hi, start=start, stop=False, skip_group_check=True)
                nc.tensor.matmul(out_ap, a_hi, b_lo, start=False, stop=False, skip_group_check=True)
                last = nc.tensor.matmul(out_ap, a_lo, b_hi, start=False, stop=stop, skip_group_check=True)
                if inc is not None:
                    last.then_inc(inc, 1)

            def split_ready(n):
                pe.wait_ge(w_hi_done, n + 1)
                pe.wait_ge(w_lo_done, n + 1)

            def tile(n, slot, src_hi, src_lo, before_block=None, ks=range(KB), src0=0, first=True, last=True, finish=True,
                     bank=None, order=(0, 1), between=None, half_done=None):
                split_ready(n)
                bank = slot if bank is None else bank
                if before_block is None:
                    steps = [(m, k) for m in order for k in ks]
                else:
                    steps = [(m, k) for k in ks for m in order]
                for m, k in steps:
                    if before_block is not None and m == order[0]:
                        before_block(k)
                    if between is not None and (m, k) == (order[1], ks[0]):
                        between()
                    c = slice(P * m, P * m + P)
                    inc = (tile_done if m == order[1] else half_done) if finish and k == ks[-1] else None
                    three(ps[:, bank, m, :], w_hi[:, slot, k, c], w_lo[:, slot, k, c],
                          src_hi[:, src0 + k, :], src_lo[:, src0 + k, :],
                          first and k == ks[0], last and k == ks[-1], inc)

            def tile_tokens(n, slot):
                split_ready(n)
                for tb in range(TB):
                    for k in range(KB):
                        c = slice(P * tb, P * tb + P)
                        three(ps_tok[:, slot, tb, :], h_hi[:, k, c], h_lo[:, k, c],
                              w_hi[:, slot, k, :], w_lo[:, slot, k, :], k == 0, k == KB - 1,
                              tile_done if tb == TB - 1 and k == KB - 1 else None)

            def h_block(fill):
                return lambda k: pe.wait_ge(h_lo_ready, 8 * fill + k + 1)

            def last_stats(u):
                pe.wait_ge(sq_added, 5 * (u - 1))
                pe.wait_ge(root_ready, u)
                nc.tensor.matmul(at_ps[:, 0, :], mean_m[:, :], rs[:, :], start=True, stop=False, skip_group_check=True)
                for k in (6, 7):
                    pe.wait_ge(sq_ready, 8 * u + k + 1)
                    nc.tensor.matmul(at_ps[:, 0, :], mean_m[:, :], sq_buf(u)[:, k % SQ_RING, :], start=False,
                                     stop=(k == 7), skip_group_check=True).then_inc(sq_used, 1)

            def norm_stat(u, k):
                pe.wait_ge(sq_ready, 8 * u + k + 1)
                if u and k == 0:
                    pe.wait_ge(root_ready, u)
                nc.tensor.matmul(at_ps[:, STAT_BANK[u], :], mean_m[:, :], sq_buf(u)[:, k % SQ_RING, :], start=(k == 0),
                                 stop=(k == KB - 1), skip_group_check=True).then_inc(sq_used, 1)

            def mod_sum(bs, ready, count):
                pe.wait_ge(ready, count)
                for i, b in enumerate(bs):
                    last = nc.tensor.matmul(at_ps[:, 3, i:i + 1], mod_acc[:, P * b:P * (b + 1)],
                                            ones_c[:, 0:1], start=True, stop=True, skip_group_check=True)
                last.then_inc(mod_summed, 1)

            def update_tiles(n0, fill, u, src_hi=h_hi, src_lo=h_lo, ready=None):
                for j in range(4):
                    tile(n0 + j, (n0 + j) % 2, src_hi, src_lo, ready if j == 0 else None,
                         half_done=half_ready if j == 3 else None)
                last_stats(u)

            pe.wait_ge(consts_done, 1)
            for k in range(KB):
                norm_stat(0, k)
            pe.wait_ge(ones_done, 1)
            def first_sums(half):
                mod_sum([4 * half + i + 8 * part for part in range(2) for i in range(4)], first_mod, 2 * KB * (half + 1))

            def first_tile(n, half):
                tile(N_CONV + n, n, h_hi, h_lo, h_block(0), ks=range(4 * half, 4 * half + 4), first=(half == 0),
                     last=(half == 1), finish=(half == 1))

            first_sums(0)
            first_tile(0, 0)
            first_tile(1, 0)
            pe.wait_ge(mods_ready, 1)
            first_sums(1)
            first_tile(0, 1)
            first_tile(1, 1)

            def conv_taps(j):
                pe.wait_ge(y_ready, 2 * j + 2)
                pe.wait_ge(diag_ready, 2 * j + 2)
                if j:
                    pe.wait_ge(conv_step, CONV_BEFORE[j])
                for m in range(2):
                    for i in range(PE_TAPS[j]):
                        t = CONV_W - PE_TAPS[j] + i
                        last = nc.tensor.matmul(at_ps[:, 1 + m, :], diag[:, diag_at[j % 2] + PE_TAPS[j] * m + i, :],
                                                ypad[:, m, t:t + T], start=(i == 0), stop=(i == PE_TAPS[j] - 1),
                                                skip_group_check=True)
                    last.then_inc(pe_taps_done, 1)

            for j in range(4):
                for i in range(3):
                    n = N_CONV + 3 * j + i
                    if n >= N_CONV + 2:
                        tile(n, n % 2, h_hi, h_lo)
                conv_taps(j)
                if j == 0:
                    pe.wait_ge(mods_ready, 2)
                    mod_sum(range(16, 24), mod_step, mod_steps(0))
            for k in range(KB):
                pe.wait_ge(conv_step, CONV_BEFORE[k // 2 + 1] - 1 + k % 2)
                nc.tensor.matmul(at_ps[:, 0, :], mean_m[:, :], y_sb[:, k, :], start=(k == 0), stop=(k == KB - 1),
                                 skip_group_check=True).then_inc(conv_summed, 1)
            for k in range(KB):
                norm_stat(1, k)
            pe.wait_ge(mods_ready, 3)
            mod_sum(range(24), mod_step, mod_steps(1))
            update_tiles(N_CONV_OUT, 1, 2, ready=h_block(1))

            tile(N_POOL, 0, h_hi, h_lo, h_block(2))
            tile(N_POOL + 1, 1, h_hi, h_lo)
            tile(N_POOL + 2, 0, h_hi, h_lo)
            tile(N_POOL + 3, 1, h_hi, h_lo)
            with pe.Fori(2, 4) as i:
                tile(2 * i + N_POOL, 0, h_hi, h_lo)
                tile(2 * i + N_POOL + 1, 1, h_hi, h_lo)
            pe.wait_ge(mods_ready, 4)
            mod_sum(range(24), mod_step, mod_steps(2))
            pe.wait_ge(mods_ready, 5)
            split_ready(N_GRP)
            for g in range(4):
                pe.wait_ge(g_lo_ready, 2 * g + 2)
                if g == 0:
                    pe.wait_ge(w_hi_done, N_GRP + 2)
                for m in range(2):
                    out_ap = (ps[:, 1, m, :], at_ps[:, m, :], at_ps[:, 2 + m, :], ps[:, 0, m, :])[g]
                    for k in range(2):
                        c = slice(P * m, P * m + P)
                        three(out_ap, w_hi[:, 0, 2 * g + k, c], w_lo[:, 0, 2 * g + k, c], g_hi[:, 2 * g + k, :],
                              g_lo[:, 2 * g + k, :], k == 0, k == 1,
                              (tile_done if g == 3 and m == 1 else grp_done) if k == 1 else None)
            update_tiles(N_POOL_OUT, 3, 3, ready=h_block(3))

            def scores(hd):
                rows, zp = slice(64 * (hd % 2), 64 * (hd % 2) + 64), z_ps[hd % 2]
                blk, s = hd % 4 // 2, hd // 4 % 2
                for j in range(TB):
                    w = T - P * j
                    z = zp[:, z_off(j):z_off(j) + w]
                    three(z, sbk_hi[s][rows, blk, P * j:P * j + P], sbk_lo[s][rows, blk, P * j:P * j + P],
                          sbq_hi[s][rows, blk, P * j:T], sbq_lo[s][rows, blk, P * j:T], j < 3, False)
                    last = nc.tensor.matmul(z[:, 0:P], eye_r[:, :], neg_r[:, :], start=False, stop=False,
                                            skip_group_check=True)
                last.then_inc(z_done, 1)

            def subtract_after(hd):
                pe.wait_ge(sp_split, hd + 1)
                zp = z_ps[hd % 2]
                for part in (att_hi, att_lo):
                    for j in range(TB):
                        for j2 in range(j, TB):
                            w = T - P * j2
                            o = z_off(j) + P * (j2 - j)
                            last = nc.tensor.matmul(zp[:, o:o + w], (ntri_r if j2 == j else none_r)[:, :],
                                                    part[:, hd % 2, z_off(j2):z_off(j2) + w],
                                                    start=False, stop=False, skip_group_check=True)
                last.then_inc(after_done, 1)

            def attend(hd):
                pe.wait_ge(a_split, hd + 1)
                if hd:
                    pe.wait_ge(o_lo_ready, hd)
                if hd == 0:
                    pe.wait_ge(mods_ready, 6)
                s = hd // 4 % 2
                c = slice(P * (hd % 4 // 2), P * (hd % 4 // 2) + P)
                for j in range(TB):
                    w = T - P * j
                    three(o_ps[:, P * j:T], sbv_hi[s][:, j, c], sbv_lo[s][:, j, c],
                          att_hi[:, hd % 2, z_off(j):z_off(j) + w], att_lo[:, hd % 2, z_off(j):z_off(j) + w],
                          j == 0, j == TB - 1, o_done if j == TB - 1 else None)

            def half_tile(n, m, bank):
                if m == 0:
                    split_ready(n)
                for k in range(KB):
                    c = slice(P * m, P * m + P)
                    three(ps_flat[:, T * bank:T * bank + T], w_hi[:, n % 2, k, c], w_lo[:, n % 2, k, c],
                          h_hi[:, k, :], h_lo[:, k, :], k == 0, k == KB - 1,
                          (tile_done if m else block_done) if k == KB - 1 else None)

            def quarter_tokens(n, tb, bank):
                if tb == 0:
                    split_ready(n)
                o = T * bank + TILE_W * (tb % 2)
                inc = {0: None, 1: block_done, 2: None, 3: tile_done}[tb]
                for k in range(KB):
                    c = slice(P * tb, P * tb + P)
                    three(ps_flat[:, o:o + TILE_W], h_hi[:, k, c], h_lo[:, k, c], w_hi[:, n % 2, k, :], w_lo[:, n % 2, k, :],
                          k == 0, k == KB - 1, inc if k == KB - 1 else None)

            def qkv_block(grp, b, bank, behind):
                n = N_SB + 3 * grp
                if 6 * grp + b - behind > 0:
                    pe.wait_ge(qkv_lo, 6 * grp + b - behind)
                half_tile(n + b // 2, b % 2, bank)

            def v_block(grp, tb, bank, behind):
                b = 4 + tb // 2
                if tb % 2 == 0:
                    pe.wait_ge(qkv_lo, 6 * grp + b - behind)
                quarter_tokens(N_SB + 3 * grp + 2, tb, bank)

            def gate_block(b):
                if b:
                    pe.wait_ge(gate_raw, b)
                else:
                    pe.wait_ge(qkv_lo, 24)
                half_tile(N_SB_GATE + b // 2, b % 2, 0)

            tile(N_SB, N_SB % 2, h_hi, h_lo, h_block(4), bank=0, half_done=block_done)
            for b in (2, 3):
                qkv_block(0, b, b, 4)
            for tb in range(TB):
                v_block(0, tb, tb // 2, 4)
            for grp in range(4):
                hd = 4 * grp

                def block(b):
                    if grp < 3:
                        qkv_block(grp + 1, b, 0, 0)
                    else:
                        gate_block(b)

                pe.wait_ge(qkv_lo, 6 * grp + 4)
                scores(hd)
                block(0)
                if grp == 0:
                    pe.wait_ge(qkv_lo, 6)
                scores(hd + 1)
                block(1)
                subtract_after(hd)
                block(2)
                subtract_after(hd + 1)
                pe.wait_ge(qkv_lo, 6 * grp + 6)
                if grp == 0:
                    mod_sum(range(24), mod_step, mod_steps(3))
                attend(hd)
                block(3)
                scores(hd + 2)
                attend(hd + 1)
                scores(hd + 3)
                if grp < 3:
                    v_block(grp + 1, 0, 0, 0)
                    v_block(grp + 1, 1, 0, 0)
                    subtract_after(hd + 2)
                    v_block(grp + 1, 2, 0, 0)
                    subtract_after(hd + 3)
                    attend(hd + 2)
                    v_block(grp + 1, 3, 0, 0)
                    attend(hd + 3)
                else:
                    gate_block(4)
                    subtract_after(hd + 2)
                    gate_block(5)
                    subtract_after(hd + 3)
                    attend(hd + 2)
                    gate_block(6)
                    attend(hd + 3)
                    gate_block(7)

            pe.wait_ge(o_lo_ready, 16)
            pe.wait_ge(gate_raw, 8)
            with pe.Fori(0, 2) as i:
                tile(2 * i + N_SB_OUT, N_SB_OUT % 2, g_hi, g_lo)
                tile(2 * i + N_SB_OUT + 1, (N_SB_OUT + 1) % 2, g_hi, g_lo)

            def head(hd, n, parity):
                tile(n, parity, h_hi, h_lo)
                tile(n + 1, 1 - parity, h_hi, h_lo)
                tile_tokens(n + 2, parity)
                pe.wait_ge(rot_lo, hd * 4 + 4)
                for j in range(TB):
                    w = T - P * j
                    for c in range(2):
                        three(at_ps[:, j, 0:w], rk_hi[:, c, P * j:P * j + P], rk_lo[:, c, P * j:P * j + P],
                              rq_hi[:, c, P * j:T], rq_lo[:, c, P * j:T], c == 0, c == 1, s_done if c == 1 else None)
                tile_tokens(n + 3, 1 - parity)
                pe.wait_ge(s_lo_ready, hd * 4 + 4)
                for e in range(4):
                    if e % 2 == 0:
                        pe.wait_ge(rv_lo_ready, hd * 2 + e // 2 + 1)
                    for j in range(TB):
                        w = T - P * j
                        three(at_ps[:, e, P * j:T], rv_hi[:, j, P * e:P * e + P], rv_lo[:, j, P * e:P * e + P],
                              s_hi[:, z_off(j):z_off(j) + w], s_lo[:, z_off(j):z_off(j) + w],
                              j == 0, j == TB - 1, ro_done if j == TB - 1 else None)
                tile(n + 4, parity, h_hi, h_lo)
                pe.wait_ge(ro_added, hd * 3 + 3)
                nc.tensor.matmul(ps[:, 1 - parity, 0, :], mean_m[:, :], rs[:, :], start=True, stop=True,
                                 skip_group_check=True).then_inc(ro_stat, 1)
                tile(n + 5, 1 - parity, h_hi, h_lo, order=(1, 0), between=lambda: pe.wait_ge(ro_root, hd + 1))

            with pe.Fori(0, 2) as i:
                head(i, i * 6 + N_RET1, N_RET1 % 2)
            for j in range(4):
                tile(N_RETP + j, (N_RETP + j) % 2, g_hi, g_lo, None if j else lambda k: pe.wait_ge(o_lo_ready, 16 + k + 1))
            with pe.Fori(0, 2) as i:
                head(i + 2, i * 6 + N_RET2, N_RET2 % 2)
            with pe.Fori(0, 2) as i:
                tile(2 * i + N_GATE, N_GATE % 2, h_hi, h_lo)
                tile(2 * i + N_GATE + 1, (N_GATE + 1) % 2, h_hi, h_lo)
            pe.wait_ge(o_lo_ready, 16 + 16)
            with pe.Fori(0, 2) as i:
                tile(2 * i + N_MERGE, N_MERGE % 2, g_hi, g_lo)
                tile(2 * i + N_MERGE + 1, (N_MERGE + 1) % 2, g_hi, g_lo)
            update_tiles(N_OUT, 5, 4, ready=h_block(5))

            tile(N_FFN, N_FFN % 2, h_hi, h_lo, h_block(6))
            tile(N_FFN + 1, (N_FFN + 1) % 2, h_hi, h_lo)
            with pe.Fori(1, 11) as i:
                tile(2 * i + N_FFN, N_FFN % 2, h_hi, h_lo)
                tile(2 * i + N_FFN + 1, (N_FFN + 1) % 2, h_hi, h_lo)

            def ffn_out(n, parity, bank):
                pe.wait_ge(ff_lo, 8)
                tile(n, parity, f_hi, f_lo, first=True, last=False, bank=bank)
                pe.wait_ge(ff_lo, 16)
                tile(n + 1, 1 - parity, f_hi, f_lo, src0=8, first=False, last=False, bank=bank)
                pe.wait_ge(ff_lo, FFB)
                tile(n + 2, parity, f_hi, f_lo, half_done=half_ready if n + 2 == N_TILES - 1 else None, ks=range(FFB - 16), src0=16, first=False, last=True, bank=bank)

            for j in range(4):
                n = N_FFN_OUT + 3 * j
                ffn_out(n, n % 2, FFN_BANK[j])
            last_stats(5)

        @block.scalar
        def _(act):
            def split(n, slot):
                act.wait_ge(w_landed[slot], (n - slot) * 8 + 16)
                nc.scalar.activation(w_hi[:, slot], w_raw[:, slot], ACT.Copy).then_inc(w_hi_done, 1)

            def done(n):
                act.wait_ge(tile_done, n + 1)

            def squares(u, k, src):
                if u >= 2 and k >= SQ_RING:
                    act.wait_ge(sq_added, 5 * (u - 2) + max(k - SQ_RING, 1))
                elif u >= 2 and k < 2:
                    act.wait_ge(sq_used, 16 + 2 * (u - 2))
                elif u < 2 and 8 * u + k >= SQ_RING:
                    act.wait_ge(sq_used, 8 * u + k - SQ_RING + 1)
                nc.scalar.activation(sq_buf(u)[:, k % SQ_RING, :], src, ACT.Square).then_inc(sq_ready, 1)

            def log_table():
                nc.scalar.preload_act_table_set("natural_log_exp_and_others")

            def inverse_root(u):
                log_table()
                act.wait_ge(sq_used, 8 * u + 8 if u < 2 else 16 + 2 * (u - 1))
                nc.scalar.activation(rs[:, :], at_ps[:, STAT_BANK[u], :], ACT.Ln, bias=eps_c[:, 0:1]).then_inc(root_ready, 1)
                act.wait_ge(root_ready, u + 1)
                nc.scalar.activation(rs[:, :], rs[:, :], ACT.Exp, scale=-0.5).then_inc(rs_ready, 1)

            def norm_hi(u, n_free, ks=range(KB)):
                r, part = SHIFT[u]
                idx = {0: 0, 2: 1, 3: 2, 4: 3}[u]
                if n_free:
                    done(n_free - 1)
                for k in ks:
                    act.wait_ge(t_ready, 8 * idx + k + 1)
                    c = mod_col(r, part, k)
                    nc.scalar.activation(h_hi[:, k, :], t_buf(u)[:, k % 4, :], ACT.Identity,
                                         bias=mods[:, c:c + 1]).then_inc(h_hi_ready, 1)

            def update_steps(n0, u):
                for j in range(4):
                    if j < 3:
                        done(n0 + j)
                        split(n0 + j + 2, (n0 + j) % 2)
                    for m in range(2):
                        act.wait_ge(x_updated, x_count(u, 2 * j + m))
                        squares(u, 2 * j + m, x_sb[:, 2 * j + m, :])
                inverse_root(u)

            for i in range(8):
                act.dma_start(first_chunk[i // 4][:, i % 4], mod_stream[2 * (i % 2), i // 2]).then_inc(first_in[i], 16)
            act.wait_ge(cols_in_s, 16)
            for i, name in enumerate(("c", "c_2")):
                nc.scalar.activation(csil[:, 8 * i:8 * i + 8], cols[:, COLS[name]:COLS[name] + 8], ACT.Silu).then_inc(csil_done, 1)
            act.wait_ge(x_in_s, 16)
            act.wait_ge(pads_done, 1)
            for k in range(KB):
                squares(0, k, x_sb[:, k, :])
            inverse_root(0)
            split(0, 0)
            norm_hi(0, 0, range(4))
            split(1, 1)
            norm_hi(0, 0, range(4, KB))

            for j in range(4):
                n = N_CONV + 3 * j
                done(n)
                if j:
                    act.wait_ge(y_ready, 2 * j)
                else:
                    act.wait_ge(h_lo_ready, 8)
                nc.scalar.activation(sa[:, 0:2, :], ps[:, n % 2], ACT.Copy).then_inc(a_copied, 1)
                split(n + 2, n % 2)
                done(n + 1)
                nc.scalar.activation(sa[:, 2:4, :], ps[:, (n + 1) % 2], ACT.Sigmoid).then_inc(sig_ready, 1)
                split(n + 3, (n + 1) % 2)
                if j >= 2:
                    act.wait_ge(pe_taps_done, 2 * j - 2)
                for m in range(2):
                    for i in range(PE_TAPS[j]):
                        c = COLS["dw"] + CONV_W * (2 * j + m) + CONV_W - PE_TAPS[j] + i
                        last = nc.scalar.activation(diag[:, diag_at[j % 2] + PE_TAPS[j] * m + i, :],
                                                    eye_r[:, :].bitcast(F32), ACT.Copy, scale=cols[:, c:c + 1])
                    last.then_inc(diag_ready, 1)
                done(n + 2)
                if j == 0:
                    act.wait_ge(first_mod, 4 * KB)
                nc.scalar.activation(gs_sb[:, 2 * j:2 * j + 2, :], ps[:, n % 2], ACT.Silu).then_inc(gs_ready, 1)
                split(n + 4, n % 2)
            for k in range(KB):
                act.wait_ge(centred, k + 1)
                squares(1, k, y_sb[:, k, :])
            inverse_root(1)
            done(N_CONV_OUT - 1)

            def ln_activate(k):
                act.wait_ge(ln_t, k + 1)
                c = COLS["cv_ln_b"] + k
                nc.scalar.activation(sa[:, k % 4, :], sa[:, k % 4, :], ACT.Silu, bias=cols[:, c:c + 1]).then_inc(ln_silu, 1)

            ln_activate(0)
            for k in range(KB):
                if k + 1 < KB:
                    ln_activate(k + 1)
                act.wait_ge(ln_y, k + 1)
                nc.scalar.activation(h_hi[:, k, :], y_sb[:, k, :], ACT.Copy).then_inc(h_hi_ready, 1)
            update_steps(N_CONV_OUT, 2)
            norm_hi(2, N_POOL)

            act.wait_ge(pads_done, 2)
            for j in range(4):
                n = N_POOL + j
                done(n)
                if j:
                    act.wait_ge(g_lo_ready, 2 * j)
                nc.scalar.activation(vpad[:, :, POOL_PAD:POOL_PAD + T], ps[:, n % 2], ACT.Copy).then_inc(v_copied, 1)
                split(n + 2, n % 2)
                for m in range(2):
                    act.wait_ge(pooled, 2 * j + m + 1)
                    nc.scalar.activation(g_hi[:, 2 * j + m, :], pool_b[:, m, 0:T], ACT.Copy).then_inc(g_hi_ready, 1)
            for j in range(4):
                n = N_POOL + 4 + j
                done(n)
                nc.scalar.activation(gs_sb[:, 2 * j:2 * j + 2, :], ps[:, n % 2], ACT.Silu).then_inc(gs_ready, 1)
                split(n + 2, n % 2)
            for k in range(KB):
                act.wait_ge(grp_y, k + 1)
                nc.scalar.activation(h_hi[:, k, :], sa[:, k % 4, :], ACT.Copy).then_inc(h_hi_ready, 1)
            done(N_GRP)
            split(N_GRP + 2, N_GRP % 2)
            update_steps(N_POOL_OUT, 3)
            norm_hi(3, N_SB)
            act.wait_ge(h_lo_ready, 8 * 4 + 8)
            act.dma_start(x_spill, x_sb).then_inc(x_spilled, 16)

            def softplus_log(hd):
                s = hd % 2
                act.wait_ge(z_done, hd + 1)
                if hd >= 2:
                    act.wait_ge(a_split, hd - 1)
                zt = z_tmp[:, s, :]
                nc.scalar.activation(zt, z_ps[s][:, 0:Z_W], ACT.Abs).then_inc(stick_step, 1)
                act.wait_ge(stick_step, hd * 2 + 1)
                nc.scalar.activation(zt, zt, ACT.Exp, scale=-1.0).then_inc(stick_step, 1)
                act.wait_ge(stick_step, hd * 2 + 2)
                nc.scalar.activation(zt, zt, ACT.Ln, bias=1.0).then_inc(stick_ln, 1)

            def weights(hd):
                act.wait_ge(after_done, hd + 1)
                nc.scalar.activation(z_tmp[:, hd % 2, :], z_ps[hd % 2][:, 0:Z_W], ACT.Exp).then_inc(a_exp, 1)

            def output_hi(hd):
                act.wait_ge(o_done, hd + 1)
                rows = slice(64 * (hd % 2), 64 * (hd % 2) + 64)
                nc.scalar.activation(g_hi[rows, hd // 2, :], o_ps[rows, :], ACT.Copy).then_inc(o_hi_ready, 1)

            def half_done(n, b):
                if b % 2:
                    done(n)
                else:
                    act.wait_ge(block_done, (n - N_SB) + 1)

            def qkv_high(grp, b, bank):
                half_done(N_SB + 3 * grp + b // 2, b)
                kind, m, s = b // 2, b % 2, grp % 2
                src = ps_flat[:, T * bank:T * bank + T]
                if kind == 2:
                    dst, src = sbv_hi[s][:, 2 * m:2 * m + 2, :], src.rearrange("p (b c) -> p b c", c=TILE_W)
                else:
                    dst = (sbq_hi, sbk_hi)[kind][s][:, m, :]
                nc.scalar.activation(dst, src, ACT.Copy, scale=SB_SCALE if kind == 0 else 1.0).then_inc(qkv_hi, 1)

            def gate_high(b):
                half_done(N_SB_GATE + b // 2, b)
                if b == 0:
                    act.wait_ge(o_done, 12)
                c = COLS["b_branch"] + b
                nc.scalar.activation(sb_gates[:, b, :], ps_flat[:, 0:T], ACT.Identity, bias=cols[:, c:c + 1]).then_inc(gate_raw, 1)

            log_table()
            for b in range(6):
                qkv_high(0, b, b % 4)
                if b % 2:
                    split(N_SB + b // 2 + 2, (N_SB + b // 2) % 2)
            act.wait_ge(x_spilled, 16)
            for grp in range(4):
                hd, n = 4 * grp, N_SB + 3 * grp + 3

                def high(b):
                    if grp < 3:
                        qkv_high(grp + 1, b, 0)
                    else:
                        gate_high(b)

                softplus_log(hd)
                high(0)
                softplus_log(hd + 1)
                high(1)
                split(n + 2, n % 2)
                weights(hd)
                high(2)
                weights(hd + 1)
                output_hi(hd)
                high(3)
                softplus_log(hd + 2)
                output_hi(hd + 1)
                softplus_log(hd + 3)
                split(n + 3, (n + 1) % 2)
                high(4)
                weights(hd + 2)
                if grp == 3:
                    high(5)
                weights(hd + 3)
                output_hi(hd + 2)
                high(5 if grp < 3 else 6)
                output_hi(hd + 3)
                split(n + 4, n % 2)
            gate_high(7)

            for half in range(2):
                act.wait_ge(gate_raw, 8)
                part = sb_gates[:, 4 * half:4 * half + 4, :]
                nc.scalar.activation(part, part, ACT.Sigmoid).then_inc(gate_ready, 1)
                if half == 0:
                    split(N_SB_OUT + 1, (N_SB_OUT + 1) % 2)
            for j in range(4):
                n = N_SB_OUT + j
                done(n)
                split(n + 2, n % 2)
            act.wait_ge(mg_ready, 4)
            act.wait_ge(mods_ready, 6)
            act.dma_start(rope, rope_in).then_inc(rope_in_s, 16)

            def head(hd, n, parity, g_at):
                if not (isinstance(hd, int) and hd == 0):
                    act.wait_ge(s_decayed, hd * 4)
                act.dma_start(decay[:, :], decay_in[hd]).then_inc(decay_in_s, 16)
                for i, (dst, scale) in enumerate(((rq_hi, 1.0), (rk_hi, RK_SCALE))):
                    slot = (parity + i) % 2
                    done(n + i)
                    for m in range(2):
                        act.wait_ge(rot_step, hd * 4 + 2 * i + m + 1)
                        nc.scalar.activation(dst[:, m, :], rt[:, m, :], ACT.Copy, scale=scale).then_inc(rot_hi, 1)
                    split(n + i + 2, slot)
                for i in range(2):
                    slot = (parity + i) % 2
                    done(n + 2 + i)
                    nc.scalar.activation(rv_hi[:, :, TILE_W * i:TILE_W * (i + 1)], ps_tok[:, slot], ACT.Copy).then_inc(rv_hi_ready, 1)
                    split(n + i + 4, slot)
                    if i == 0:
                        for j in range(TB):
                            w = T - P * j
                            act.wait_ge(s_decayed, hd * 4 + j + 1)
                            nc.scalar.activation(s_hi[:, z_off(j):z_off(j) + w], rt[:, j % 2, 0:w], ACT.Copy).then_inc(s_hi_ready, 1)
                for e in range(4):
                    act.wait_ge(ro_done, hd * 4 + e + 1)
                    if e == 2:
                        act.wait_ge(ro_added, hd * 3 + 1)
                    nc.scalar.activation(rt[:, e % 2, :], at_ps[:, e, :], ACT.Square).then_inc(ro_sq, 1)
                nc.scalar.preload_act_table_set("sqrt_and_others")
                act.wait_ge(ro_stat, hd + 1)
                nc.scalar.activation(rs[:, :], ps[:, 1 - parity, 0, :], ACT.Sqrt, scale=2.0, bias=eps_c[:, 0:1]).then_inc(ro_root, 1)
                for i in range(2):
                    slot = (parity + i) % 2
                    done(n + 4 + i)
                    if i:
                        act.wait_ge(ro_w, hd * 4 + 2)
                    nc.scalar.activation(rt[:, 2:4, :], ps[:, slot], ACT.Silu).then_inc(ro_silu, 1)
                    split(n + 6 + i, slot)
                    for m in range(2):
                        e = 2 * i + m
                        act.wait_ge(ro_w, hd * 4 + e + 1)
                        nc.scalar.activation(g_hi[:, g_at + e, :], rt[:, m, :], ACT.Copy).then_inc(o_hi_ready, 1)

            for i in range(2):
                head(i, i * 6 + N_RET1, N_RET1 % 2, i * 4)
            for j in range(4):
                n = N_RETP + j
                done(n)
                nc.scalar.activation(pr[:, 2 * j:2 * j + 2, :], ps[:, n % 2], ACT.Copy).then_inc(pr_ready, 1)
                split(n + 2, n % 2)
            for i in range(2):
                head(i + 2, i * 6 + N_RET2, N_RET2 % 2, i * 4)
            for j in range(4):
                n = N_GATE + j
                done(n)
                if j == 0:
                    act.wait_ge(o_lo_ready, 16 + 16)
                for m in range(2):
                    c = COLS["b_branch"] + 8 + 2 * j + m
                    nc.scalar.activation(gates[:, 2 * j + m, :], ps[:, n % 2, m, :], ACT.Sigmoid, bias=cols[:, c:c + 1]).then_inc(gate_ready, 1)
                split(n + 2, n % 2)
            for j in range(4):
                n = N_MERGE + j
                done(n)
                for m in range(2):
                    act.wait_ge(merge_step, 3 * (2 * j + m) + 3)
                    nc.scalar.activation(h_hi[:, 2 * j + m, :], mg[:, 2 * j + m, :], ACT.Copy).then_inc(h_hi_ready, 1)
                split(n + 2, n % 2)
            act.wait_ge(h_lo_ready, 8 * 5 + 8)
            act.dma_start(x_sb, x_spill).then_inc(x_back, 16)
            update_steps(N_OUT, 4)
            norm_hi(4, N_FFN)

            def ffn_pair(j, n, parity):
                done(n)
                if not (isinstance(j, int) and j == 0):
                    act.wait_ge(ff_prod, j * 2)
                nc.scalar.activation(ft[:, 0:2, :], ps[:, parity], ACT.Silu).then_inc(ff_silu, 1)
                split(n + 2, parity)
                done(n + 1)
                for m in range(2):
                    act.wait_ge(ff_prod, j * 2 + m + 1)
                    nc.scalar.activation(f_hi[:, j * 2 + m, :], ft[:, 2 + m, :], ACT.Copy).then_inc(ff_hi, 1)
                split(n + 3, 1 - parity)

            act.wait_ge(h_lo_ready, 8 * 6 + 8)
            ffn_pair(0, N_FFN, N_FFN % 2)
            with act.Fori(1, 11) as i:
                ffn_pair(i, 2 * i + N_FFN, N_FFN % 2)
            for j in range(4):
                for i in range(3):
                    n = N_FFN_OUT + 3 * j + i
                    done(n)
                    if n + 2 < N_TILES:
                        split(n + 2, n % 2)
                for m in range(2):
                    act.wait_ge(x_updated, x_count(5, 2 * j + m))
                    squares(5, 2 * j + m, x_sb[:, 2 * j + m, :])
            inverse_root(5)
            for k in range(KB):
                act.wait_ge(t_ready, 8 * 4 + k + 1)
                act.dma_start(out[:, k, :], x_sb[:, k, :]).then_inc(out_stored, 16)
            act.wait_ge(out_stored, 16 * KB)

        @block.vector
        def _(dve):
            def split(n, slot):
                dve.wait_ge(w_hi_done, n + 1)
                nc.vector.tensor_tensor(w_lo[:, slot], w_raw[:, slot], w_hi[:, slot].bitcast(F32),
                                        ALU.subtract).then_inc(w_lo_done, 1)

            def done(n):
                dve.wait_ge(tile_done, n + 1)

            def low(dst, src, hi, inc, scale=None):
                if scale is None:
                    nc.vector.tensor_tensor(dst, src, hi.bitcast(F32), ALU.subtract).then_inc(inc, 1)
                else:
                    nc.vector.scalar_tensor_tensor(dst, src, scale, hi.bitcast(F32), ALU.mult, ALU.subtract).then_inc(inc, 1)

            def take_mods(r, b0, nb, count):
                dve.wait_ge(mod_summed, count)
                src = COLS["b_mod"] + 24 * r + b0 if r < 2 else COLS["b_ada"] + 24 * (r - 2) + b0
                dst = 24 * r + b0
                nc.vector.tensor_tensor(mods[:, dst:dst + nb], at_ps[:, 3, 0:nb], cols[:, src:src + nb],
                                        ALU.add).then_inc(mods_ready, 1)
                dve.wait_ge(mods_ready, count)

            def gain(u):
                idx = {0: 0, 2: 1, 3: 2, 4: 3}[u]
                r, part = SHIFT[u]
                c, g = mod_col(r, part + 1, 0), COLS[GAIN[u]] + GAIN_AT[u]
                nc.vector.scalar_tensor_tensor(gp[:, :], mods[:, c:c + 8], 1.0, cols[:, g:g + 8], ALU.add,
                                               ALU.mult).then_inc(gp_ready, 1)
                dve.wait_ge(gp_ready, idx + 2)

            def root_there(u):
                dve.wait_ge(rs_ready, u + 1)

            def norm(u, ks=range(KB)):
                idx = {0: 0, 2: 1, 3: 2, 4: 3}[u]
                r, part = SHIFT[u]
                tb = t_buf(u)

                def lows(k):
                    dve.wait_ge(h_hi_ready, 8 * FILL[u] + k + 1)
                    c = mod_col(r, part, k)
                    nc.vector.scalar_tensor_tensor(h_lo[:, k, :], tb[:, k % 4, :], mods[:, c:c + 1],
                                                   h_hi[:, k, :].bitcast(F32), ALU.add, ALU.subtract).then_inc(h_lo_ready, 1)

                for k in ks:
                    if k >= 4:
                        dve.wait_ge(h_lo_ready, 8 * FILL[u] + k - 3)
                    nc.vector.scalar_tensor_tensor(tb[:, k % 4, :], x_sb[:, k, :], gp[:, k:k + 1], rs[:, :], ALU.mult,
                                                   ALU.mult).then_inc(t_ready, 1)
                    if k > ks[0]:
                        lows(k - 1)
                lows(ks[-1])

            def add_squares(u, j):
                before = 5 * (u - 2)
                for k in (2 * j, 2 * j + 1):
                    dve.wait_ge(sq_ready, 8 * u + k + 1)
                    if k == 0:
                        continue
                    a, b = sq_buf(u)[:, k % SQ_RING, :], sq_buf(u)[:, 0, :] if k == 1 else rs[:, :]
                    if k > 1:
                        dve.wait_ge(sq_added, before + k - 1)
                    op = nc.vector.tensor_tensor(rs[:, :], a, b, ALU.add)
                    op.then_inc(sq_added, 1)

            def update_steps(n0, u, gate, x0):
                r, part = GATE[gate]
                for j in range(4):
                    n = n0 + j
                    if j:
                        add_squares(u, j - 1)
                    for m in range(2):
                        if j == 3 and m == 0:
                            dve.wait_ge(half_ready, u - 1)
                        else:
                            done(n)
                        k = 2 * j + m
                        c = mod_col(r, part, k)
                        nc.vector.scalar_tensor_tensor(x_sb[:, k, :], ps[:, n % 2, m, :], mods[:, c:c + 1], x_sb[:, k, :],
                                                       ALU.mult, ALU.add).then_inc(x_updated, 1)
                    if j == 3:
                        dve.wait_ge(w_landed[n % 2], (n + 2 - n % 2) * 8 + 16)
                        nc.vector.tensor_copy(w_hi[:, n % 2], w_raw[:, n % 2]).then_inc(w_hi_done, 1)
                    split(n + 2, n % 2)

            nc.vector.memset(eps_c[:, :], EPS)
            nc.vector.memset(ypad[:, :, :], 0.0).then_inc(pads_done, 1)
            dve.wait_ge(const_in_s, 16)
            nc.vector.tensor_copy(pool_edge[:, :], c_stage[:, C_POOL:C_POOL + 64])
            for dst, c in ((eye_r, C_EYE), (neg_r, C_NEG), (ntri_r, C_NTRI), (none_r, C_NONE)):
                nc.vector.tensor_copy(dst[:, :], c_stage[:, c:c + P])
            nc.vector.tensor_copy(mean_m[:, :], c_stage[:, C_MEAN:C_MEAN + P]).then_inc(consts_done, 1)
            dve.wait_ge(csil_done, 2)
            for half in range(2):
                for kb in range(KB):
                    for part in range(2):
                        g = 2 * part + half
                        acc = mod_acc[:, MOD_G * g:MOD_G * (g + 1)]
                        step = 2 * KB * half + 2 * kb + part
                        i = 2 * (kb // 2) + part
                        if kb % 2 == 0:
                            dve.wait_ge(first_in[i], 16 * half + 16)
                        src = first_chunk[i // 4][:, i % 4, kb % 2]
                        c = csil[:, kb:kb + 1]
                        if kb == 0:
                            nc.vector.tensor_scalar(acc, src, c, None, ALU.mult).then_inc(first_mod, 1)
                        else:
                            dve.wait_ge(first_mod, step - 1)
                            nc.vector.scalar_tensor_tensor(acc, src, c, acc, ALU.mult, ALU.add).then_inc(first_mod, 1)
                if half == 0:
                    split(0, 0)
                dve.wait_ge(mod_summed, half + 1)
                both = [t.rearrange("p (s h k) -> p s h k", s=2, h=2)[:, :, half, :]
                        for t in (mods[:, 0:16], cols[:, COLS["b_mod"]:COLS["b_mod"] + 16])]
                nc.vector.tensor_tensor(both[0], at_ps[:, 3, 0:8].rearrange("p (s k) -> p s k", s=2), both[1],
                                        ALU.add).then_inc(mods_ready, 1)
                dve.wait_ge(mods_ready, half + 1)
                c, gc = mod_col(0, 1, 4 * half), COLS["norm_g"] + 4 * half
                nc.vector.scalar_tensor_tensor(gp[:, 4 * half:4 * half + 4], mods[:, c:c + 4], 1.0, cols[:, gc:gc + 4],
                                               ALU.add, ALU.mult).then_inc(gp_ready, 1)
                dve.wait_ge(gp_ready, half + 1)
                if half == 0:
                    root_there(0)
                norm(0, range(4 * half, 4 * half + 4))
                if half == 0:
                    split(1, 1)

            def convolve(j, t0, t1):
                for t in range(t0, t1):
                    for m in range(2):
                        k = 2 * j + m
                        w, db = COLS["dw"] + CONV_W * k, COLS["cv_db"] + k
                        src = ypad[:, m, :]
                        if t == 0:
                            nc.vector.tensor_scalar(y_sb[:, k, :], src[:, 0:T], cols[:, w:w + 1], cols[:, db:db + 1],
                                                    ALU.mult, ALU.add).then_inc(conv_step, 1)
                        else:
                            dve.wait_ge(conv_step, CONV_BEFORE[j] + 2 * t + m - 1)
                            nc.vector.scalar_tensor_tensor(y_sb[:, k, :], src[:, t:t + T], cols[:, w + t:w + t + 1],
                                                           y_sb[:, k, :], ALU.mult, ALU.add).then_inc(conv_step, 1)

            for j in range(4):
                n = N_CONV + 3 * j
                done(n)
                split(n + 2, n % 2)
                done(n + 1)
                dve.wait_ge(a_copied, j + 1)
                dve.wait_ge(sig_ready, j + 1)
                if j:
                    dve.wait_ge(conv_step, CONV_BEFORE[j])
                for m in range(2):
                    nc.vector.tensor_tensor(ypad[:, m, PAD:PAD + T], sa[:, m, :], sa[:, 2 + m, :], ALU.mult).then_inc(y_ready, 1)
                split(n + 3, (n + 1) % 2)
                dve.wait_ge(y_ready, 2 * j + 2)
                convolve(j, 0, CONV_W // 2)
                done(n + 2)
                split(n + 4, n % 2)
                convolve(j, CONV_W // 2, CONV_W - PE_TAPS[j])
                for m in range(2):
                    dve.wait_ge(pe_taps_done, 2 * j + m + 1)
                    dve.wait_ge(conv_step, CONV_BEFORE[j + 1] - 3 + m)
                    nc.vector.tensor_tensor(y_sb[:, 2 * j + m, :], at_ps[:, 1 + m, :], y_sb[:, 2 * j + m, :],
                                            ALU.add).then_inc(conv_step, 1)
                if j == 1:
                    take_mods(0, 16, 8, 3)
            dve.wait_ge(conv_summed, KB)
            for k in range(KB):
                nc.vector.tensor_tensor(y_sb[:, k, :], y_sb[:, k, :], at_ps[:, 0, :], ALU.subtract).then_inc(centred, 1)
            root_there(1)

            def scaled(k):
                if k >= 4:
                    dve.wait_ge(ln_y, k - 3)
                c = COLS["cv_ln_g"] + k
                nc.vector.scalar_tensor_tensor(sa[:, k % 4, :], y_sb[:, k, :], cols[:, c:c + 1], rs[:, :], ALU.mult,
                                               ALU.mult).then_inc(ln_t, 1)

            def gated(k):
                dve.wait_ge(ln_silu, k + 1)
                nc.vector.tensor_tensor(y_sb[:, k, :], sa[:, k % 4, :], gs_sb[:, k, :], ALU.mult).then_inc(ln_y, 1)

            def gated_low(k):
                dve.wait_ge(h_hi_ready, 8 + k + 1)
                low(h_lo[:, k, :], y_sb[:, k, :], h_hi[:, k, :], h_lo_ready)

            scaled(0)
            scaled(1)
            for k in range(KB):
                gated(k)
                if k + 2 < KB:
                    scaled(k + 2)
                if k:
                    gated_low(k - 1)
            gated_low(KB - 1)
            take_mods(1, 0, 24, 4)
            update_steps(N_CONV_OUT, 2, "conv", 0)
            gain(2)
            root_there(2)
            norm(2)

            nc.vector.memset(vpad[:, :, 0:POOL_PAD], 0.0)
            nc.vector.memset(vpad[:, :, POOL_PAD + T:PW], 0.0).then_inc(pads_done, 1)
            steps = 0
            for j in range(4):
                n = N_POOL + j
                win = 2 << j
                done(n)
                dve.wait_ge(v_copied, j + 1)
                src, ln = vpad, PW
                for lvl in range(j + 1):
                    d = 1 << lvl
                    dst = pool_a if (j - lvl) % 2 == 0 else pool_b
                    ln -= d
                    nc.vector.tensor_tensor(dst[:, :, 0:ln], src[:, :, 0:ln], src[:, :, d:d + ln], ALU.add).then_inc(pool_step, 1)
                    steps += 1
                    dve.wait_ge(pool_step, steps)
                    src = dst
                assert src is pool_a
                o = POOL_PAD - win // 2
                tok = vpad[:, :, POOL_PAD:POOL_PAD + T]
                nc.vector.scalar_tensor_tensor(pool_b[:, :, 0:T], pool_a[:, :, o:o + T], 1.0 / win, tok, ALU.mult,
                                               ALU.subtract).then_inc(pool_step, 1)
                dve.wait_ge(pool_step, steps + 1)
                for m in range(2):
                    for side, e in ((0, 0), (T - 8, 8)):
                        nc.vector.tensor_tensor(pool_a[:, m, o + side:o + side + 8], pool_a[:, m, o + side:o + side + 8],
                                                pool_edge[:, 16 * j + e:16 * j + e + 8], ALU.mult).then_inc(pool_step, 1)
                steps += 5
                dve.wait_ge(pool_step, steps)
                for m in range(2):
                    nc.vector.tensor_tensor(pool_b[:, m, 0:8], pool_a[:, m, o:o + 8], tok[:, m, 0:8],
                                            ALU.subtract).then_inc(pool_step, 1)
                    nc.vector.tensor_tensor(pool_b[:, m, T - 8:T], pool_a[:, m, o + T - 8:o + T], tok[:, m, T - 8:T],
                                            ALU.subtract).then_inc(pooled, 1)
                steps += 2
                split(n + 2, n % 2)
                for m in range(2):
                    dve.wait_ge(g_hi_ready, 2 * j + m + 1)
                    low(g_lo[:, 2 * j + m, :], pool_b[:, m, 0:T], g_hi[:, 2 * j + m, :], g_lo_ready)
            for j in range(4):
                n = N_POOL + 4 + j
                done(n)
                if n + 2 < N_GRP + 2:
                    split(n + 2, n % 2)
            take_mods(2, 0, 24, 5)
            dve.wait_ge(gs_ready, 8)

            def group_y(k):
                if k == 7:
                    done(N_GRP)
                else:
                    dve.wait_ge(grp_done, k + 1)
                if k >= 4:
                    dve.wait_ge(h_lo_ready, 24 + k - 3)
                src = (ps[:, 1, k % 2, :], at_ps[:, k % 2, :], at_ps[:, 2 + k % 2, :], ps[:, 0, k % 2, :])[k // 2]
                c = COLS["pl_scale"] + k
                nc.vector.scalar_tensor_tensor(sa[:, k % 4, :], src, cols[:, c:c + 1], gs_sb[:, k, :], ALU.mult,
                                               ALU.mult).then_inc(grp_y, 1)

            def group_low(k):
                dve.wait_ge(h_hi_ready, 24 + k + 1)
                low(h_lo[:, k, :], sa[:, k % 4, :], h_hi[:, k, :], h_lo_ready)

            done(N_GRP - 1)
            for k in range(KB):
                group_y(k)
                if k:
                    group_low(k - 1)
            group_low(KB - 1)
            split(N_GRP + 2, N_GRP % 2)
            update_steps(N_POOL_OUT, 3, "pool", 8)
            gain(3)
            root_there(3)
            norm(3)

            def softplus_high(hd):
                s = hd % 2
                dve.wait_ge(stick_ln, hd + 1)
                zt = z_tmp[:, s, :]
                nc.vector.scalar_tensor_tensor(zt, z_ps[s][:, 0:Z_W], 0.0, zt, ALU.max, ALU.add).then_inc(sp_step, 1)
                dve.wait_ge(sp_step, hd * 2 + 1)
                nc.vector.tensor_copy(att_hi[:, s, :], zt).then_inc(sp_step, 1)

            def softplus_low(hd):
                s = hd % 2
                dve.wait_ge(sp_step, hd * 2 + 2)
                low(att_lo[:, s, :], z_tmp[:, s, :], att_hi[:, s, :], sp_split)

            def weights_split(hd):
                s = hd % 2
                dve.wait_ge(a_exp, hd + 1)
                zt = z_tmp[:, s, :]
                nc.vector.tensor_copy(att_hi[:, s, :], zt).then_inc(a_step, 1)
                dve.wait_ge(a_step, hd + 1)
                low(att_lo[:, s, :], zt, att_hi[:, s, :], a_split)

            def output_low(hd):
                dve.wait_ge(o_hi_ready, hd + 1)
                rows = slice(64 * (hd % 2), 64 * (hd % 2) + 64)
                low(g_lo[rows, hd // 2, :], o_ps[rows, :], g_hi[rows, hd // 2, :], o_lo_ready)

            def qkv_low_part(grp, b, bank):
                dve.wait_ge(qkv_hi, 6 * grp + b + 1)
                kind, m, s = b // 2, b % 2, grp % 2
                src = ps_flat[:, T * bank:T * bank + T]
                if kind == 2:
                    c = slice(2 * m, 2 * m + 2)
                    low(sbv_lo[s][:, c, :], src.rearrange("p (b c) -> p b c", c=TILE_W), sbv_hi[s][:, c, :], qkv_lo)
                else:
                    dst, hi = ((sbq_lo, sbq_hi), (sbk_lo, sbk_hi))[kind]
                    low(dst[s][:, m, :], src, hi[s][:, m, :], qkv_lo, SB_SCALE if kind == 0 else None)

            for b in range(6):
                qkv_low_part(0, b, b % 4)
                if b % 2:
                    split(N_SB + b // 2 + 2, (N_SB + b // 2) % 2)
            for grp in range(4):
                hd, n = 4 * grp, N_SB + 3 * grp + 3

                def lows(b):
                    if grp < 3:
                        qkv_low_part(grp + 1, b, 0)

                softplus_high(hd)
                lows(0)
                softplus_low(hd)
                softplus_high(hd + 1)
                lows(1)
                softplus_low(hd + 1)
                split(n + 2, n % 2)
                weights_split(hd)
                lows(2)
                if grp == 0:
                    take_mods(3, 0, 24, 6)
                weights_split(hd + 1)
                output_low(hd)
                lows(3)
                softplus_high(hd + 2)
                softplus_low(hd + 2)
                output_low(hd + 1)
                softplus_high(hd + 3)
                lows(4)
                softplus_low(hd + 3)
                weights_split(hd + 2)
                split(n + 3, (n + 1) % 2)
                weights_split(hd + 3)
                output_low(hd + 2)
                lows(5)
                output_low(hd + 3)
                split(n + 4, n % 2)

            split(N_SB_OUT + 1, (N_SB_OUT + 1) % 2)
            for j in range(4):
                n = N_SB_OUT + j
                done(n)
                dve.wait_ge(gate_ready, j // 2 + 1)
                nc.vector.tensor_tensor(mg[:, 2 * j:2 * j + 2, :], ps[:, n % 2], sb_gates[:, 2 * j:2 * j + 2, :],
                                        ALU.mult).then_inc(mg_ready, 1)
                split(n + 2, n % 2)

            dve.wait_ge(rope_in_s, 16)
            cos, sin = rope[:, 0, :], rope[:, 1, :]

            def rotate(i, slot, hd):
                a, b = ps[:, slot, 0, :], ps[:, slot, 1, :]
                for half, (p, q, op) in enumerate(((cos, sin, ALU.subtract), (sin, cos, ALU.add))):
                    nc.vector.tensor_tensor(rt[:, half, :], a, p, ALU.mult).then_inc(ro_norm, 1)
                    nc.vector.tensor_tensor(rt[:, 2 + half, :], b, q, ALU.mult).then_inc(ro_norm, 1)
                    dve.wait_ge(ro_norm, hd * 12 + 4 * i + 2 * half + 2)
                    nc.vector.tensor_tensor(rt[:, half, :], rt[:, half, :], rt[:, 2 + half, :], op).then_inc(rot_step, 1)

            def head(hd, n, parity, g_at):
                for i, (dst, hi, scale) in enumerate(((rq_lo, rq_hi, None), (rk_lo, rk_hi, RK_SCALE))):
                    slot = (parity + i) % 2
                    done(n + i)
                    rotate(i, slot, hd)
                    for m in range(2):
                        dve.wait_ge(rot_hi, hd * 4 + 2 * i + m + 1)
                        low(dst[:, m, :], rt[:, m, :], hi[:, m, :], rot_lo, scale)
                    dve.wait_ge(rot_lo, hd * 4 + 2 * i + 2)
                    split(n + i + 2, slot)
                dve.wait_ge(decay_in_s, hd * 16 + 16)
                for i in range(2):
                    slot = (parity + i) % 2
                    done(n + 2 + i)
                    dve.wait_ge(rv_hi_ready, hd * 2 + i + 1)
                    low(rv_lo[:, :, TILE_W * i:TILE_W * (i + 1)], ps_tok[:, slot], rv_hi[:, :, TILE_W * i:TILE_W * (i + 1)], rv_lo_ready)
                    split(n + i + 4, slot)
                    if i == 0:
                        def s_low(j):
                            w = T - P * j
                            dve.wait_ge(s_hi_ready, hd * 4 + j + 1)
                            low(s_lo[:, z_off(j):z_off(j) + w], rt[:, j % 2, 0:w], s_hi[:, z_off(j):z_off(j) + w], s_lo_ready)

                        for j in range(TB):
                            w = T - P * j
                            dve.wait_ge(s_done, hd * 4 + j + 1)
                            if j >= 2:
                                dve.wait_ge(s_lo_ready, hd * 4 + j - 1)
                            nc.vector.tensor_tensor(rt[:, j % 2, 0:w], at_ps[:, j, 0:w], decay[:, 0:w], ALU.mult).then_inc(s_decayed, 1)
                            if j:
                                s_low(j - 1)
                        s_low(TB - 1)
                for e in range(1, 4):
                    dve.wait_ge(ro_sq, hd * 4 + e + 1)
                    if e > 1:
                        dve.wait_ge(ro_added, hd * 3 + e - 1)
                    nc.vector.tensor_tensor(rs[:, :], rt[:, 0, :] if e == 1 else rs[:, :], rt[:, e % 2, :],
                                            ALU.add).then_inc(ro_added, 1)
                dve.wait_ge(ro_root, hd + 1)
                nc.vector.reciprocal(rs[:, :], rs[:, :]).then_inc(ro_rs, 1)
                dve.wait_ge(ro_rs, hd + 1)
                for i in range(2):
                    slot = (parity + i) % 2
                    done(n + 4 + i)
                    dve.wait_ge(ro_silu, hd * 2 + i + 1)
                    for m in range(2):
                        e = 2 * i + m
                        if i:
                            dve.wait_ge(o_lo_ready, hd * 4 + 16 + m + 1)
                        nc.vector.tensor_tensor(rt[:, m, :], at_ps[:, e, :], rs[:, :], ALU.mult).then_inc(ro_norm, 1)
                        dve.wait_ge(ro_norm, hd * 12 + 8 + e + 1)
                        nc.vector.tensor_tensor(rt[:, m, :], rt[:, m, :], rt[:, 2 + m, :], ALU.mult).then_inc(ro_w, 1)
                    for m in range(2):
                        e = 2 * i + m
                        dve.wait_ge(o_hi_ready, hd * 4 + 16 + e + 1)
                        low(g_lo[:, g_at + e, :], rt[:, m, :], g_hi[:, g_at + e, :], o_lo_ready)
                    split(n + 6 + i, slot)
                dve.wait_ge(o_lo_ready, hd * 4 + 20)

            for i in range(2):
                head(i, i * 6 + N_RET1, N_RET1 % 2, i * 4)
            for j in range(4):
                n = N_RETP + j
                done(n)
                split(n + 2, n % 2)
            for i in range(2):
                head(i + 2, i * 6 + N_RET2, N_RET2 % 2, i * 4)
            for j in range(4):
                n = N_GATE + j
                done(n)
                split(n + 2, n % 2)
            dve.wait_ge(gate_ready, 10)
            for j in range(4):
                n = N_MERGE + j
                done(n)
                for m in range(2):
                    k = 2 * j + m
                    nc.vector.tensor_tensor(pr[:, k, :], ps[:, n % 2, m, :], pr[:, k, :], ALU.add).then_inc(merge_step, 1)
                    dve.wait_ge(merge_step, 3 * k + 1)
                    nc.vector.tensor_tensor(pr[:, k, :], pr[:, k, :], gates[:, k, :], ALU.mult).then_inc(merge_step, 1)
                    dve.wait_ge(merge_step, 3 * k + 2)
                    nc.vector.tensor_tensor(mg[:, k, :], pr[:, k, :], mg[:, k, :], ALU.add).then_inc(merge_step, 1)
                    dve.wait_ge(h_hi_ready, 8 * 5 + k + 1)
                    low(h_lo[:, k, :], mg[:, k, :], h_hi[:, k, :], h_lo_ready)
                split(n + 2, n % 2)
            dve.wait_ge(x_back, 16)
            update_steps(N_OUT, 4, "out", 16)
            gain(4)
            root_there(4)
            norm(4)

            def ffn_pair(j, n, parity):
                done(n)
                split(n + 2, parity)
                done(n + 1)
                dve.wait_ge(ff_silu, j + 1)
                for m in range(2):
                    nc.vector.tensor_tensor(ft[:, 2 + m, :], ps[:, 1 - parity, m, :], ft[:, m, :], ALU.mult).then_inc(ff_prod, 1)
                for m in range(2):
                    dve.wait_ge(ff_hi, j * 2 + m + 1)
                    low(f_lo[:, j * 2 + m, :], ft[:, 2 + m, :], f_hi[:, j * 2 + m, :], ff_lo)
                split(n + 3, 1 - parity)
                dve.wait_ge(ff_lo, j * 2 + 2)

            ffn_pair(0, N_FFN, N_FFN % 2)
            with dve.Fori(1, 11) as i:
                ffn_pair(i, 2 * i + N_FFN, N_FFN % 2)
            r, part = GATE["ffn"]
            for j in range(4):
                for i in range(3):
                    n = N_FFN_OUT + 3 * j + i
                    if j and i == 1:
                        add_squares(5, j - 1)
                    if (j, i) != (3, 2):
                        done(n)
                    if i == 2:
                        for m in range(2):
                            if j == 3:
                                if m == 0:
                                    dve.wait_ge(half_ready, 4)
                                else:
                                    done(n)
                            k = 2 * j + m
                            c = mod_col(r, part, k)
                            nc.vector.scalar_tensor_tensor(x_sb[:, k, :], ps[:, FFN_BANK[j], m, :], mods[:, c:c + 1], x_sb[:, k, :],
                                                           ALU.mult, ALU.add).then_inc(x_updated, 1)
                    if n + 2 < N_TILES:
                        split(n + 2, n % 2)
            root_there(5)
            for k in range(KB):
                c = COLS["g_final"] + k
                nc.vector.scalar_tensor_tensor(x_sb[:, k, :], x_sb[:, k, :], cols[:, c:c + 1], rs[:, :], ALU.mult,
                                               ALU.mult).then_inc(t_ready, 1)


def _columns(v):
    return np.asarray(v).reshape(-1, P).T


def _weight_tiles(w):
    w = np.asarray(w)
    if w.shape[0] < D:
        w = np.concatenate([w, np.zeros((D - w.shape[0], w.shape[1]), w.dtype)])
    return list(w.reshape(KB, P, -1, TILE_W).transpose(2, 1, 0, 3))


def _shape_constants():
    f = np.float32
    const = np.zeros((P, N_CONST), f)
    const[:, C_MEAN:C_MEAN + P] = 1.0 / D
    const[:, C_EYE:C_EYE + P] = np.eye(P)
    s, t = np.arange(P)[:, None], np.arange(P)[None, :]
    const[:, C_NEG:C_NEG + P] = np.where(s >= t, f(NEG_BIG), f(0))
    const[:, C_NTRI:C_NTRI + P] = np.where(s >= t, f(-1), f(0))
    const[:, C_NONE:C_NONE + P] = -1
    tok = np.arange(T)
    for j in range(4):
        win = 2 << j
        cnt = (np.clip(tok + win - win // 2, 0, T) - np.clip(tok - win // 2, 0, T)).astype(f)
        const[:, C_POOL + 16 * j:C_POOL + 16 * j + 16] = (1 / cnt)[np.r_[0:8, T - 8:T]]
    ang_freq = f(10000.0) ** (-np.arange(0, 256, 2, dtype=f) / f(256))
    ang = ang_freq[:, None] * tok.astype(f)[None, :]
    rope = np.stack([np.cos(ang), np.sin(ang)], axis=1).astype(f)
    log_gamma = np.log(f(1) - f(2) ** (f(-5) - np.arange(RET_HEADS, dtype=f)))
    diff = (tok[None, :] - np.arange(P)[:, None]).astype(f)
    decay = np.where(diff >= 0, np.exp(np.maximum(diff, 0)[None] * log_gamma[:, None, None]), 0).astype(f)
    return const, rope, decay


def kernel(**inputs):
    import concourse.bacc as bacc
    from concourse.bass_utils import run_bass_kernel_spmd

    a = {k: np.asarray(v) for k, v in inputs.items()}

    def pick(groups, order):
        return [groups[g][j] for g, j in order]

    conv = _weight_tiles(a["cv_w_in"][0])
    w_in = a["w_in_2"][0]
    cuts = np.cumsum([0, 1024, 1024, 1024, 1024, 1024, 2048, 2048, 1024, 1024])
    parts = [_weight_tiles(w_in[:, p:q]) for p, q in zip(cuts[:-1], cuts[1:])]
    sq, sk, sv, rq, rk, rv, rg, b_sb, b_ret = parts
    proj_sb = _weight_tiles(a["w_proj_sb_2"][0])
    proj_ret = [_weight_tiles(a["w_proj_ret_2"][0][D * i:D * (i + 1)]) for i in range(2)]
    ffn = _weight_tiles(a["w_ffn_in_2"][0])
    ffn_out = [_weight_tiles(a["w_ffn_out_2"][0][D * i:D * (i + 1)]) for i in range(3)]
    tiles = []
    for j in range(4):
        tiles += [conv[j], conv[4 + j], conv[8 + j]]
    tiles += _weight_tiles(a["cv_w_out"][0])
    tiles += _weight_tiles(a["pl_w_in"][0])
    tiles += _weight_tiles(a["pl_w_grp"][0].reshape(D, TILE_W))
    tiles += _weight_tiles(a["pl_w_out"][0])
    for j in range(4):
        tiles += [sq[j], sk[j], sv[j]]
    tiles += b_sb + proj_sb
    for h in range(RET_HEADS):
        tiles += [rq[h], rk[h], rv[2 * h], rv[2 * h + 1], rg[2 * h], rg[2 * h + 1]]
        if h == 1:
            tiles += proj_ret[0]
    tiles += b_ret + proj_ret[1]
    tiles += _weight_tiles(a["w_out_2"][0])
    for j in range(11):
        tiles += [ffn[j], ffn[11 + j]]
    for j in range(4):
        tiles += [ffn_out[i][j] for i in range(3)]
    assert len(tiles) == N_TILES
    w_stream = np.stack(tiles)

    mod = np.concatenate([a["w_mod"][0], a["w_mod"][1], a["w_ada_2"][0]], axis=1)
    mod_stream = np.ascontiguousarray(mod.reshape(4, 2, P, N_MOD_GROUPS, MOD_G).transpose(3, 0, 2, 1, 4))
    vectors = {
        "norm_g": a["norm_g"], "b_mod": a["b_mod"], "b_ada": a["b_ada_2"], "cv_db": a["cv_db"], "cv_ln_g": a["cv_ln_g"],
        "cv_ln_b": a["cv_ln_b"], "pl_scale": a["pl_scale"], "g_norm1": a["g_norm1_2"], "g_norm2": a["g_norm2_2"],
        "g_final": a["g_final_2"], "b_branch": a["b_branch_2"], "c": a["c"], "c_2": a["c_2"],
        "dw": a["cv_dw"][0].reshape(CONV_W, KB, P).transpose(1, 0, 2),
    }
    cols = np.ascontiguousarray(np.concatenate([_columns(vectors[n]) for n in COLS], axis=1))
    assert cols.shape == (P, N_COLS)
    x_t = np.ascontiguousarray(a["x"][0].T.reshape(KB, P, T).transpose(1, 0, 2))
    const, rope, decay = _shape_constants()

    arrays = {"w_stream": w_stream, "mod_stream": mod_stream, "x_t": x_t, "cols_in": cols, "const_in": const,
              "rope_in": rope, "decay_in": decay}
    nc = bacc.Bacc("TRN2", target_bir_lowering=False, num_devices=1)
    aps = {k: nc.dram_tensor(k, v.shape, F32, kind="ExternalInput").ap() for k, v in arrays.items()}
    x_spill = nc.dram_tensor("x_spill", (P, KB, T), F32).ap()
    out = nc.dram_tensor("out_t", (P, KB, T), F32, kind="ExternalOutput").ap()
    build_program(nc, aps["w_stream"], aps["mod_stream"], aps["x_t"], aps["cols_in"], aps["const_in"],
                  aps["rope_in"], aps["decay_in"], x_spill, out)
    got = run_bass_kernel_spmd(nc, [arrays], core_ids=[0]).results[0]["out_t"]
    return np.ascontiguousarray(got.transpose(1, 0, 2).reshape(D, T).T)[None]
```
